# Optimizing a Trainium2 kernel written in Bass

```python
import jax, jax.numpy as jnp
from jax import lax
import numpy as np

D_MODEL = 2048
BATCH = 1
SEQ = 512
DEPTH = 1
DEC_BATCH = 8
DEC_SEQ = 1
PAST_LEN = 2048
PAGE_SIZE = 128

HEAD_DIM = 64
D_RWKV = D_MODEL // 2
D_ATT = D_MODEL - D_RWKV
D_MIX = D_RWKV + D_ATT
N_RWKV_HEADS = D_RWKV // HEAD_DIM
N_ATT_HEADS = D_ATT // HEAD_DIM
LORA_W = 96
LORA_A = 96
SHIFT_W = 3 * D_RWKV + LORA_W + LORA_A
D_IN = SHIFT_W + D_RWKV + 4 * D_ATT
DIL_PATTERNS = ((128, 1), (512, 4), (2048, 16))
WIN_MAX = max(w for w, _ in DIL_PATTERNS)
BLK = 128
RMS_EPS = 1e-6
GN_EPS = 64e-5
L2_EPS = 1e-12

kernel_name = 'rwkv7_dilated_swa_parallel_heads_step'

def rms_norm(x, g, eps=RMS_EPS):
    x32 = x.astype(jnp.float32)
    return x32 * lax.rsqrt(jnp.mean(x32 * x32, axis=-1, keepdims=True) + eps) * g.astype(jnp.float32)

def alibi_slopes(n_heads):
    return 2.0 ** (-8.0 * jnp.arange(1, n_heads + 1, dtype=jnp.float32) / n_heads)

def wkv7_scan(S0, r, decay, k, v, a_vec, b_vec):
    def step(S, inp):
        r_t, w_t, k_t, v_t, a_t, b_t = inp
        sa = jnp.einsum('bhij,bhj->bhi', S, a_t)
        S = S * w_t[:, :, None, :] + sa[..., None] * b_t[:, :, None, :] + v_t[..., None] * k_t[:, :, None, :]
        y_t = jnp.einsum('bhij,bhj->bhi', S, r_t)
        return S, y_t
    xs = tuple(jnp.swapaxes(t, 0, 1) for t in (r, decay, k, v, a_vec, b_vec))
    S_T, ys = lax.scan(step, S0, xs)
    return S_T, jnp.swapaxes(ys, 0, 1)

def rwkv7_branch(zs_mix, g_r, S0, w0, w_up, a0, a_up, k_k, k_a, r_k, gn_w, gn_b):
    B, T, _ = zs_mix.shape
    heads = lambda t: t.reshape(B, T, N_RWKV_HEADS, HEAD_DIM)
    r = zs_mix[..., 0:D_RWKV]
    k = zs_mix[..., D_RWKV:2 * D_RWKV]
    v = zs_mix[..., 2 * D_RWKV:3 * D_RWKV]
    wd = zs_mix[..., 3 * D_RWKV:3 * D_RWKV + LORA_W]
    ad = zs_mix[..., 3 * D_RWKV + LORA_W:SHIFT_W]
    w_raw = w0 + jnp.tanh(wd) @ w_up.astype(jnp.float32)
    decay = jnp.exp(-jnp.exp(-jax.nn.softplus(-w_raw) - 0.5))
    a = jax.nn.sigmoid(a0 + ad @ a_up.astype(jnp.float32))
    kk = heads(k * k_k)
    kk = kk / jnp.maximum(jnp.sqrt(jnp.sum(kk * kk, axis=-1, keepdims=True)), L2_EPS)
    k = k * (1.0 + (a - 1.0) * k_a)
    rh, kh, vh, ah = heads(r), heads(k), heads(v), heads(a)
    S_T, y = wkv7_scan(S0, rh, heads(decay), kh, vh, -kk, kk * ah)
    mean = jnp.mean(y, axis=-1, keepdims=True)
    var = jnp.mean(jnp.square(y - mean), axis=-1, keepdims=True)
    y = ((y - mean) * lax.rsqrt(var + GN_EPS)).reshape(B, T, D_RWKV) * gn_w + gn_b
    y = y + (jnp.sum(rh * kh * r_k, axis=-1, keepdims=True) * vh).reshape(B, T, D_RWKV)
    return y * jax.nn.silu(g_r), S_T

def dilated_band_attention(q, k, v, slopes, window, dil):
    B, T, H, D = q.shape
    n_back = window // dil
    L = -(-T // dil)
    nb = -(-L // BLK)
    pad = nb * BLK * dil - T
    blockify = lambda t: jnp.pad(t, ((0, 0), (0, pad), (0, 0), (0, 0))).reshape(B, nb, BLK, dil, H, D)
    with_prev = lambda t: jnp.concatenate(
        [jnp.pad(t, ((0, 0), (1, 0), (0, 0), (0, 0), (0, 0), (0, 0)))[:, :-1], t], axis=2)
    qb = blockify(q)
    kc = with_prev(blockify(k))
    vc = with_prev(blockify(v))
    qi = jnp.arange(BLK)[:, None]
    kj = jnp.arange(2 * BLK)[None, :]
    off = BLK + qi - kj
    valid = ((off >= 0) & (off <= n_back))[None] & ((jnp.arange(nb)[:, None, None] > 0) | (kj[None] >= BLK))
    bias = -slopes[:, None, None] * (off * dil).astype(jnp.float32)[None]
    s = jnp.einsum('bnqrhd,bnkrhd->bnrhqk', qb, kc) + bias[None, None, None]
    s = jnp.where(valid[None, :, None, None], s, -jnp.inf)
    lse = jax.nn.logsumexp(s, axis=-1)
    p = jnp.exp(s - lse[..., None])
    o = jnp.einsum('bnrhqk,bnkrhd->bnqrhd', p, vc).reshape(B, nb * BLK * dil, H, D)[:, :T]
    lse = jnp.transpose(lse, (0, 1, 4, 2, 3)).reshape(B, nb * BLK * dil, H)[:, :T]
    return o, lse

def dilated_gather_attention(q, k_ext, v_ext, slopes, window, dil, buf):
    S = q.shape[1]
    n_keys = window // dil + 1
    offs = jnp.arange(n_keys) * dil
    idx = buf + jnp.arange(S)[:, None] - offs[None, :]
    valid = idx >= 0
    idx = jnp.maximum(idx, 0)
    kg = k_ext[:, idx]
    vg = v_ext[:, idx]
    s = jnp.einsum('bshd,bsjhd->bshj', q, kg) - slopes[None, None, :, None] * offs.astype(jnp.float32)[None, None, None, :]
    s = jnp.where(valid[None, :, None, :], s, -jnp.inf)
    lse = jax.nn.logsumexp(s, axis=-1)
    p = jnp.exp(s - lse[..., None])
    return jnp.einsum('bshj,bsjhd->bshd', p, vg), lse

def mixer_layer(x, shift_prev, S0, k_past, v_past, norm_w, w_in, mu_shift, w0, w_up, a0, a_up,
                k_k, k_a, r_k, gn_w, gn_b, q_norm, k_norm, w_out):
    B, T, _ = x.shape
    xn = rms_norm(x, norm_w).astype(w_in.dtype)
    z = jnp.einsum('btd,de->bte', xn, w_in).astype(jnp.float32)
    zs = z[..., :SHIFT_W]
    zs_prev = jnp.concatenate([shift_prev.astype(jnp.float32)[:, None], zs[:, :-1]], axis=1)
    zs_mix = zs + mu_shift.astype(jnp.float32) * (zs_prev - zs)
    o0 = SHIFT_W
    g_r = z[..., o0:o0 + D_RWKV]
    o0 += D_RWKV
    q = z[..., o0:o0 + D_ATT].reshape(B, T, N_ATT_HEADS, HEAD_DIM)
    ka = z[..., o0 + D_ATT:o0 + 2 * D_ATT].reshape(B, T, N_ATT_HEADS, HEAD_DIM)
    va = z[..., o0 + 2 * D_ATT:o0 + 3 * D_ATT].reshape(B, T, N_ATT_HEADS, HEAD_DIM)
    g_a = z[..., o0 + 3 * D_ATT:o0 + 4 * D_ATT]

    y_r, S_T = rwkv7_branch(zs_mix, g_r, S0, w0, w_up, a0, a_up, k_k, k_a, r_k, gn_w, gn_b)

    qn = rms_norm(q, q_norm) * (HEAD_DIM ** -0.5)
    kn = rms_norm(ka, k_norm)
    slopes = alibi_slopes(N_ATT_HEADS)
    if k_past is None:
        outs = [dilated_band_attention(qn, kn, va, slopes, w, d) for w, d in DIL_PATTERNS]
        keep = min(WIN_MAX, T)
        k_rows, v_rows = kn[:, T - keep:], va[:, T - keep:]
    else:
        buf = k_past.shape[1]
        k_ext = jnp.concatenate([k_past.astype(jnp.float32), kn], axis=1)
        v_ext = jnp.concatenate([v_past.astype(jnp.float32), va], axis=1)
        outs = [dilated_gather_attention(qn, k_ext, v_ext, slopes, w, d, buf) for w, d in DIL_PATTERNS]
        k_rows, v_rows = kn, va
    o_stack = jnp.stack([o for o, _ in outs])
    lse_stack = jnp.stack([l for _, l in outs])
    mix_w = jax.nn.softmax(lse_stack, axis=0)
    o_att = jnp.sum(mix_w[..., None] * o_stack, axis=0).reshape(B, T, D_ATT) * jax.nn.silu(g_a)

    mix = jnp.concatenate([y_r, o_att], axis=-1).astype(w_out.dtype)
    y = x + jnp.einsum('bte,ed->btd', mix, w_out).astype(x.dtype)
    return y, S_T, zs[:, -1], k_rows, v_rows

def setup_inputs(seed: int = 0) -> dict:
    key = jax.random.key(seed)
    ks = jax.random.split(key, 24)
    f32 = jnp.float32
    buf = min(WIN_MAX, PAST_LEN)
    nrm = lambda k, shape, s: s * jax.random.normal(k, shape, f32)
    return {
        'x_prompt': nrm(ks[0], (BATCH, SEQ, D_MODEL), 1.0),
        'x_sample': nrm(ks[1], (DEC_BATCH, DEC_SEQ, D_MODEL), 1.0),
        'state_wkv': nrm(ks[2], (DEC_BATCH, N_RWKV_HEADS, HEAD_DIM, HEAD_DIM), 0.3),
        'state_shift': nrm(ks[3], (DEC_BATCH, SHIFT_W), 1.0),
        'cache_k_win': nrm(ks[4], (DEC_BATCH, buf, N_ATT_HEADS, HEAD_DIM), 1.0),
        'cache_v_win': nrm(ks[5], (DEC_BATCH, buf, N_ATT_HEADS, HEAD_DIM), 1.0),
        'norm_w': 1.0 + nrm(ks[6], (D_MODEL,), 0.05),
        'w_in': nrm(ks[7], (D_MODEL, D_IN), D_MODEL ** -0.5),
        'mu_shift': jax.random.uniform(ks[8], (SHIFT_W,), f32, 0.0, 1.0),
        'w0': jax.random.uniform(ks[9], (D_RWKV,), f32, -2.5, 0.5),
        'w_up': nrm(ks[10], (LORA_W, D_RWKV), 0.5 * LORA_W ** -0.5),
        'a0': nrm(ks[11], (D_RWKV,), 0.5),
        'a_up': nrm(ks[12], (LORA_A, D_RWKV), 0.5 * LORA_A ** -0.5),
        'k_k': 0.85 + nrm(ks[13], (D_RWKV,), 0.05),
        'k_a': 1.0 + nrm(ks[14], (D_RWKV,), 0.05),
        'r_k': nrm(ks[15], (N_RWKV_HEADS, HEAD_DIM), 0.1),
        'gn_w': 1.0 + nrm(ks[16], (D_RWKV,), 0.05),
        'gn_b': nrm(ks[17], (D_RWKV,), 0.05),
        'q_norm': 1.0 + nrm(ks[18], (HEAD_DIM,), 0.05),
        'k_norm': 1.0 + nrm(ks[19], (HEAD_DIM,), 0.05),
        'w_out': nrm(ks[20], (D_MIX, D_MODEL), D_MIX ** -0.5),
    }

def reference(x_prompt, x_sample, state_wkv, state_shift, cache_k_win, cache_v_win,
              norm_w, w_in, mu_shift, w0, w_up, a0, a_up, k_k, k_a, r_k, gn_w, gn_b,
              q_norm, k_norm, w_out):
    weights = (norm_w, w_in, mu_shift, w0, w_up, a0, a_up, k_k, k_a, r_k, gn_w, gn_b, q_norm, k_norm, w_out)
    B = x_prompt.shape[0]
    shift0 = jnp.zeros((B, SHIFT_W), jnp.float32)
    S0 = jnp.zeros((B, N_RWKV_HEADS, HEAD_DIM, HEAD_DIM), jnp.float32)
    y_prompt, wkv_p, shift_p, k_p, v_p = mixer_layer(x_prompt, shift0, S0, None, None, *weights)
    y_sample, wkv_s, shift_s, k_s, v_s = mixer_layer(
        x_sample, state_shift, state_wkv.astype(jnp.float32), cache_k_win, cache_v_win, *weights)
    return (y_prompt, y_sample,
            wkv_p.astype(state_wkv.dtype), shift_p.astype(state_shift.dtype),
            k_p.astype(cache_k_win.dtype), v_p.astype(cache_v_win.dtype),
            wkv_s.astype(state_wkv.dtype), shift_s.astype(state_shift.dtype),
            k_s.astype(cache_k_win.dtype), v_s.astype(cache_v_win.dtype))


_drawn_inputs = setup_inputs


def setup_inputs(seed=0):
    import zlib

    import numpy as np

    out = dict(_drawn_inputs(seed))
    spreads = {}
    factors = {'k_k': 3.301, 'gn_w': 2.974, 'gn_b': 3.022, 'q_norm': 8.0}
    for name, (base, spread) in spreads.items():
        noise = np.random.default_rng([zlib.crc32(name.encode()), seed]).standard_normal(out[name].shape)
        drawn = base * np.exp(spread * noise) if base else spread * noise
        out[name] = __import__('jax').numpy.asarray(drawn.astype(out[name].dtype))
    for name, factor in factors.items():
        out[name] = (out[name] * factor).astype(out[name].dtype)
    return out
```

```python
from contextlib import ExitStack

import numpy as np

import concourse.bass as bass
from concourse import mybir
from concourse.alu_op_type import AluOpType as ALU

ACT = mybir.ActivationFunctionType
F32 = mybir.dt.float32
F32R = mybir.dt.float32r

D = 2048
T = 512
NB = 8
TT = T + NB
HT = TT // 2
HD = 64
DR = D // 2
NH = DR // HD
PAIRS = NH // 2
KT = D // 128
LORA = 96
SHIFT = 3 * DR + 2 * LORA
DIN = SHIFT + DR + 4 * DR
OFF_A = (0, DR, 2 * DR, SHIFT)
OFF_B = tuple(SHIFT + DR * (1 + j) for j in range(4))
C = 128
NC = T // C
MID = C // 2 - 1
LEVELS = 7
WIN = 2048
DEC = float(np.exp(-0.5))
RMS_EPS = 1e-6
GN_EPS = 64e-5
L2_EPS = 1e-12
BIG = 1e30
LNS = 30
TS = (128, 97, 96)
NS = sum(TS)

PV = ("mu_r", "mu_k", "mu_v", "w0", "a0", "k_k", "k_a", "r_k", "gn_w", "gn_b")
NPV = len(PV)
ROW_NW = NPV * 8
ROW_MU = ROW_NW + KT
ROW_QK = ROW_MU + 2
ROWS = ROW_QK + 2
N_ROWS = NPV + 1 + 1 + 4


def multiplicity(dist):
    dist = np.asarray(dist)
    ok = dist >= 0
    return ((ok & (dist <= 128)).astype(np.float32) + (ok & (dist % 4 == 0) & (dist <= 512))
            + (ok & (dist % 16 == 0) & (dist <= 2048))).astype(np.float32)


def constants():
    p = np.arange(128)[:, None]
    f = np.arange(128)[None, :]
    out = {}
    out["ident"] = (p == f)
    out["blk"] = (p // HD == f // HD)
    out["blkmean"] = (p // HD == f // HD) / HD
    out["causal"] = np.concatenate([p < f, p < f, p <= f, p <= f], axis=1)
    for lv in range(LEVELS):
        m = 2 ** lv
        out[f"lev{lv}"] = (p // (2 * m) == f // (2 * m)) & (p % (2 * m) >= m) & (f % (2 * m) < m)
    out["lev0t"] = out["lev0"].T
    out["carry"] = np.broadcast_to((np.arange(T)[None, :] % C != 0), (128, T))
    ca = {k: np.ascontiguousarray(v, dtype=np.float32) for k, v in out.items()}
    slopes = 2.0 ** (-8.0 * np.arange(1, NH + 1) / NH)
    dist = (T - 128) + p - np.arange(T)[None, :]
    mult = multiplicity(dist)
    cb = {"dist": np.where(mult > 0, -dist, -BIG), "mult": mult,
          "slope": np.broadcast_to(slopes[None, :], (128, NH))}
    ds = np.concatenate([128 - np.arange(128), 512 - 4 * np.arange(96), [0], 2048 - 16 * np.arange(96)])
    cb["sdist"] = np.broadcast_to(-ds[None, :], (128, NS))
    cb["smult"] = np.broadcast_to(multiplicity(ds)[None, :], (128, NS))
    cb["sslope"] = slopes[2 * np.arange(PAIRS)[None, :] + (np.arange(128) % 2)[:, None]]
    cb = {k: np.ascontiguousarray(v, dtype=np.float32) for k, v in cb.items()}
    return ca, cb


CONST_A, CONST_B = constants()


def layout(table):
    at, n = {}, 0
    for k, v in table.items():
        at[k] = (n, n + v.shape[1])
        n += v.shape[1]
    return at, n


AT_A, NCA = layout(CONST_A)
AT_B, NCB = layout(CONST_B)


class Steps:

    def __init__(self, names):
        self.names = names
        self.n = len(names)
        self.index = {k: j for j, k in enumerate(names)}
        assert len(self.index) == self.n
        self.turn = 0

    def at(self, i, name):
        return i * self.n + (self.index[name] + 1)

    def start(self, i):
        return i * self.n

    def one(self, name):
        assert self.names[self.turn % self.n] == name, (self.names[self.turn % self.n], name)
        self.turn += 1
        return 1


class Arena:
    def __init__(self, base, size):
        self.base, self.size, self.pos = base, size, 0

    def take(self, *shape):
        n = int(np.prod(shape))
        a = self.base[:, self.pos:self.pos + n]
        self.pos += n
        assert self.pos <= self.size, (self.pos, self.size)
        if len(shape) == 2:
            a = a.rearrange("p (a b) -> p a b", a=shape[0])
        elif len(shape) == 3:
            a = a.rearrange("p (a b c) -> p a b c", a=shape[0], b=shape[1])
        return a


LV = range(1, LEVELS)
GRAMS = ("gb0", "gk0", "gb1", "gk1", "nn01", "gb2", "gk2", "gb3", "gk3", "nn23")
UNITS = 4 * KT
BEHIND_A = {"lora": 6, "kk": 3, "tail": 3, "bonus": 4, "vec": 12, "gb0": 1, "nn23": 1,
            **{f"{s}{l}b": 1 for l in LV for s in ("qt", "dx", "tr") if (l, s) != (LEVELS - 1, "tr")},
            **{f"{s}{c}": 1 for c in range(NC) for s in ("rhs", "u", "s")},
            "mean": 2, "var": 3}
QB = T // 128
JS = [(h, b) for h in range(2) for b in range(QB)]
BEHIND_B = {"ssum": 8, "tokv": 2, "stok": 2, "qb": 8, "s0": 2,
            **{f"{s}{j}": 2 for j in range(len(JS)) for s in ("s", "t")},
            "sct": 3, "pwt": 3, "av": 0}


def spread(behind, names):
    behind = dict(behind)
    behind[names[-1]] = behind.get(names[-1], 0) + UNITS - sum(behind.values())
    assert behind[names[-1]] >= 0, behind[names[-1]]
    out, at = {}, 0
    for k in names:
        out[k] = range(at, at + behind.get(k, 0))
        at += behind.get(k, 0)
    return out


def build(nc, x_prompt, x_sample, state_wkv, state_shift, cache_k, cache_v, norm_w, w_in, mu_shift,
          w0, w_up, a0, a_up, k_k, k_a, r_k, gn_w, gn_b, q_norm, k_norm, w_out, const_a, const_b,
          y_prompt, y_sample, wkv_p, shift_p, k_p, v_p, wkv_s, shift_s, k_s, v_s):
    w_view = w_in.rearrange("(t p) n -> p t n", p=128)
    wo_view = w_out.rearrange("(t p) n -> p t n", p=128)
    xp = x_prompt[0].rearrange("(t p) d -> p t d", p=128)
    xs = x_sample[:, 0, :]
    yp = y_prompt[0].rearrange("(t p) d -> p t d", p=128)
    ys = y_sample[:, 0, :]
    kc_view = cache_k.rearrange("b s h d -> s b (h d)")
    vc_view = cache_v.rearrange("b s h d -> s b (h d)")
    kp_view = k_p[0].rearrange("(t p) h d -> p t (h d)", p=128)
    vp_view = v_p[0].rearrange("(t p) h d -> p t (h d)", p=128)
    ks_view = k_s[:, 0].rearrange("b h d -> b (h d)")
    vs_view = v_s[:, 0].rearrange("b h d -> b (h d)")
    mix_d = nc.dram_tensor("mix_scratch", (D, TT), F32, kind="Internal").ap()
    vec_d = nc.dram_tensor("vec_scratch", (8, NB, DR), F32, kind="Internal").ap()
    ys_d = nc.dram_tensor("ysample_scratch", (NB, DR), F32, kind="Internal").ap()

    with ExitStack() as ctx:
        def sb(name, shape, dt=F32):
            return ctx.enter_context(nc.sbuf_tensor(name, shape, dt))

        def sem(name):
            return ctx.enter_context(nc.semaphore(name))

        XH = sb("XH", [128, KT, TT], F32R)
        XL = sb("XL", [128, KT, TT], F32R)
        WR = sb("WR", [128, 4, 8, 128])
        WH = sb("WH", [128, 2, 8, 128], F32R)
        WL = sb("WL", [128, 2, 8, 128], F32R)
        CA = sb("CA", [128, NCA])
        PT = sb("PT", [128, ROWS])
        SST = sb("SST", [128, 26, NB])
        BIAS = sb("BIAS", [128, 3])
        ARENA_N = 25460
        AREN = sb("AREN", [128, ARENA_N])
        ACC = [ctx.enter_context(nc.psum_tensor(f"acc{j}", [128, 2, 512], F32)) for j in range(2)]
        HB = ctx.enter_context(nc.psum_tensor("head_banks", [128, 4, 512], F32))
        ca = {k: CA[:, a:b] for k, (a, b) in AT_A.items()}
        ident, blk, blkmean = ca["ident"], ca["blk"], ca["blkmean"]

        def bc(a, n):
            return a.unsqueeze(1).to_broadcast([a.shape[0], n, a.shape[1]])

        s_const, s_rows, s_srow = sem("const_landed"), sem("param_rows_landed"), sem("shift_rows_landed")
        s_xt = [sem(f"x_landed{t}") for t in range(5)]
        s_w = [sem(f"w_landed{j}") for j in range(4)]
        s_lu = sem("lora_up_landed")
        s_hi, s_lo = sem("half_rounded"), sem("half_rest")
        s_half, s_evac = sem("half_multiplied"), sem("tile_evacuated")
        s_zero = sem("pair_buffers_zeroed")
        p_pe, p_act, p_dve, p_pool = sem("pro_pe"), sem("pro_act"), sem("pro_dve"), sem("pro_pool")
        a_pe, a_act, a_dve, a_pool = sem("a_pe"), sem("a_act"), sem("a_dve"), sem("a_pool")
        b_pe, b_act, b_dve, b_pool = sem("b_pe"), sem("b_act"), sem("b_dve"), sem("b_pool")
        c_pe, c_act, c_dve, c_pool = sem("c_pe"), sem("c_act"), sem("c_dve"), sem("c_pool")
        s_passed = sem("waits_passed")
        r_act, r_dve = sem("r_act"), sem("r_dve")
        o_ltail, o_tail, o_vec, o_state, o_mix = (sem("lora_tail_out"), sem("tail_out"), sem("vec_out"),
                                                  sem("state_out"), sem("mix_out"))
        o_k, o_v, o_skv = sem("k_out"), sem("v_out"), sem("sample_kv_out")
        s_krow, s_vrow = sem("k_row_landed"), sem("v_row_landed")
        s_kc, s_vc = sem("k_cache_landed"), sem("v_cache_landed")
        s_cb = sem("const_b_landed")
        s_sv, s_sst, o_sst = sem("sample_vectors_landed"), sem("sample_state_landed"), sem("sample_state_out")
        o_ys, s_mt = sem("ysample_out"), sem("mix_landed")
        s_xr = [sem(f"x_again{j}") for j in range(2)]
        o_y = [sem(f"y_out{j}") for j in range(2)]

        pro = Arena(AREN, ARENA_N)
        XTOK = pro.take(5, D)
        ROWT = pro.take(128)
        SROW = pro.take(SHIFT)
        SSQ = pro.take(16)
        XF = pro.take(2, TT)
        SQJ = pro.take(D)
        aa = Arena(AREN, ARENA_N)
        TW, AD = aa.take(TT), aa.take(TT)
        LU = aa.take(2, 128)
        z_at, z_end = aa.pos, aa.pos + 4 * (TT + 1)
        Z = aa.take(4, TT + 1)
        PAR, SSP = aa.take(NPV), aa.take(3, NB)
        M3 = aa.take(3, TT)
        A_, GG, BON = aa.take(TT), aa.take(TT), aa.take(TT)
        DCS = aa.take(NB)
        GL, G = aa.take(NC), aa.take(NC)
        BT, KTL = aa.take(T), aa.take(T)
        ARP = aa.take(NC, 4, C)
        TOKB, TOKK, TOKV = aa.take(NC, 128), aa.take(NC, 128), aa.take(NC, 128)
        GB, GK = aa.take(NC, 4, C), aa.take(NC, 4, C)
        NN = aa.take(2 * NC, C)
        RHS, U, S = aa.take(2, 128), aa.take(NC, 128), aa.take(NC + 1, 128)
        ST = aa.take(128)
        TAIL = aa.take(3, 128)
        VEC = aa.take(8, 128)
        early = aa.pos
        SGW, KSQ, SSM, RN = aa.take(TT), aa.take(TT), aa.take(TT), aa.take(TT)
        LS, LC = aa.take(T), aa.take(NC, C + 1)
        E1, E2 = aa.take(NC, C + 1), aa.take(NC, C + 1)
        KP, KK, KKA, T1 = aa.take(TT), aa.take(TT), aa.take(TT), aa.take(TT)
        D3 = AREN[:, early + TT * 2:early + TT * 5].rearrange("p (a b) -> p a b", a=3)
        late = Arena(AREN, ARENA_N)
        late.pos = early
        NM = [late.take(8, C), late.take(8, C)]
        X, XT, QT = late.take(8, C), late.take(8, C), late.take(8, C)
        Y = AREN[:, early:early + T]
        YC = AREN[:, early + T:early + 2 * T]
        YSQ = AREN[:, early + 2 * T:early + 3 * T]
        MIXO = BT
        lo = Arena(AREN, ARENA_N)
        lo.pos = pro.pos
        ZL, DL, ML = lo.take(2, TT + 1), lo.take(2, TT), lo.take(2, TT)
        LTAIL = lo.take(2, LORA)
        ba = Arena(AREN, ARENA_N)
        PTR = ba.take(2, T)
        SL, SSL, QW, QS = ba.take(2), ba.take(1), ba.take(2), ba.take(NB)
        MX, ZS, RZ, SMX = ba.take(8), ba.take(8), ba.take(8), ba.take(4)
        PW, SCO = ba.take(3, 16), ba.take(3, 16)
        ZB = Z[:, :, 1:TT + 1]
        assert ba.pos <= z_at
        ba.pos = z_end
        SQ, LN, RNB = ba.take(2, TT), ba.take(2, TT), ba.take(2, TT)
        QP = ba.take(2, TT)
        KN, GGB = ba.take(TT), ba.take(TT)
        KTOK, VTOK = ba.take(QB, 128), ba.take(QB, 128)
        SKV = ba.take(2, 128)
        BTB = ba.take(2, T)
        SC2, EE, PP = ba.take(2, T), ba.take(2, T), ba.take(2, T)
        DG = ba.take(2, 128)
        MIXB = ba.take(TT)
        PR = ba.take(NB, 128)
        BTS = ba.take(NS)
        SS_, SE, SP_, SPN = ba.take(NS), ba.take(NS), ba.take(NS), ba.take(NS)
        behind_r = ARENA_N - NCB - 2 * 3 * NB * 128
        assert ba.pos <= behind_r
        ba.pos = behind_r
        CB = ba.take(NCB)
        cb = {k: CB[:, a:b] for k, (a, b) in AT_B.items()}
        KC, VC = ba.take(3, NB, 128), ba.take(3, NB, 128)
        ra = Arena(AREN, ARENA_N)
        ra.pos = z_end
        SV = ra.take(8, HD)
        SG = ra.take(2, HD)
        S0, S1 = ra.take(HD, HD), ra.take(HD, HD)
        PX = ra.take(HD, HD)
        SA, YR, YQ, YD = ra.take(HD), ra.take(HD), ra.take(HD), ra.take(HD)
        SM = ra.take(4)
        assert ra.pos <= behind_r
        cc = Arena(AREN, ARENA_N)
        MT = cc.take(KT, TT)
        YB = cc.take(DR)
        YT = cc.take(2, TT)
        XR, XRS = cc.take(2, 4, 128), cc.take(2, 128)
        YO, YOS = cc.take(2, 4, 128), cc.take(2, 128)

        PE_P = Steps(["rows", "shift", *[f"x{k}" for k in range(KT)], "ltail"])
        ACT_P = Steps([*[f"sq{t}" for t in range(5)], "ln", "rs",
                       *[f"xf{k}" for k in range(KT)], "tanh", "ltail"])
        DVE_P = Steps(["zrow", "bias", "rows", "shift", *[f"xn{t}" for t in range(5)],
                       *[f"hi{k}" for k in range(KT)], "lz", "ldiff", "lds", "lmix"])
        POOL_P = Steps([f"lo{k}" for k in range(KT)])
        last = LEVELS - 1
        PE_A = Steps(["lora", "kk", "tail", "bonus", "vec", *GRAMS, "tokb", "tokk", "tokv",
                      *[f"{s}{l}{h}" for l in LV for s in ("qt", "dx", "tr") for h in "ab"
                        if (l, s) != (last, "tr")],
                      *[f"{s}{c}" for c in range(NC) for s in ("rhs", "u", "s", "y")],
                      "st", "mean", "var"])
        ACT_A = Steps(["sgw", "sga", "sgg", "ksq", "tail", "ln", "rn", "e1", "e2", "g", "dcs", "vec",
                       "nn01", "nn23", "tokb", "tokk", "tokv",
                       *[f"{s}{l}" for l in LV for s in ("qt", "tr") if (l, s) != (last, "tr")],
                       *[f"{s}{c}" for c in range(NC) for s in ("rhs", "u")],
                       "st", "y", "ysq", "yln", "yrs"])
        DVE_A = Steps(["par", "dsh", "dss", "mix", "t1", "kp", "prod", "scan", "lcm", "lc0", "gl0", "gl",
                       "ssm", "gate", "kt", "rt", "bon", "kk", "at", "kka", "bt",
                       "gb0", "gk0", "gb1", "gk1", "gb2", "gk2", "gb3", "gk3", "x0", "xt0",
                       *[f"{s}{l}" for l in LV for s in ("qt", "xa", "xb", "tr")
                         if (l, s) != (last, "tr")],
                       *[f"s{c}" for c in range(NC)], "yc", "yn", "yb", "ym"])
        POOL_A = Steps(["nm0", "nt0", *[f"nm{l}" for l in LV]])
        nj = len(JS)
        seq = ["s0"] + [x for j in range(nj) for x in ([f"s{j + 1}"] if j + 1 < nj else []) + [f"t{j}", f"o{j}"]]
        PE_B = Steps(["ssum", "tokk", "tokv", "stok", "qb", *seq, "sct", "pwt", "av"])
        ACT_B = Steps(["sq", "sgg", "ln", "rn", "tokk", "tokv", "stok",
                       *[x for j in range(nj) for x in (f"ex{j}", f"tp{j}")], "sex", "pwc"])
        DVE_B = Steps(["sl", "qn", "kn", "qs", "gate",
                       *[x for t in range(3) for x in (f"pr{t}", f"rd{t}")],
                       "mx0", *[x for j in range(nj) for x in
                                ([f"mx{j + 1}"] if j + 1 < nj else []) + [f"pm{j}", f"rz{j}", f"dg{j}"]],
                       "smx", "spm", "srz", "spn", "mixp", "mixs"])
        POOL_B = Steps(["bt", "bts"])
        DVE_R = Steps(["p1", "sa", "sw", "p2", "sb", "p3", "sc", "p4", "y", "m", "ms", "yd", "v", "vs",
                       "rz", "rs", "yg", "yb", "yo"])
        ACT_R = Steps(["ln"])
        ACT_CP = Steps(["yb", *[f"hi{k}" for k in range(KT)]])
        DVE_C = Steps(["ya", "yb"])

        span_a, span_b = spread(BEHIND_A, PE_A.names), spread(BEHIND_B, PE_B.names)

        def group_a(i):
            return i * 2 + 1

        def group_b(i):
            return i * 2 + (1 + 2 * PAIRS)

        GROUP_C = 1 + 4 * PAIRS

        def load_half(sp, g, k, src):
            if not (isinstance(g, int) and 4 * g + k < 4):
                sp.wait_ge(s_hi, g * 4 + (k - 3))
                sp.wait_ge(s_lo, g * 4 + (k - 3))
            sp.dma_start(WR[:, k % 4, :, 0:src.shape[2]], src).then_inc(s_w[k % 4], 16)

        def round_half(act, g, k, M=128):
            act.wait_ge(s_w[k % 4], (g + (k // 4 + 1)) * 16)
            if not (isinstance(g, int) and 4 * g + k < 2):
                act.wait_ge(s_half, g * 4 + (k - 1))
            act.activation(WH[:, k % 2, :, 0:M], WR[:, k % 4, :, 0:M], ACT.Copy).then_inc(s_hi, 1)

        def rest_half(pool, g, k, M=128):
            pool.wait_ge(s_w[k % 4], (g + (k // 4 + 1)) * 16)
            pool.wait_ge(s_hi, g * 4 + (k + 1))
            if not (isinstance(g, int) and 4 * g + k < 2):
                pool.wait_ge(s_half, g * 4 + (k - 1))
            pool.tensor_tensor(WL[:, k % 2, :, 0:M], WR[:, k % 4, :, 0:M],
                               WH[:, k % 2, :, 0:M].bitcast(F32), ALU.subtract).then_inc(s_lo, 1)

        def multiply_unit(pe, g, u, M=128):
            t, kt, k = u // KT, u % KT, u // 8
            if u % 8 == 0:
                pe.wait_ge(s_lo, g * 4 + (k + 1))
            if kt == 0 and not (isinstance(g, int) and 2 * g + t < 2):
                pe.wait_ge(s_evac, g * 2 + (t - 1))
            acc = ACC[t % 2]
            j = kt % 8
            for n, (w, x) in enumerate(((WH, XH), (WH, XL), (WL, XH))):
                for hf in range(2):
                    mm = pe.matmul(acc[0:M, hf, 0:HT], w[:, k % 2, j, 0:M], x[:, kt, hf * HT:(hf + 1) * HT],
                                   start=(kt == 0 and n == 0), stop=(kt == KT - 1 and n == 2))
            if u % 8 == 7:
                mm.then_inc(s_half, 1)

        def evacuate(act, g, t, dst, M=128):
            act.wait_ge(s_half, g * 4 + (2 * t + 2))
            act.activation(dst, ACC[t % 2][0:M, :, 0:HT], ACT.Copy).then_inc(s_evac, 1)

        def two(a):
            return a.rearrange("p (a b) -> p a b", a=2)

        def pe_fill(pe, span, g, name):
            for u in span[name]:
                multiply_unit(pe, g, u)

        def act_feed(act, span, g, name, dst, ahead=True):
            for u in span[name]:
                if u % 8 == 4 and (ahead or u // 8 < 7):
                    round_half(act, g, u // 8 + 1)
                if u % KT == KT - 1:
                    evacuate(act, g, u // KT, dst(u // KT))

        def pool_feed(pool, span, g, name, ahead=True):
            for u in span[name]:
                if u % 8 == 4 and (ahead or u // 8 < 7):
                    rest_half(pool, g, u // 8 + 1)

        block = ctx.enter_context(nc.Block())
        HBF = HB[:, :, :].rearrange("p a b -> p (a b)")
        par_view = PT[:, 0:8 * NPV].rearrange("p (v i) -> p i v", i=8)
        ssp_view = SST[:, 0:24, :].rearrange("p (s i) b -> p i s b", i=8)
        P_ = {k: PAR[:, j:j + 1] for j, k in enumerate(PV)}
        eps_rms, eps_gn, ln_back = BIAS[:, 0:1], BIAS[:, 1:2], BIAS[:, 2:3]

        def w_half(off, i, k):
            cols = w_view[:, :, off:off + DR].rearrange("p t (i c) -> p t i c", i=PAIRS)
            return cols[:, 8 * (k % 2):8 * (k % 2) + 8, i, :]

        @block.sync
        def _(sp):
            sp.dma_start(CA[:, :], const_a).then_inc(s_const, 16)
            for t in range(4):
                sp.dma_start(XTOK[:, t, :], xp[:, t, :]).then_inc(s_xt[t], 16)
            sp.dma_start(XTOK[0:NB, 4, :], xs).then_inc(s_xt[4], 16)
            for k in range(4):
                src = w_view[:, 8 * (k % 2):8 * (k % 2) + 8, 3 * DR + LORA * (k // 2):3 * DR + LORA * (k // 2 + 1)]
                load_half(sp, 0, k, src)
            for k in range(8):
                load_half(sp, group_a(0), k, w_half(OFF_A[k // 2], 0, k))

            def lora_up(i):
                if not isinstance(i, int) or i > 0:
                    sp.wait_ge(a_pe, PE_A.at(i - 1, "lora"))
                else:
                    sp.wait_ge(p_pe, PE_P.at(0, f"x{KT - 1}"))
                up = (w_up, a_up)
                for j in range(2):
                    sp.dma_start(LU[0:LORA, j, :], up[j].rearrange("l (i c) -> l i c", i=PAIRS)[:, i, :]).then_inc(s_lu, 16)

            lora_up(0)
            with sp.Fori(1, PAIRS) as i:
                for k in range(8):
                    load_half(sp, group_a(i), k, w_half(OFF_A[k // 2], i, k))
                    if k == 3:
                        lora_up(i)

            def phase_a_done():
                sp.wait_ge(a_pe, PE_A.start(PAIRS))
                sp.wait_ge(a_act, ACT_A.start(PAIRS))
                sp.wait_ge(a_dve, DVE_A.start(PAIRS))
                sp.wait_ge(a_pool, POOL_A.start(PAIRS))
                sp.wait_ge(o_mix, 16 * PAIRS)
                sp.wait_ge(o_vec, 16 * PAIRS)
                sp.wait_ge(o_state, 32 * PAIRS)
                sp.wait_ge(o_tail, 32 * PAIRS)

            def caches(i):
                if not isinstance(i, int) or i > 0:
                    sp.wait_ge(b_dve, DVE_B.at(i - 1, "pr2"))
                for n, (dst, view, s) in enumerate(((KC, kc_view, s_kc), (VC, vc_view, s_vc))):
                    if n == 1 and (not isinstance(i, int) or i > 0):
                        sp.wait_ge(b_pe, PE_B.at(i - 1, "av"))
                    cols = view.rearrange("s b (i c) -> s b i c", i=PAIRS)
                    sp.dma_start(dst[:, 0, :, :], cols[WIN - 128:WIN, :, i, :]).then_inc(s, 16)
                    sp.dma_start(dst[0:96, 1, :, :], cols[WIN - 512:WIN - 128:4, :, i, :]).then_inc(s, 16)
                    sp.dma_start(dst[0:96, 2, :, :], cols[0:WIN - 512:16, :, i, :]).then_inc(s, 16)

            def group_b_on(i):
                for k in range(1, 8):
                    load_half(sp, group_b(i), k, w_half(OFF_B[k // 2], i, k))
                load_half(sp, group_b(i), 8, w_half(OFF_B[0], i + 1, 0))

            load_half(sp, group_b(0), 0, w_half(OFF_B[0], 0, 0))
            group_b_on(0)
            phase_a_done()
            sp.dma_start(SV, vec_d.rearrange("v b (h d) -> (b h) v d", d=HD)).then_inc(s_sv, 16)
            for j, v in enumerate((gn_w, gn_b)):
                for b in range(NB):
                    sp.dma_start(SG[NH * b:NH * (b + 1), j, :], v.rearrange("(h d) -> h d", d=HD)).then_inc(s_sv, 16)
            sp.dma_start(S0, state_wkv.rearrange("b h v k -> (b h) v k")).then_inc(s_sst, 16)
            sp.dma_start(CB, const_b).then_inc(s_cb, 16)
            caches(0)
            with sp.Fori(1, PAIRS - 1) as i:
                group_b_on(i)
                caches(i)
            for k in range(1, 8):
                load_half(sp, group_b(PAIRS - 1), k, w_half(OFF_B[k // 2], PAIRS - 1, k))
            wo_half = lambda m, k: (wo_view.rearrange("p t (m u c) -> p t m u c", u=2, c=128)
                                    [:, 8 * (k % 2):8 * (k % 2) + 8, m, k // 2, :])
            load_half(sp, GROUP_C, 0, wo_half(0, 0))
            caches(PAIRS - 1)

            def x_again(m, t):
                cols = xp.rearrange("p t (m u c) -> p t m u c", u=2, c=128)
                scol = xs.rearrange("b (m u c) -> b m u c", u=2, c=128)
                sp.wait_ge(c_dve, DVE_C.start(m))
                sp.dma_start(XR[:, t, :, :], cols[:, :, m, t, :]).then_inc(s_xr[t], 16)
                sp.dma_start(XRS[0:NB, t, :], scol[:, m, t, :]).then_inc(s_xr[t], 16)

            for k in range(1, 4):
                load_half(sp, GROUP_C, k, wo_half(0, k))
            sp.wait_ge(c_act, ACT_CP.n)
            for t in range(2):
                x_again(0, t)
            with sp.Fori(1, D // 256) as m:
                for k in range(4):
                    load_half(sp, m + GROUP_C, k, wo_half(m, k))
                for t in range(2):
                    x_again(m, t)

        @block.gpsimd
        def _(pool):
            for k in range(KT):
                pool.wait_ge(p_dve, DVE_P.at(0, f"hi{k}"))
                pool.tensor_tensor(XL[:, k, :], XF[:, k % 2, :], XH[:, k, :].bitcast(F32),
                                   ALU.subtract).then_inc(p_pool, POOL_P.one(f"lo{k}"))
            for k in range(4):
                rest_half(pool, 0, k, LORA)
            for k in range(9):
                rest_half(pool, group_a(0), k)

            def pair_a(i, g, ahead=True):
                def feed(name):
                    pool_feed(pool, span_a, g, name, ahead)

                for name in ("lora", "kk", "tail", "bonus", "vec", *GRAMS):
                    feed(name)
                pool.wait_ge(a_act, ACT_A.at(i, "nn23"))
                pool.tensor_tensor(NM[0], NN, bc(ca["lev0"], 8), ALU.mult).then_inc(a_pool, POOL_A.one("nm0"))
                pool.wait_ge(a_dve, DVE_A.at(i, "gk3"))
                for h in range(2):
                    nt = pool.tensor_tensor(NM[1].rearrange("p (c h) t -> p c h t", h=2)[:, :, h, :], GB[:, :, h, :],
                                            bc(ca["lev0t"], NC), ALU.mult)
                nt.then_inc(a_pool, POOL_A.one("nt0"))
                for l in LV:
                    if l <= 2:
                        pool.wait_ge(a_dve, DVE_A.at(i, ("x0", "xt0")[l - 1]))
                    else:
                        pool.wait_ge(a_pe, PE_A.at(i, f"qt{l - 2}b"))
                    pool.tensor_tensor(NM[(l - 1) % 2], NN, bc(ca[f"lev{l}"], 8), ALU.mult)\
                        .then_inc(a_pool, POOL_A.one(f"nm{l}"))
                    for s in ("qt", "dx", "tr") if l < last else ():
                        for h in "ab":
                            feed(f"{s}{l}{h}")
                for name in PE_A.names[PE_A.index[f"qt{last}a"]:]:
                    feed(name)

            with pool.Fori(0, PAIRS - 1) as i:
                pair_a(i, group_a(i + 1))
            pair_a(PAIRS - 1, group_b(0))

            def pair_b(i, g, ahead=True, fill=True):
                def feed(name):
                    if fill:
                        pool_feed(pool, span_b, g, name, ahead)

                feed("ssum")
                pool.wait_ge(b_dve, DVE_B.at(i, "sl"))
                pool.sem_inc(s_passed, 1)
                pool.wait_ge(s_cb, 16)
                for h in range(2):
                    bt = pool.tensor_scalar(BTB[:, h, :], cb["dist"], SL[:, h:h + 1], 1.0, ALU.mult, ALU.mult)
                bt.then_inc(b_pool, POOL_B.one("bt"))
                pool.tensor_scalar(BTS[0:16, :], cb["sdist"][0:16, :], SSL[0:16, :], 1.0, ALU.mult, ALU.mult)\
                    .then_inc(b_pool, POOL_B.one("bts"))
                for name in PE_B.names[1:]:
                    feed(name)

            with pool.Fori(0, PAIRS - 1) as i:
                pair_b(i, group_b(i + 1))
            pair_b(PAIRS - 1, 0, fill=False)

            for k in range(KT):
                pool.wait_ge(c_act, ACT_CP.at(0, f"hi{k}"))
                pool.tensor_tensor(XL[:, k, :], MT[:, k, :], XH[:, k, :].bitcast(F32),
                                   ALU.subtract).then_inc(c_pool, 1)
            for k in range(1, 4):
                rest_half(pool, GROUP_C, k)
            with pool.Fori(1, D // 256) as m:
                for k in range(4):
                    rest_half(pool, m + GROUP_C, k)

        @block.tensor
        def _(pe):
            pe.wait_ge(s_const, 16)
            pe.wait_ge(s_rows, 16 * N_ROWS)
            pe.transpose(HB[:, 0, 0:ROWS], ROWT[0:ROWS, :], ident[0:ROWS, 0:ROWS]).then_inc(p_pe, PE_P.one("rows"))
            pe.wait_ge(s_srow, 16)
            for j in range(24):
                pe.transpose(HB[:, 1, NB * j:NB * (j + 1)], SROW[0:NB, 128 * j:128 * (j + 1)], ident[0:NB, 0:NB])
            for j in range(2):
                tr = pe.transpose(HB[0:LORA, 1, NB * (24 + j):NB * (25 + j)],
                                  SROW[0:NB, 3 * DR + LORA * j:3 * DR + LORA * (j + 1)], ident[0:NB, 0:NB])
            tr.then_inc(p_pe, PE_P.one("shift"))
            for k in range(KT):
                b = k % 2
                if k == 0:
                    pe.wait_ge(p_dve, DVE_P.at(0, "xn4"))
                if k < 2:
                    pe.wait_ge(p_dve, DVE_P.at(0, "shift"))
                else:
                    pe.wait_ge(p_act, ACT_P.at(0, f"xf{k - 2}"))
                for t in range(4):
                    pe.transpose(HB[:, 2 * b, 128 * t:128 * (t + 1)], XTOK[:, t, 128 * k:128 * (k + 1)], ident)
                pe.transpose(HB[:, 2 * b + 1, 0:NB], XTOK[0:NB, 4, 128 * k:128 * (k + 1)], ident[0:NB, 0:NB])\
                    .then_inc(p_pe, PE_P.one(f"x{k}"))
            pe.wait_ge(p_dve, DVE_P.at(0, f"hi{KT - 1}"))
            pe.wait_ge(p_pool, POOL_P.n)
            for u in range(2 * KT):
                multiply_unit(pe, 0, u, LORA)
            for u in range(UNITS):
                if u == 2 * KT:
                    pe.wait_ge(s_evac, 2)
                    for j in range(2):
                        tr = pe.transpose(HB[0:NB + 1, 0, LORA * j:LORA * (j + 1)], ZL[0:LORA, j, T:TT + 1],
                                          ident[0:LORA, 0:LORA])
                    tr.then_inc(p_pe, PE_P.one("ltail"))
                multiply_unit(pe, group_a(0), u)

            pe.wait_ge(p_act, ACT_P.n)

            def pair_a(i, g):
                def fill(name):
                    pe_fill(pe, span_a, g, name)

                def step(mm, name):
                    mm.then_inc(a_pe, PE_A.one(name))

                pe.wait_ge(s_lu, (i + 1) * 32)
                pe.wait_ge(a_act, ACT_A.start(i))
                pe.wait_ge(a_dve, DVE_A.start(i))
                for j, act_in in enumerate((TW, AD)):
                    for hf in range(2):
                        mm = pe.matmul(HB[:, 2 * j + hf, 0:HT], LU[0:LORA, j, :],
                                       act_in[0:LORA, hf * HT:(hf + 1) * HT], start=True, stop=True)
                mm.then_inc(a_pe, PE_A.one("lora"))
                fill("lora")
                pe.wait_ge(a_act, ACT_A.at(i, "ksq"))
                for hf in range(2):
                    mm = pe.matmul(HB[:, hf, 0:HT], blk, KSQ[:, hf * HT:(hf + 1) * HT], start=True, stop=True)
                mm.then_inc(a_pe, PE_A.one("kk"))
                fill("kk")
                for s in range(3):
                    mm = pe.transpose(HB[0:NB + 1, 2, 128 * s:128 * (s + 1)], Z[:, s, T:TT + 1], ident)
                mm.then_inc(a_pe, PE_A.one("tail"))
                fill("tail")
                pe.wait_ge(a_dve, DVE_A.at(i, "prod"))
                pe.wait_ge(a_act, ACT_A.at(i, "tail"))
                for hf in range(2):
                    mm = pe.matmul(HB[:, 2 + hf, 0:HT], blk, T1[:, hf * HT:(hf + 1) * HT], start=True, stop=True)
                mm.then_inc(a_pe, PE_A.one("bonus"))
                fill("bonus")
                pe.wait_ge(a_dve, DVE_A.at(i, "bt"))
                pe.wait_ge(a_act, ACT_A.at(i, "dcs"))
                for v, src in enumerate((M3[:, 0], None, KP, M3[:, 2], KK, KKA, GG, BON)):
                    src = DCS if src is None else src[:, T:TT]
                    mm = pe.transpose(HB[0:NB, v // 4, 128 * (v % 4):128 * (v % 4 + 1)], src, ident)
                mm.then_inc(a_pe, PE_A.one("vec"))
                fill("vec")
                read_by = {"gb0": (a_dve, DVE_A, "bon"), "gk0": (a_dve, DVE_A, "bon"),
                           "gb1": (a_act, ACT_A, "vec"), "gk1": (a_act, ACT_A, "vec"),
                           "nn01": (a_dve, DVE_A, "gb0"), "gb2": (a_dve, DVE_A, "gk0"),
                           "gk2": (a_dve, DVE_A, "gb1"), "gb3": (a_dve, DVE_A, "gk1"),
                           "gk3": (a_act, ACT_A, "nn01"), "nn23": (a_dve, DVE_A, "gb2"),
                           "tokb": (a_dve, DVE_A, "gk2"), "tokk": (a_dve, DVE_A, "gb3"),
                           "tokv": (a_dve, DVE_A, "gk3")}
                for n, name in enumerate((*GRAMS, "tokb", "tokk", "tokv")):
                    bank = (2 + n) % 4
                    s, steps, what = read_by[name]
                    pe.wait_ge(s, steps.at(i, what))
                    if name[:2] in ("gb", "gk"):
                        c = int(name[2])
                        lhs = (BT if name[1] == "b" else KTL)[:, c * C:(c + 1) * C]
                        mm = pe.matmul(HB[:, bank, :], lhs, ARP[:, c, :, :].rearrange("p a b -> p (a b)"),
                                       start=True, stop=True)
                    elif name[:2] == "nn":
                        for q in range(4):
                            c = int(name[2]) + q // 2
                            mm = pe.matmul(HB[:, bank, q * C:(q + 1) * C], ARP[:, c, q % 2, :],
                                           BT[:, c * C:(c + 1) * C], start=True, stop=True)
                    else:
                        src = {"tokb": BT, "tokk": KTL, "tokv": M3[:, 2]}[name]
                        for c in range(NC):
                            mm = pe.transpose(HB[:, bank, c * C:(c + 1) * C], src[:, c * C:(c + 1) * C], ident)
                    mm.then_inc(a_pe, PE_A.one(name))
                    fill(name)
                for l in LV:
                    nm = NM[(l - 1) % 2]
                    for h in range(2):
                        hn = "ab"[h]
                        bank = (3, 0)[h]
                        if h == 0:
                            pe.wait_ge(a_pool, POOL_A.at(i, f"nm{l}"))
                            if l == 1:
                                pe.wait_ge(a_dve, DVE_A.at(i, "xt0"))
                                pe.wait_ge(a_act, ACT_A.at(i, "nn23"))
                            else:
                                pe.wait_ge(a_act, ACT_A.at(i, f"tr{l - 1}"))
                        elif l == 1:
                            pe.wait_ge(a_act, ACT_A.at(i, "tokb"))
                        else:
                            pe.wait_ge(a_dve, DVE_A.at(i, f"tr{l - 1}"))
                        for q in range(4):
                            mm = pe.matmul(HB[:, bank, q * C:(q + 1) * C], nm[:, 4 * h + q, :],
                                           XT[:, 4 * h + q, :], start=True, stop=True)
                        mm.then_inc(a_pe, PE_A.one(f"qt{l}{hn}"))
                        fill(f"qt{l}{hn}")
                    for h in range(2):
                        hn = "ab"[h]
                        bank = (1, 2)[h]
                        if h == 0:
                            pe.wait_ge(a_act, ACT_A.at(i, f"qt{l}"))
                            if l == 1:
                                pe.wait_ge(a_act, ACT_A.at(i, "tokk"))
                            else:
                                pe.wait_ge(a_dve, DVE_A.at(i, f"xa{l - 1}"))
                        else:
                            pe.wait_ge(a_dve, DVE_A.at(i, f"qt{l}"))
                            if l == 1:
                                pe.wait_ge(a_act, ACT_A.at(i, "tokv"))
                            else:
                                pe.wait_ge(a_dve, DVE_A.at(i, f"xb{l - 1}"))
                        for q in range(4):
                            a, b = QT[:, 4 * h + q, :], X[:, 4 * h + q, :]
                            if l == last:
                                a, b = b, a
                            mm = pe.matmul(HB[:, bank, q * C:(q + 1) * C], a, b, start=True, stop=True)
                        mm.then_inc(a_pe, PE_A.one(f"dx{l}{hn}"))
                        fill(f"dx{l}{hn}")
                    for h in range(2) if l < last else ():
                        hn = "ab"[h]
                        bank = (3, 0)[h]
                        pe.wait_ge(a_dve, DVE_A.at(i, f"x{hn}{l}"))
                        for q in range(4):
                            mm = pe.transpose(HB[:, bank, q * C:(q + 1) * C], X[:, 4 * h + q, :], ident)
                        mm.then_inc(a_pe, PE_A.one(f"tr{l}{hn}"))
                        fill(f"tr{l}{hn}")
                for c in range(NC):
                    if c == 0:
                        pe.wait_ge(a_dve, DVE_A.at(i, f"xb{last}"))
                        pe.wait_ge(a_act, ACT_A.at(i, f"qt{last}"))
                    else:
                        pe.wait_ge(a_dve, DVE_A.at(i, f"s{c - 1}"))
                        pe.wait_ge(a_act, ACT_A.at(i, f"rhs{c - 1}"))
                    first = True
                    for kind in ("state", "chunk") if c else ("chunk",):
                        for h in range(2):
                            cols = slice(HD * h, HD * (h + 1))
                            lhs, rhs = ((ARP[:, c, h, :], S[:, c, cols]) if kind == "state" else
                                        (GK[:, c, h, :], TOKV[:, c, cols]))
                            mm = pe.matmul(HB[:, 3, cols], lhs, rhs, start=first, stop=(kind == "chunk"),
                                           skip_group_check=True)
                            first = False
                    mm.then_inc(a_pe, PE_A.one(f"rhs{c}"))
                    fill(f"rhs{c}")
                    pe.wait_ge(a_act, ACT_A.at(i, f"rhs{c}"))
                    if c:
                        pe.wait_ge(a_act, ACT_A.at(i, f"u{c - 1}"))
                    for h in range(2):
                        cols = slice(HD * h, HD * (h + 1))
                        mm = pe.matmul(HB[:, 0, cols], XT[:, 2 * c + h, :], RHS[:, c % 2, cols],
                                       start=(h == 0), stop=True, skip_group_check=True)
                    mm.then_inc(a_pe, PE_A.one(f"u{c}"))
                    fill(f"u{c}")
                    pe.wait_ge(a_act, ACT_A.at(i, f"u{c}"))
                    if c:
                        pe.matmul(HB[:, 2, 0:128], ident, S[:, c, :], start=True, stop=False)
                    pe.matmul(HB[:, 2, 0:128], TOKK[:, c, :], TOKV[:, c, :], start=(c == 0), stop=False)
                    pe.matmul(HB[:, 2, 0:128], TOKB[:, c, :], U[:, c, :], start=False, stop=True)\
                        .then_inc(a_pe, PE_A.one(f"s{c}"))
                    fill(f"s{c}")
                    for h in range(2):
                        cols = slice(HD * h, HD * (h + 1))
                        out = HB[cols, 1, c * C:(c + 1) * C]
                        first = c == 0
                        if c:
                            pe.matmul(out, S[:, c, cols], ARP[:, c, 2 + h, :], start=first, stop=False,
                                      skip_group_check=True)
                        pe.matmul(out, TOKV[:, c, cols], GK[:, c, 2 + h, :], start=first, stop=False,
                                  skip_group_check=True)
                        mm = pe.matmul(out, U[:, c, cols], GB[:, c, 2 + h, :], start=False, stop=True,
                                       skip_group_check=True)
                    mm.then_inc(a_pe, PE_A.one(f"y{c}"))
                    fill(f"y{c}")
                pe.wait_ge(a_dve, DVE_A.at(i, f"s{NC - 1}"))
                pe.transpose(HB[:, 3, 0:128], S[:, NC, :], ident).then_inc(a_pe, PE_A.one("st"))
                fill("st")
                pe.wait_ge(a_act, ACT_A.at(i, "y"))
                pe.matmul(HB[:, 0, :], blkmean, Y, start=True, stop=True).then_inc(a_pe, PE_A.one("mean"))
                fill("mean")
                pe.wait_ge(a_act, ACT_A.at(i, "ysq"))
                pe.matmul(HB[:, 2, :], blkmean, YSQ, start=True, stop=True).then_inc(a_pe, PE_A.one("var"))
                fill("var")

            with pe.Fori(0, PAIRS - 1) as i:
                pair_a(i, group_a(i + 1))
            pair_a(PAIRS - 1, group_b(0))

            def pair_b(i, g, fills=True):
                def fill(name):
                    if fills:
                        pe_fill(pe, span_b, g, name)

                pe.wait_ge(b_act, ACT_B.at(i, "sq"))
                pe.wait_ge(b_dve, DVE_B.start(i))
                for j in range(2):
                    for hf in range(2):
                        mm = pe.matmul(HB[:, 2 * j + hf, 0:HT], blkmean, SQ[:, j, hf * HT:(hf + 1) * HT],
                                       start=True, stop=True)
                mm.then_inc(b_pe, PE_B.one("ssum"))
                fill("ssum")
                pe.wait_ge(b_act, ACT_B.at(i, "ln"))
                pe.wait_ge(b_dve, DVE_B.at(i, "kn"))
                for t in range(QB):
                    mm = pe.transpose(HB[:, 0, 128 * t:128 * (t + 1)], KN[:, 128 * t:128 * (t + 1)], ident)
                mm.then_inc(b_pe, PE_B.one("tokk"))
                for t in range(QB):
                    mm = pe.transpose(HB[:, 1, 128 * t:128 * (t + 1)], ZB[:, 2, 128 * t:128 * (t + 1)], ident)
                mm.then_inc(b_pe, PE_B.one("tokv"))
                fill("tokv")
                pe.transpose(HB[0:NB, 2, 0:128], KN[:, T:TT], ident)
                pe.transpose(HB[0:NB, 2, 128:256], ZB[:, 2, T:TT], ident).then_inc(b_pe, PE_B.one("stok"))
                fill("stok")
                pe.wait_ge(b_dve, DVE_B.at(i, "qs"))
                pe.wait_ge(b_act, ACT_B.at(i, "tokv"))
                for b in range(NB):
                    mm = pe.matmul(HB[:, b // 4, 128 * (b % 4):128 * (b % 4 + 1)], QS[:, b:b + 1].to_broadcast([128, 128]),
                                   ident, start=True, stop=True)
                mm.then_inc(b_pe, PE_B.one("qb"))
                fill("qb")

                def score(j):
                    h, b = JS[j]
                    n = 128 * (b + 1)
                    if j < 2:
                        pe.wait_ge(b_dve, DVE_B.at(i, "pr2"))
                    else:
                        pe.wait_ge(b_dve, DVE_B.at(i, f"mx{j - 2}"))
                    pe.matmul(HB[:, j % 2, 0:n], QP[:, h, 128 * b:128 * (b + 1)], KN[:, 0:n], start=True, stop=True)\
                        .then_inc(b_pe, PE_B.one(f"s{j}"))
                    fill(f"s{j}")

                score(0)
                for j, (h, b) in enumerate(JS):
                    if j + 1 < nj:
                        score(j + 1)
                    pe.wait_ge(b_dve, DVE_B.at(i, f"dg{j}"))
                    pe.wait_ge(b_act, ACT_B.at(i, f"tp{j - 1}" if j else "stok"))
                    for t in range(b + 1):
                        mm = pe.matmul(HB[:, 2, 128 * t:128 * (t + 1)], PP[:, j % 2, 128 * t:128 * (t + 1)],
                                       DG[:, j % 2, :], start=True, stop=True)
                    mm.then_inc(b_pe, PE_B.one(f"t{j}"))
                    fill(f"t{j}")
                    pe.wait_ge(b_act, ACT_B.at(i, f"tp{j}"))
                    cols = slice(HD * h, HD * (h + 1))
                    for t in range(b + 1):
                        mm = pe.matmul(HB[cols, 3, 128 * b:128 * (b + 1)], VTOK[:, t, cols],
                                       PTR[:, j % 2, 128 * t:128 * (t + 1)], start=(b == 0 and t == 0),
                                       stop=(t == b), skip_group_check=True)
                    mm.then_inc(b_pe, PE_B.one(f"o{j}"))
                    fill(f"o{j}")
                pe.wait_ge(b_dve, DVE_B.at(i, f"dg{nj - 1}"))
                at = 0
                for t, n in enumerate(TS):
                    mm = pe.transpose(HB[0:16, 0, at:at + n], SCO[0:n, t, :], ident[0:n, 0:n])
                    at += n
                mm.then_inc(b_pe, PE_B.one("sct"))
                fill("sct")
                pe.wait_ge(b_dve, DVE_B.at(i, "spn"))
                pe.sem_inc(s_passed, 1)
                at = 0
                for t, n in enumerate(TS):
                    mm = pe.transpose(HB[0:n, 1, 16 * t:16 * (t + 1)], SPN[0:16, at:at + n], ident[0:16, 0:16])
                    at += n
                mm.then_inc(b_pe, PE_B.one("pwt"))
                fill("pwt")
                pe.wait_ge(b_act, ACT_B.at(i, "pwc"))
                pe.wait_ge(s_vc, (i + 1) * 48)
                pe.wait_ge(s_vrow, (i + 1) * 16)
                for b in range(NB):
                    for t, n in enumerate(TS):
                        mm = pe.matmul(HB[:, 2, 2 * b:2 * b + 2], VC[0:n, t, b, :], PW[0:n, t, 2 * b:2 * b + 2],
                                       start=(b == 0 and t == 0), stop=(t == 2), skip_group_check=True)
                mm.then_inc(b_pe, PE_B.one("av"))
                fill("av")

            with pe.Fori(0, PAIRS - 1) as i:
                pair_b(i, group_b(i + 1))
            pair_b(PAIRS - 1, 0, fills=False)

            pe.wait_ge(s_mt, 48)
            pe.wait_ge(b_dve, DVE_B.start(PAIRS))
            for k in range(DR // 128):
                mm = pe.transpose(HB[:, 0, NB * k:NB * (k + 1)], YB[0:NB, 128 * k:128 * (k + 1)], ident[0:NB, 0:NB])
            mm.then_inc(c_pe, 1)
            pe.wait_ge(c_pool, KT)

            def out_pair(m):
                for u in range(2 * KT):
                    multiply_unit(pe, m + GROUP_C, u)
                for t in range(2):
                    pe.wait_ge(s_evac, m * 2 + (2 * GROUP_C + t + 1))
                    pe.wait_ge(c_dve, m * 2)
                    for q in range(4):
                        pe.transpose(HB[:, 2 * t, 128 * q:128 * (q + 1)], YT[:, t, 128 * q:128 * (q + 1)], ident)
                    pe.transpose(HB[0:NB, 2 * t + 1, 0:128], YT[:, t, T:TT], ident).then_inc(c_pe, 1)

            with pe.Fori(0, D // 256) as m:
                out_pair(m)

        @block.scalar
        def _(act):
            act.wait_ge(p_dve, DVE_P.at(0, "zrow"))
            n = 0
            for v in (mu_shift[0:DR], mu_shift[DR:2 * DR], mu_shift[2 * DR:3 * DR], w0, a0, k_k, k_a,
                      r_k.rearrange("h d -> (h d)"), gn_w, gn_b, norm_w):
                m = v.shape[0] // 128
                act.dma_start(ROWT[n:n + m, :], v.rearrange("(i c) -> i c", c=128)).then_inc(s_rows, 16)
                n += m
            act.dma_start(ROWT[ROW_MU:ROW_MU + 2, 0:LORA], mu_shift[3 * DR:SHIFT].rearrange("(i c) -> i c", c=LORA))\
               .then_inc(s_rows, 16)
            for j, v in enumerate((q_norm, k_norm)):
                for h in range(2):
                    act.dma_start(ROWT[ROW_QK + j:ROW_QK + j + 1, HD * h:HD * (h + 1)],
                                  v.rearrange("(a c) -> a c", a=1)).then_inc(s_rows, 16)
            act.dma_start(SROW[0:NB, :], state_shift).then_inc(s_srow, 16)
            act.wait_ge(p_dve, DVE_P.at(0, "bias"))
            for t in range(5):
                m = 128 if t < 4 else NB
                act.wait_ge(s_xt[t], 16)
                if t:
                    act.wait_ge(p_act, ACT_P.at(0, f"sq{t - 1}"))
                act.activation(SQJ[0:m, :], XTOK[0:m, t, :], ACT.Square, accum_out=SSQ[0:m, t:t + 1])\
                   .then_inc(p_act, ACT_P.one(f"sq{t}"))
            act.wait_ge(p_act, ACT_P.at(0, "sq4"))
            act.activation(SSQ[:, 5:10], SSQ[:, 0:5], ACT.Ln, bias=eps_rms, scale=1.0 / D)\
               .then_inc(p_act, ACT_P.one("ln"))
            act.wait_ge(p_act, ACT_P.at(0, "ln"))
            act.activation(SSQ[:, 10:15], SSQ[:, 5:10], ACT.Exp, scale=-0.5).then_inc(p_act, ACT_P.one("rs"))
            round_half(act, 0, 0, LORA)
            round_half(act, 0, 1, LORA)
            for k in range(KT):
                act.wait_ge(p_pe, PE_P.at(0, f"x{k}"))
                act.wait_ge(p_dve, DVE_P.at(0, "rows"))
                if k >= 2:
                    act.wait_ge(p_dve, DVE_P.at(0, f"hi{k - 2}"))
                    act.wait_ge(p_pool, POOL_P.at(0, f"lo{k - 2}"))
                act.activation(XF[:, k % 2, :], HBF[:, 1024 * (k % 2):1024 * (k % 2) + TT], ACT.Copy,
                               scale=PT[:, ROW_NW + k:ROW_NW + k + 1]).then_inc(p_act, ACT_P.one(f"xf{k}"))
            round_half(act, 0, 2, LORA)
            round_half(act, 0, 3, LORA)
            act.wait_ge(p_dve, DVE_P.at(0, "lz"))
            evacuate(act, 0, 0, two(ZL[0:LORA, 0, 1:TT + 1]), LORA)
            round_half(act, group_a(0), 0)
            round_half(act, group_a(0), 1)
            evacuate(act, 0, 1, two(ZL[0:LORA, 1, 1:TT + 1]), LORA)
            for k in range(1, 8):
                round_half(act, group_a(0), k + 1)
                if k % 2:
                    if k == 1:
                        act.wait_ge(s_zero, 1)
                    evacuate(act, group_a(0), k // 2, two(Z[:, k // 2, 1:TT + 1]))
                if k == 3:
                    act.wait_ge(p_dve, DVE_P.at(0, "lmix"))
                    act.activation(TW[0:LORA, :], ML[0:LORA, 0, :], ACT.Tanh)
                    act.activation(AD[0:LORA, :], ML[0:LORA, 1, :], ACT.Copy).then_inc(p_act, ACT_P.one("tanh"))
                if k == 6:
                    act.wait_ge(p_pe, PE_P.at(0, "ltail"))
                    act.activation(LTAIL[0:NB + 1, :, :], HB[0:NB + 1, 0, 0:2 * LORA].rearrange("p (a b) -> p a b", a=2),
                                   ACT.Copy).then_inc(p_act, ACT_P.one("ltail"))
                    act.wait_ge(p_act, ACT_P.at(0, "ltail"))
                    act.dma_start(shift_p[0:1, 3 * DR:SHIFT], LTAIL[0:1, :, :].rearrange("p a b -> p (a b)"))\
                       .then_inc(o_ltail, 16)
                    act.dma_start(shift_s[:, 3 * DR:SHIFT], LTAIL[1:NB + 1, :, :].rearrange("p a b -> p (a b)"))\
                       .then_inc(o_ltail, 16)
            act.wait_ge(o_ltail, 32)

            def pair_a(i, g, z_next):
                def feed(name):
                    act_feed(act, span_a, g, name, z_next)

                act.wait_ge(a_pe, PE_A.at(i, "lora"))
                act.wait_ge(a_dve, DVE_A.at(i, "mix"))
                act.activation(two(SGW), HB[:, 0:2, 0:HT], ACT.Sigmoid, bias=P_["w0"]).then_inc(a_act, ACT_A.one("sgw"))
                act.activation(two(A_), HB[:, 2:4, 0:HT], ACT.Sigmoid, bias=P_["a0"]).then_inc(a_act, ACT_A.one("sga"))
                act.wait_ge(s_evac, group_a(i) * 2 + 4)
                act.activation(GG, Z[:, 3, 1:TT + 1], ACT.Sigmoid).then_inc(a_act, ACT_A.one("sgg"))
                act.activation(KSQ, M3[:, 1], ACT.Square, scale=P_["k_k"]).then_inc(a_act, ACT_A.one("ksq"))
                feed("lora")
                feed("kk")
                act.wait_ge(a_pe, PE_A.at(i, "tail"))
                act.wait_ge(o_tail, i * 32)
                act.activation(TAIL[0:NB + 1, :, :].rearrange("p a b -> p (a b)"), HB[0:NB + 1, 2, 0:384], ACT.Copy)\
                   .then_inc(a_act, ACT_A.one("tail"))
                act.wait_ge(a_act, ACT_A.at(i, "tail"))
                tails = lambda v: v[:, 0:3 * DR].rearrange("p (s i c) -> p i s c", s=3, i=PAIRS)[:, i, :, :]
                act.dma_start(tails(shift_p), TAIL[0:1, :, :]).then_inc(o_tail, 16)
                act.dma_start(tails(shift_s), TAIL[1:NB + 1, :, :]).then_inc(o_tail, 16)
                feed("tail")
                act.wait_ge(a_dve, DVE_A.at(i, "ssm"))
                act.activation(SSM, SSM, ACT.Ln, scale=float(2 ** LNS)).then_inc(a_act, ACT_A.one("ln"))
                act.wait_ge(a_act, ACT_A.at(i, "ln"))
                act.activation(RN, SSM, ACT.Exp, scale=-0.5, bias=ln_back).then_inc(a_act, ACT_A.one("rn"))
                act.wait_ge(a_dve, DVE_A.at(i, "gl"))
                act.activation(E1, LC, ACT.Exp, scale=-DEC).then_inc(a_act, ACT_A.one("e1"))
                act.activation(E2, LC, ACT.Exp, scale=DEC).then_inc(a_act, ACT_A.one("e2"))
                act.activation(G, GL, ACT.Exp, scale=-DEC).then_inc(a_act, ACT_A.one("g"))
                act.activation(DCS, SGW[:, T:TT], ACT.Exp, scale=-DEC).then_inc(a_act, ACT_A.one("dcs"))
                feed("bonus")
                act.wait_ge(a_pe, PE_A.at(i, "vec"))
                act.wait_ge(o_vec, i * 16)
                act.activation(VEC[0:NB, :, :].rearrange("p a b -> p (a b)"), HBF[0:NB, 0:1024], ACT.Copy)\
                   .then_inc(a_act, ACT_A.one("vec"))
                act.wait_ge(a_act, ACT_A.at(i, "vec"))
                act.dma_start(vec_d.rearrange("v b (i c) -> b i v c", i=PAIRS)[:, i, :, :], VEC[0:NB, :, :])\
                   .then_inc(o_vec, 16)
                feed("vec")
                for name, bank in (("nn01", 2), ("nn23", 3)):
                    act.wait_ge(a_pe, PE_A.at(i, name))
                    q = 2 * int(name[2])
                    act.activation(NN[:, q:q + 4, :].rearrange("p a b -> p (a b)"), HB[:, bank, :], ACT.Copy)\
                       .then_inc(a_act, ACT_A.one(name))
                for name in GRAMS:
                    feed(name)
                for name, bank, dst in (("tokb", 0, TOKB), ("tokk", 1, TOKK), ("tokv", 2, TOKV)):
                    act.wait_ge(a_pe, PE_A.at(i, name))
                    act.activation(dst.rearrange("p a b -> p (a b)"), HB[:, bank, :], ACT.Copy)\
                       .then_inc(a_act, ACT_A.one(name))
                for l in LV:
                    for s in ("qt", "tr") if l < last else ("qt",):
                        act.wait_ge(a_pe, PE_A.at(i, f"{s}{l}a"))
                        if s == "qt" and l == 1:
                            act.wait_ge(a_dve, DVE_A.at(i, "xt0"))
                        dst = (QT if s == "qt" else XT)[:, 0:4, :].rearrange("p a b -> p (a b)")
                        act.activation(dst, HB[:, 3, :], ACT.Copy).then_inc(a_act, ACT_A.one(f"{s}{l}"))
                        feed(f"{s}{l}a")
                        feed(f"{s}{l}b")
                        if s == "qt":
                            feed(f"dx{l}a")
                            feed(f"dx{l}b")
                for c in range(NC):
                    act.wait_ge(a_pe, PE_A.at(i, f"rhs{c}"))
                    act.activation(RHS[:, c % 2, :], HB[:, 3, 0:128], ACT.Copy).then_inc(a_act, ACT_A.one(f"rhs{c}"))
                    feed(f"rhs{c}")
                    act.wait_ge(a_pe, PE_A.at(i, f"u{c}"))
                    act.activation(U[:, c, :], HB[:, 0, 0:128], ACT.Copy, scale=-1.0).then_inc(a_act, ACT_A.one(f"u{c}"))
                    feed(f"u{c}")
                    feed(f"s{c}")
                    feed(f"y{c}")
                act.wait_ge(a_pe, PE_A.at(i, "st"))
                act.wait_ge(o_state, i * 32)
                act.activation(ST, HB[:, 3, 0:128], ACT.Copy).then_inc(a_act, ACT_A.one("st"))
                act.activation(Y, HB[:, 1, :], ACT.Copy).then_inc(a_act, ACT_A.one("y"))
                act.wait_ge(a_act, ACT_A.at(i, "st"))
                for h in range(2):
                    act.dma_start(wkv_p[0].rearrange("(i h) v k -> i h v k", h=2)[i, h],
                                  ST[HD * h:HD * (h + 1), HD * h:HD * (h + 1)]).then_inc(o_state, 16)
                feed("st")
                act.wait_ge(a_dve, DVE_A.at(i, "yc"))
                act.activation(YSQ, YC, ACT.Square).then_inc(a_act, ACT_A.one("ysq"))
                feed("mean")
                act.wait_ge(a_pe, PE_A.at(i, "var"))
                act.wait_ge(a_dve, DVE_A.at(i, "yc"))
                act.activation(Y, HB[:, 2, :], ACT.Ln, bias=eps_gn).then_inc(a_act, ACT_A.one("yln"))
                act.wait_ge(a_act, ACT_A.at(i, "yln"))
                act.activation(Y, Y, ACT.Exp, scale=-0.5).then_inc(a_act, ACT_A.one("yrs"))
                feed("var")
                act.wait_ge(a_dve, DVE_A.at(i, "ym"))
                act.dma_start(mix_d[0:DR, 0:T].rearrange("(i p) t -> i p t", p=128)[i], MIXO).then_inc(o_mix, 16)

            def next_a(i):
                def dst(s):
                    if s == 0:
                        act.wait_ge(a_dve, DVE_A.at(i, "gate"))
                        act.wait_ge(a_pe, PE_A.at(i, "tail"))
                    return two(Z[:, s, 1:TT + 1])
                return dst

            with act.Fori(0, PAIRS - 1) as i:
                pair_a(i, group_a(i + 1), next_a(i))
            pair_a(PAIRS - 1, group_b(0), next_a(PAIRS - 1))

            def pair_b(i, g, fills=True):
                def dst(s):
                    if s == 0:
                        act.wait_ge(b_dve, DVE_B.at(i, "gate"))
                        act.wait_ge(b_pe, PE_B.at(i, "stok"))
                    return two(ZB[:, s, :])

                def feed(name):
                    if fills:
                        act_feed(act, span_b, g, name, dst, ahead=True)

                act.wait_ge(b_dve, DVE_B.start(i))
                act.wait_ge(s_evac, group_b(i) * 2 + 4)
                for j in range(2):
                    sq = act.activation(SQ[:, j, :], ZB[:, j, :], ACT.Square)
                sq.then_inc(b_act, ACT_B.one("sq"))
                act.activation(GGB, ZB[:, 3, :], ACT.Sigmoid).then_inc(b_act, ACT_B.one("sgg"))
                act.wait_ge(b_pe, PE_B.at(i, "ssum"))
                for j in range(2):
                    ln = act.activation(two(LN[:, j, :]), HB[:, 2 * j:2 * j + 2, 0:HT], ACT.Ln, bias=eps_rms)
                ln.then_inc(b_act, ACT_B.one("ln"))
                act.wait_ge(b_act, ACT_B.at(i, "ln"))
                for j in range(2):
                    rn = act.activation(RNB[:, j, :], LN[:, j, :], ACT.Exp, scale=-0.5)
                rn.then_inc(b_act, ACT_B.one("rn"))
                feed("ssum")
                for name, bank, dstk, view, o in (("tokk", 0, KTOK, kp_view, o_k), ("tokv", 1, VTOK, vp_view, o_v)):
                    act.wait_ge(b_pe, PE_B.at(i, name))
                    act.wait_ge(o, i * 16)
                    act.activation(dstk.rearrange("p a b -> p (a b)"), HB[:, bank, :], ACT.Copy)\
                       .then_inc(b_act, ACT_B.one(name))
                    act.wait_ge(b_act, ACT_B.at(i, name))
                    act.dma_start(view.rearrange("p t (i c) -> p t i c", i=PAIRS)[:, :, i, :], dstk).then_inc(o, 16)
                feed("tokv")
                act.wait_ge(b_pe, PE_B.at(i, "stok"))
                act.wait_ge(o_skv, i * 32)
                act.wait_ge(s_krow, i * 16)
                act.wait_ge(s_vrow, i * 16)
                act.activation(SKV[0:NB, :, :].rearrange("p a b -> p (a b)"), HB[0:NB, 2, 0:256], ACT.Copy)\
                   .then_inc(b_act, ACT_B.one("stok"))
                act.wait_ge(b_act, ACT_B.at(i, "stok"))
                act.dma_start(ks_view.rearrange("b (i c) -> b i c", i=PAIRS)[:, i, :], SKV[0:NB, 0, :]).then_inc(o_skv, 16)
                act.dma_start(vs_view.rearrange("b (i c) -> b i c", i=PAIRS)[:, i, :], SKV[0:NB, 1, :]).then_inc(o_skv, 16)
                if not isinstance(i, int) or i > 0:
                    act.wait_ge(b_dve, DVE_B.start(i))
                    act.wait_ge(b_pe, PE_B.start(i))
                act.dma_start(KC[96:97, 1, :, :], SKV[0:NB, 0, :]).then_inc(s_krow, 16)
                act.dma_start(VC[96:97, 1, :, :], SKV[0:NB, 1, :]).then_inc(s_vrow, 16)
                feed("stok")
                feed("qb")
                feed("s0")
                for j, (h, b) in enumerate(JS):
                    n = 128 * (b + 1)
                    if j + 1 < nj:
                        feed(f"s{j + 1}")
                    act.wait_ge(b_dve, DVE_B.at(i, f"mx{j}"))
                    act.activation(EE[:, j % 2, 0:n], SC2[:, j % 2, 0:n], ACT.Exp, scale=-1.0, bias=MX[:, j:j + 1])\
                       .then_inc(b_act, ACT_B.one(f"ex{j}"))
                    act.wait_ge(b_pe, PE_B.at(i, f"t{j}"))
                    act.activation(PTR[:, j % 2, 0:n], HB[:, 2, 0:n], ACT.Copy).then_inc(b_act, ACT_B.one(f"tp{j}"))
                    feed(f"t{j}")
                act.wait_ge(b_dve, DVE_B.at(i, "smx"))
                act.activation(SE[0:16, :], SS_[0:16, :], ACT.Exp, scale=-1.0, bias=SMX[0:16, 0:1])\
                   .then_inc(b_act, ACT_B.one("sex"))
                feed("sct")
                act.wait_ge(b_pe, PE_B.at(i, "pwt"))
                for t, n in enumerate(TS):
                    pw = act.activation(PW[0:n, t, :], HB[0:n, 1, 16 * t:16 * (t + 1)], ACT.Copy)
                pw.then_inc(b_act, ACT_B.one("pwc"))
                feed("pwt")
                feed("av")
                act.wait_ge(b_dve, DVE_B.at(i, "mixs"))
                act.dma_start(mix_d[DR:D, :].rearrange("(i p) t -> i p t", p=128)[i], MIXB).then_inc(o_mix, 16)

            act.wait_ge(r_dve, DVE_R.at(0, "vs"))
            act.activation(SM[:, 2:3], SM[:, 1:2], ACT.Ln, bias=eps_gn, scale=1.0 / HD).then_inc(r_act, 1)
            act.wait_ge(r_act, 1)
            act.activation(SM[:, 3:4], SM[:, 2:3], ACT.Exp, scale=-0.5).then_inc(r_act, 1)
            act.wait_ge(r_dve, DVE_R.at(0, "yo"))
            act.dma_start(ys_d.rearrange("b (h d) -> (b h) d", d=HD), YQ).then_inc(o_ys, 16)
            act.dma_start(wkv_s.rearrange("b h v k -> (b h) v k"), S1).then_inc(o_sst, 16)
            act.wait_ge(o_ys, 16)
            act.wait_ge(o_sst, 16)

            with act.Fori(0, PAIRS - 1) as i:
                pair_b(i, group_b(i + 1))
            pair_b(PAIRS - 1, 0, fills=False)

            for s, n in ((o_mix, 2 * PAIRS), (o_k, PAIRS), (o_v, PAIRS), (o_skv, 2 * PAIRS)):
                act.wait_ge(s, 16 * n)
            act.wait_ge(b_pe, PE_B.start(PAIRS))
            act.wait_ge(b_dve, DVE_B.start(PAIRS))
            mt = mix_d.rearrange("(t p) c -> p t c", p=128)
            act.dma_start(MT[:, 0:8, 0:T], mt[:, 0:8, 0:T]).then_inc(s_mt, 16)
            act.dma_start(MT[:, 8:16, :], mt[:, 8:16, :]).then_inc(s_mt, 16)
            act.dma_start(YB[0:NB, :], ys_d).then_inc(s_mt, 16)
            act.wait_ge(s_mt, 48)
            act.wait_ge(c_pe, 1)
            act.activation(MT[:, 0:8, T:TT], HB[:, 0, 0:8 * NB].rearrange("p (k b) -> p k b", b=NB), ACT.Copy)\
               .then_inc(c_act, ACT_CP.one("yb"))
            act.wait_ge(c_act, ACT_CP.at(0, "yb"))
            for k in range(KT):
                act.activation(XH[:, k, :], MT[:, k, :], ACT.Copy).then_inc(c_act, ACT_CP.one(f"hi{k}"))

            def out_pair(m, more=True):
                def tile_to(t):
                    act.wait_ge(c_pe, m * 2 + t)
                    return two(YT[:, t, :])

                round_half(act, m + GROUP_C, 1)
                round_half(act, m + GROUP_C, 2)
                evacuate(act, m + GROUP_C, 0, tile_to(0))
                round_half(act, m + GROUP_C, 3)
                if more:
                    round_half(act, m + GROUP_C, 4)
                evacuate(act, m + GROUP_C, 1, tile_to(1))

            def store(m):
                yv = yp.rearrange("p t (m u c) -> p t m u c", u=2, c=128)
                ysv = ys.rearrange("b (m u c) -> b m u c", u=2, c=128)
                for t in range(2):
                    act.wait_ge(c_dve, m * 2 + (t + 1))
                    act.dma_start(yv[:, :, m, t, :], YO[:, t, :, :]).then_inc(o_y[t], 16)
                    act.dma_start(ysv[:, m, t, :], YOS[0:NB, t, :]).then_inc(o_y[t], 16)

            out_pair(0)
            with act.Fori(1, D // 256 - 1) as m:
                out_pair(m)
                store(m - 1)
            out_pair(D // 256 - 1, more=False)
            store(D // 256 - 2)
            store(D // 256 - 1)
            for t in range(2):
                act.wait_ge(o_y[t], 32 * (D // 256))

        @block.vector
        def _(dve):
            dve.memset(ROWT, 0.0).then_inc(p_dve, DVE_P.one("zrow"))
            dve.memset(SSQ, 1.0)
            dve.memset(BIAS[:, 0:1], RMS_EPS)
            dve.memset(BIAS[:, 1:2], GN_EPS)
            dve.memset(BIAS[:, 2:3], 0.5 * LNS * float(np.log(2.0))).then_inc(p_dve, DVE_P.one("bias"))
            dve.wait_ge(p_pe, PE_P.at(0, "rows"))
            dve.tensor_copy(PT[:, :], HB[:, 0, 0:ROWS]).then_inc(p_dve, DVE_P.one("rows"))
            dve.wait_ge(p_pe, PE_P.at(0, "shift"))
            dve.tensor_copy(SST[:, 0:24, :], HB[:, 1, 0:24 * NB].rearrange("p (s b) -> p s b", b=NB))
            dve.tensor_copy(SST[0:LORA, 24:26, :], HB[0:LORA, 1, 24 * NB:26 * NB].rearrange("p (s b) -> p s b", b=NB))\
               .then_inc(p_dve, DVE_P.one("shift"))
            dve.wait_ge(p_act, ACT_P.at(0, "rs"))
            for t in range(5):
                m = 128 if t < 4 else NB
                dve.tensor_scalar(XTOK[0:m, t, :], XTOK[0:m, t, :], SSQ[0:m, 10 + t:11 + t], None, ALU.mult)\
                   .then_inc(p_dve, DVE_P.one(f"xn{t}"))
            for k in range(KT):
                dve.wait_ge(p_act, ACT_P.at(0, f"xf{k}"))
                dve.tensor_copy(XH[:, k, :], XF[:, k % 2, :]).then_inc(p_dve, DVE_P.one(f"hi{k}"))
            dve.wait_ge(p_pe, PE_P.at(0, f"x{KT - 1}"))
            dve.memset(Z[:, :, 0:1], 0.0)
            dve.memset(ARP, 0.0).then_inc(s_zero, 1)
            dve.memset(ZL[0:LORA, :, 0:1], 0.0).then_inc(p_dve, DVE_P.one("lz"))
            dve.wait_ge(s_evac, 2)
            dve.wait_ge(p_dve, DVE_P.at(0, "lz"))
            dve.tensor_tensor(DL[0:LORA, :, 0:T], ZL[0:LORA, :, 0:T], ZL[0:LORA, :, 1:T + 1], ALU.subtract)\
               .then_inc(p_dve, DVE_P.one("ldiff"))
            dve.wait_ge(p_dve, DVE_P.at(0, "shift"))
            dve.tensor_tensor(DL[0:LORA, :, T:TT], SST[0:LORA, 24:26, :], ZL[0:LORA, :, T + 1:TT + 1], ALU.subtract)\
               .then_inc(p_dve, DVE_P.one("lds"))
            dve.wait_ge(p_dve, DVE_P.at(0, "lds"))
            for j in range(2):
                mix = dve.scalar_tensor_tensor(out=ML[0:LORA, j, :], in0=DL[0:LORA, j, :],
                                               scalar=PT[0:LORA, ROW_MU + j:ROW_MU + j + 1],
                                               in1=ZL[0:LORA, j, 1:TT + 1], op0=ALU.mult, op1=ALU.add)
            mix.then_inc(p_dve, DVE_P.one("lmix"))
            dve.wait_ge(p_act, ACT_P.n)
            dve.wait_ge(o_ltail, 32)
            dve.wait_ge(s_zero, 1)

            def pair_a(i, g):
                def after(name):
                    dve.wait_ge(a_dve, DVE_A.at(i, name))

                def done(ins, name):
                    ins.then_inc(a_dve, DVE_A.one(name))

                dve.wait_ge(a_act, ACT_A.start(i))
                dve.wait_ge(a_dve, DVE_A.start(i))
                dve.tensor_copy(PAR, par_view[:, i, :])
                dve.tensor_copy(SSP, ssp_view[:, i, :, :]).then_inc(a_dve, DVE_A.one("par"))
                dve.wait_ge(s_evac, g * 2 + 3)
                dve.tensor_tensor(D3[:, :, 0:T], Z[:, 0:3, 0:T], Z[:, 0:3, 1:T + 1], ALU.subtract)\
                   .then_inc(a_dve, DVE_A.one("dsh"))
                after("par")
                dve.tensor_tensor(D3[:, :, T:TT], SSP, Z[:, 0:3, T + 1:TT + 1], ALU.subtract)\
                   .then_inc(a_dve, DVE_A.one("dss"))
                after("dss")
                for s, mu in enumerate(("mu_r", "mu_k", "mu_v")):
                    mix = dve.scalar_tensor_tensor(out=M3[:, s], in0=D3[:, s], scalar=P_[mu],
                                                   in1=Z[:, s, 1:TT + 1], op0=ALU.mult, op1=ALU.add)
                mix.then_inc(a_dve, DVE_A.one("mix"))
                dve.wait_ge(a_act, ACT_A.at(i, "sga"))
                after("mix")
                dve.tensor_scalar(T1, A_, 1.0, P_["k_a"], ALU.subtract, ALU.mult).then_inc(a_dve, DVE_A.one("t1"))
                after("t1")
                dve.scalar_tensor_tensor(out=KP, in0=T1, scalar=1.0, in1=M3[:, 1], op0=ALU.add, op1=ALU.mult)\
                   .then_inc(a_dve, DVE_A.one("kp"))
                after("kp")
                dve.scalar_tensor_tensor(out=T1, in0=M3[:, 0], scalar=P_["r_k"], in1=KP, op0=ALU.mult, op1=ALU.mult)\
                   .then_inc(a_dve, DVE_A.one("prod"))
                dve.tensor_tensor_scan(LS, ca["carry"], SGW[:, 0:T], 0.0, ALU.mult, ALU.add)\
                   .then_inc(a_dve, DVE_A.one("scan"))
                after("scan")
                lsc = LS.rearrange("p (c t) -> p c t", c=NC)
                dve.tensor_tensor(LC[:, :, 1:C + 1], lsc, lsc[:, :, MID:MID + 1].to_broadcast([128, NC, C]), ALU.subtract)\
                   .then_inc(a_dve, DVE_A.one("lcm"))
                dve.tensor_scalar(LC[:, :, 0:1], lsc[:, :, MID:MID + 1], -1.0, None, ALU.mult)\
                   .then_inc(a_dve, DVE_A.one("lc0"))
                after("lc0")
                dve.tensor_copy(GL[:, NC - 1:NC], LC[:, NC - 1, C:C + 1]).then_inc(a_dve, DVE_A.one("gl0"))
                dve.tensor_tensor(GL[:, 0:NC - 1], LC[:, 0:NC - 1, C], LC[:, 1:NC, 0], ALU.subtract)\
                   .then_inc(a_dve, DVE_A.one("gl"))
                dve.wait_ge(a_pe, PE_A.at(i, "kk"))
                dve.tensor_scalar(two(SSM), HB[:, 0:2, 0:HT], L2_EPS * L2_EPS, None, ALU.max)\
                   .then_inc(a_dve, DVE_A.one("ssm"))
                dve.wait_ge(a_act, ACT_A.at(i, "sgg"))
                dve.tensor_tensor(GG, GG, Z[:, 3, 1:TT + 1], ALU.mult).then_inc(a_dve, DVE_A.one("gate"))
                dve.wait_ge(o_mix, i * 16)
                dve.wait_ge(a_act, ACT_A.at(i, "e2"))
                chunks = lambda a: a[:, 0:T].rearrange("p (c t) -> p c t", c=NC)
                dve.tensor_tensor(chunks(KTL), chunks(KP), E2[:, :, 1:C + 1], ALU.mult).then_inc(a_dve, DVE_A.one("kt"))
                for h in range(2):
                    rows = slice(HD * h, HD * (h + 1))
                    rt = dve.tensor_tensor(ARP[rows, :, 2 + h, :], chunks(M3[:, 0])[rows], E1[rows, :, 1:C + 1], ALU.mult)
                rt.then_inc(a_dve, DVE_A.one("rt"))
                dve.wait_ge(a_pe, PE_A.at(i, "bonus"))
                dve.tensor_tensor(two(BON), HB[:, 2:4, 0:HT], two(M3[:, 2]), ALU.mult).then_inc(a_dve, DVE_A.one("bon"))
                dve.wait_ge(a_act, ACT_A.at(i, "rn"))
                dve.scalar_tensor_tensor(out=KK, in0=M3[:, 1], scalar=P_["k_k"], in1=RN, op0=ALU.mult, op1=ALU.mult)\
                   .then_inc(a_dve, DVE_A.one("kk"))
                after("kk")
                for h in range(2):
                    rows = slice(HD * h, HD * (h + 1))
                    at = dve.tensor_tensor(ARP[rows, :, h, :], chunks(KK)[rows], E1[rows, :, 0:C], ALU.mult)
                at.then_inc(a_dve, DVE_A.one("at"))
                dve.tensor_tensor(KKA, KK, A_, ALU.mult).then_inc(a_dve, DVE_A.one("kka"))
                after("kka")
                dve.tensor_tensor(chunks(BT), chunks(KKA), E2[:, :, 1:C + 1], ALU.mult).then_inc(a_dve, DVE_A.one("bt"))
                for name, bank in (("gb0", 2), ("gk0", 3), ("gb1", 0), ("gk1", 1), ("gb2", 3), ("gk2", 0),
                                   ("gb3", 1), ("gk3", 2)):
                    dve.wait_ge(a_pe, PE_A.at(i, name))
                    dst = (GB if name[1] == "b" else GK)[:, int(name[2]), :, :].rearrange("p a b -> p (a b)")
                    dve.tensor_tensor(dst, HB[:, bank, :], ca["causal"], ALU.mult).then_inc(a_dve, DVE_A.one(name))
                dve.wait_ge(a_pool, POOL_A.at(i, "nm0"))
                dve.tensor_tensor(X, bc(ident, 8), NM[0], ALU.subtract).then_inc(a_dve, DVE_A.one("x0"))
                dve.wait_ge(a_pool, POOL_A.at(i, "nt0"))
                dve.tensor_tensor(XT, bc(ident, 8), NM[1], ALU.subtract).then_inc(a_dve, DVE_A.one("xt0"))
                flat = lambda a: a.rearrange("p a b -> p (a b)")
                for l in LV:
                    dve.wait_ge(a_pe, PE_A.at(i, f"qt{l}b"))
                    dve.tensor_copy(flat(QT[:, 4:8, :]), HB[:, 0, :]).then_inc(a_dve, DVE_A.one(f"qt{l}"))
                    tgt = XT if l == last else X
                    for h in range(2):
                        dve.wait_ge(a_pe, PE_A.at(i, f"dx{l}{'ab'[h]}"))
                        part = flat(tgt[:, 4 * h:4 * h + 4, :])
                        dve.tensor_tensor(part, part, HB[:, 1 + h, :], ALU.subtract)\
                           .then_inc(a_dve, DVE_A.one(f"x{'ab'[h]}{l}"))
                    if l < last:
                        dve.wait_ge(a_pe, PE_A.at(i, f"tr{l}b"))
                        dve.tensor_copy(flat(XT[:, 4:8, :]), HB[:, 0, :]).then_inc(a_dve, DVE_A.one(f"tr{l}"))
                for c in range(NC):
                    dve.wait_ge(a_pe, PE_A.at(i, f"s{c}"))
                    dve.tensor_scalar(S[:, c + 1, :], HB[:, 2, 0:128], G[:, c:c + 1], None, ALU.mult)\
                       .then_inc(a_dve, DVE_A.one(f"s{c}"))
                dve.wait_ge(a_pe, PE_A.at(i, "mean"))
                dve.tensor_tensor(YC, Y, HB[:, 0, :], ALU.subtract).then_inc(a_dve, DVE_A.one("yc"))
                dve.wait_ge(a_act, ACT_A.at(i, "yrs"))
                dve.scalar_tensor_tensor(out=YC, in0=YC, scalar=P_["gn_w"], in1=Y, op0=ALU.mult, op1=ALU.mult)\
                   .then_inc(a_dve, DVE_A.one("yn"))
                after("yn")
                dve.scalar_tensor_tensor(out=YC, in0=YC, scalar=P_["gn_b"], in1=BON[:, 0:T], op0=ALU.add, op1=ALU.add)\
                   .then_inc(a_dve, DVE_A.one("yb"))
                after("yb")
                dve.tensor_tensor(MIXO, YC, GG[:, 0:T], ALU.mult).then_inc(a_dve, DVE_A.one("ym"))

            with dve.Fori(0, PAIRS) as i:
                pair_a(i, group_a(i))

            vec = vec_d.rearrange("v b (h d) -> (b h) v d", d=HD)
            dve.wait_ge(s_sv, 16 * 17)
            dve.wait_ge(s_sst, 16)
            r, w, kq, v, kk, kka, gate, bon = (SV[:, j, :] for j in range(8))
            row = lambda a: a.unsqueeze(1).to_broadcast([128, HD, HD])
            col = lambda a: a.unsqueeze(2).to_broadcast([128, HD, HD])

            def rd(name):
                dve.wait_ge(r_dve, DVE_R.at(0, name))

            dve.tensor_tensor(PX, S0, row(kk), ALU.mult).then_inc(r_dve, DVE_R.one("p1"))
            rd("p1")
            dve.tensor_reduce(SA, PX, mybir.AxisListType.X, ALU.add).then_inc(r_dve, DVE_R.one("sa"))
            dve.tensor_tensor(S1, S0, row(w), ALU.mult).then_inc(r_dve, DVE_R.one("sw"))
            rd("sw")
            dve.tensor_tensor(PX, col(SA), row(kka), ALU.mult).then_inc(r_dve, DVE_R.one("p2"))
            rd("p2")
            dve.tensor_tensor(S1, S1, PX, ALU.subtract).then_inc(r_dve, DVE_R.one("sb"))
            rd("sb")
            dve.tensor_tensor(PX, col(v), row(kq), ALU.mult).then_inc(r_dve, DVE_R.one("p3"))
            rd("p3")
            dve.tensor_tensor(S1, S1, PX, ALU.add).then_inc(r_dve, DVE_R.one("sc"))
            rd("sc")
            dve.tensor_tensor(PX, S1, row(r), ALU.mult).then_inc(r_dve, DVE_R.one("p4"))
            rd("p4")
            dve.tensor_reduce(YR, PX, mybir.AxisListType.X, ALU.add).then_inc(r_dve, DVE_R.one("y"))
            rd("y")
            dve.tensor_reduce(SM[:, 0:1], YR, mybir.AxisListType.X, ALU.add).then_inc(r_dve, DVE_R.one("m"))
            rd("m")
            dve.tensor_scalar(SM[:, 0:1], SM[:, 0:1], 1.0 / HD, None, ALU.mult).then_inc(r_dve, DVE_R.one("ms"))
            rd("ms")
            dve.tensor_scalar(YD, YR, SM[:, 0:1], None, ALU.subtract).then_inc(r_dve, DVE_R.one("yd"))
            rd("yd")
            dve.tensor_tensor(YQ, YD, YD, ALU.mult).then_inc(r_dve, DVE_R.one("v"))
            rd("v")
            dve.tensor_reduce(SM[:, 1:2], YQ, mybir.AxisListType.X, ALU.add).then_inc(r_dve, DVE_R.one("vs"))
            dve.wait_ge(r_act, 2)
            dve.tensor_scalar(YQ, YD, SM[:, 3:4], None, ALU.mult).then_inc(r_dve, DVE_R.one("rz"))
            rd("rz")
            dve.tensor_tensor(YQ, YQ, SG[:, 0, :], ALU.mult).then_inc(r_dve, DVE_R.one("rs"))
            rd("rs")
            dve.tensor_tensor(YQ, YQ, SG[:, 1, :], ALU.add).then_inc(r_dve, DVE_R.one("yg"))
            rd("yg")
            dve.tensor_tensor(YQ, YQ, bon, ALU.add).then_inc(r_dve, DVE_R.one("yb"))
            rd("yb")
            dve.tensor_tensor(YQ, YQ, gate, ALU.mult).then_inc(r_dve, DVE_R.one("yo"))

            dve.wait_ge(o_ys, 16)
            dve.wait_ge(o_sst, 16)
            dve.wait_ge(a_pe, PE_A.start(PAIRS))
            dve.memset(QP, 0.0)
            dve.tensor_scalar(QW[:, 0:1], PT[:, ROW_QK:ROW_QK + 1], HD ** -0.5, None, ALU.mult)
            dve.tensor_copy(QW[:, 1:2], PT[:, ROW_QK + 1:ROW_QK + 2]).then_inc(s_zero, 1)
            dve.wait_ge(s_zero, 2)
            dve.wait_ge(s_cb, 16)

            def pair_b(i):
                def after(name):
                    dve.wait_ge(b_dve, DVE_B.at(i, name))

                dve.wait_ge(b_pe, PE_B.start(i))
                dve.wait_ge(b_act, ACT_B.start(i))
                dve.wait_ge(b_pool, POOL_B.start(i))
                dve.wait_ge(b_dve, DVE_B.start(i))
                dve.tensor_copy(SL, cb["slope"].rearrange("p (i h) -> p i h", h=2)[:, i, :])
                dve.tensor_copy(SSL[0:16, :], cb["sslope"].rearrange("p (i o) -> p i o", o=1)[0:16, i, :])\
                   .then_inc(b_dve, DVE_B.one("sl"))
                dve.wait_ge(b_act, ACT_B.at(i, "rn"))
                for h in range(2):
                    rows = slice(HD * h, HD * (h + 1))
                    qn = dve.scalar_tensor_tensor(out=QP[rows, h, :], in0=ZB[rows, 0, :], scalar=QW[rows, 0:1],
                                                  in1=RNB[rows, 0, :], op0=ALU.mult, op1=ALU.mult)
                qn.then_inc(b_dve, DVE_B.one("qn"))
                dve.scalar_tensor_tensor(out=KN, in0=ZB[:, 1, :], scalar=QW[:, 1:2], in1=RNB[:, 1, :],
                                         op0=ALU.mult, op1=ALU.mult).then_inc(b_dve, DVE_B.one("kn"))
                after("qn")
                for h in range(2):
                    rows = slice(HD * h, HD * (h + 1))
                    qs = dve.tensor_copy(QS[rows, :], QP[rows, h, T:TT])
                qs.then_inc(b_dve, DVE_B.one("qs"))
                dve.tensor_tensor(GGB, GGB, ZB[:, 3, :], ALU.mult).then_inc(b_dve, DVE_B.one("gate"))
                dve.wait_ge(b_pe, PE_B.at(i, "qb"))
                dve.wait_ge(s_kc, (i + 1) * 48)
                dve.wait_ge(s_krow, (i + 1) * 16)
                for t, n in enumerate(TS):
                    if t:
                        after(f"rd{t - 1}")
                    dve.tensor_tensor(PR[0:n, :, :].rearrange("p b c -> p (b c)"),
                                      KC[0:n, t, :, :].rearrange("p b c -> p (b c)"), HBF[0:n, 0:NB * 128], ALU.mult)\
                       .then_inc(b_dve, DVE_B.one(f"pr{t}"))
                    after(f"pr{t}")
                    dve.tensor_reduce(SCO[0:n, t, :], PR[0:n, :, :].rearrange("p b (h d) -> p (b h) d", h=2),
                                      mybir.AxisListType.X, ALU.add).then_inc(b_dve, DVE_B.one(f"rd{t}"))

                def largest(j):
                    h, b = JS[j]
                    n = 128 * (b + 1)
                    dve.wait_ge(b_pe, PE_B.at(i, f"s{j}"))
                    if j == 0:
                        dve.wait_ge(b_pool, POOL_B.at(i, "bt"))
                    if j >= 2:
                        dve.wait_ge(b_act, ACT_B.at(i, f"ex{j - 2}"))
                    dve.sem_inc(s_passed, 1)
                    dve.tensor_tensor_reduce(out=SC2[:, j % 2, 0:n], in0=HB[:, j % 2, 0:n],
                                             in1=BTB[:, h, T - n:T], scale=-1.0, scalar=3e38,
                                             op0=ALU.add, op1=ALU.min, accum_out=MX[:, j:j + 1])\
                       .then_inc(b_dve, DVE_B.one(f"mx{j}"))

                largest(0)
                for j, (h, b) in enumerate(JS):
                    n = 128 * (b + 1)
                    if j + 1 < nj:
                        largest(j + 1)
                    dve.wait_ge(b_act, ACT_B.at(i, f"ex{j}"))
                    if j >= 2:
                        dve.wait_ge(b_pe, PE_B.at(i, f"t{j - 2}"))
                    dve.tensor_tensor_reduce(out=PP[:, j % 2, 0:n], in0=EE[:, j % 2, 0:n], in1=cb["mult"][:, T - n:T],
                                             scale=1.0, scalar=0.0, op0=ALU.mult, op1=ALU.add,
                                             accum_out=ZS[:, j:j + 1]).then_inc(b_dve, DVE_B.one(f"pm{j}"))
                    after(f"pm{j}")
                    dve.reciprocal(RZ[:, j:j + 1], ZS[:, j:j + 1]).then_inc(b_dve, DVE_B.one(f"rz{j}"))
                    after(f"rz{j}")
                    dve.tensor_scalar(DG[:, j % 2, :], ident, RZ[:, j:j + 1], None, ALU.mult)\
                       .then_inc(b_dve, DVE_B.one(f"dg{j}"))
                dve.wait_ge(b_pe, PE_B.at(i, "sct"))
                dve.wait_ge(b_pool, POOL_B.at(i, "bts"))
                dve.sem_inc(s_passed, 1)
                dve.tensor_tensor_reduce(out=SS_[0:16, :], in0=HB[0:16, 0, 0:NS], in1=BTS[0:16, :], scale=-1.0,
                                         scalar=3e38, op0=ALU.add, op1=ALU.min, accum_out=SMX[0:16, 0:1])\
                   .then_inc(b_dve, DVE_B.one("smx"))
                dve.wait_ge(b_act, ACT_B.at(i, "sex"))
                dve.tensor_tensor_reduce(out=SP_[0:16, :], in0=SE[0:16, :], in1=cb["smult"][0:16, :], scale=1.0,
                                         scalar=0.0, op0=ALU.mult, op1=ALU.add, accum_out=SMX[0:16, 1:2])\
                   .then_inc(b_dve, DVE_B.one("spm"))
                after("spm")
                dve.reciprocal(SMX[0:16, 2:3], SMX[0:16, 1:2]).then_inc(b_dve, DVE_B.one("srz"))
                after("srz")
                dve.tensor_scalar(SPN[0:16, :], SP_[0:16, :], SMX[0:16, 2:3], None, ALU.mult)\
                   .then_inc(b_dve, DVE_B.one("spn"))
                dve.wait_ge(b_pe, PE_B.at(i, f"o{nj - 1}"))
                dve.wait_ge(o_mix, (i + PAIRS) * 16)
                dve.tensor_tensor(MIXB[:, 0:T], HB[:, 3, :], GGB[:, 0:T], ALU.mult).then_inc(b_dve, DVE_B.one("mixp"))
                dve.wait_ge(b_pe, PE_B.at(i, "av"))
                for h in range(2):
                    rows = slice(HD * h, HD * (h + 1))
                    ms = dve.tensor_tensor(MIXB[rows, T:TT], HB[rows, 2, 0:2 * NB].rearrange("p (b h) -> p b h", h=2)[:, :, h],
                                           GGB[rows, T:TT], ALU.mult)
                ms.then_inc(b_dve, DVE_B.one("mixs"))

            with dve.Fori(0, PAIRS) as i:
                pair_b(i)

            with dve.Fori(0, D // 256) as m:
                for t in range(2):
                    dve.wait_ge(c_pe, m * 2 + (t + 2))
                    dve.wait_ge(s_xr[t], (m + 1) * 32)
                    dve.wait_ge(o_y[t], m * 32)
                    dve.tensor_tensor(YO[:, t, :, :].rearrange("p a b -> p (a b)"), HB[:, 2 * t, :],
                                      XR[:, t, :, :].rearrange("p a b -> p (a b)"), ALU.add)
                    dve.tensor_tensor(YOS[0:NB, t, :], HB[0:NB, 2 * t + 1, 0:128], XRS[0:NB, t, :], ALU.add)\
                       .then_inc(c_dve, 1)


_INS = ["x_prompt", "x_sample", "state_wkv", "state_shift", "cache_k_win", "cache_v_win", "norm_w", "w_in",
        "mu_shift", "w0", "w_up", "a0", "a_up", "k_k", "k_a", "r_k", "gn_w", "gn_b", "q_norm", "k_norm", "w_out"]
_OUTS = [(1, T, D), (NB, 1, D), (1, NH, HD, HD), (1, SHIFT), (1, T, NH, HD), (1, T, NH, HD),
         (NB, NH, HD, HD), (NB, SHIFT), (NB, 1, NH, HD), (NB, 1, NH, HD)]


def kernel(**inputs):
    import concourse.bacc as bacc
    from concourse.bass_utils import run_bass_kernel_spmd

    nc = bacc.Bacc("TRN2", target_bir_lowering=False, num_devices=1)
    arrays = {f"in_{name}": np.ascontiguousarray(inputs[name]) for name in _INS}
    arrays["in_const_a"] = np.concatenate(list(CONST_A.values()), axis=1)
    arrays["in_const_b"] = np.concatenate(list(CONST_B.values()), axis=1)
    args = [nc.dram_tensor(k, a.shape, mybir.dt.from_np(a.dtype), kind="ExternalInput").ap()
            for k, a in arrays.items()]
    args += [nc.dram_tensor(f"out_{i}", shape, F32, kind="ExternalOutput").ap() for i, shape in enumerate(_OUTS)]
    build(nc, *args)
    r = run_bass_kernel_spmd(nc, [arrays], core_ids=[0])
    return tuple(r.results[0][f"out_{i}"] for i in range(len(_OUTS)))
```

```python
from contextlib import ExitStack

import numpy as np

import concourse.bass as bass
from concourse import mybir
from concourse.alu_op_type import AluOpType as ALU

ACT = mybir.ActivationFunctionType
F32 = mybir.dt.float32
F32R = mybir.dt.float32r

D = 2048
T = 512
NB = 8
TT = T + NB
HT = TT // 2
HD = 64
DR = D // 2
NH = DR // HD
PAIRS = NH // 2
KT = D // 128
LORA = 96
SHIFT = 3 * DR + 2 * LORA
DIN = SHIFT + DR + 4 * DR
OFF_A = (0, DR, 2 * DR, SHIFT)
OFF_B = tuple(SHIFT + DR * (1 + j) for j in range(4))
C = 128
NC = T // C
MID = C // 2 - 1
LEVELS = 7
WIN = 2048
DEC = float(np.exp(-0.5))
RMS_EPS = 1e-6
GN_EPS = 64e-5
L2_EPS = 1e-12
BIG = 1e30
LNS = 30
TS = (128, 97, 96)
NS = sum(TS)

PV = ("mu_r", "mu_k", "mu_v", "w0", "a0", "k_k", "k_a", "r_k", "gn_w", "gn_b")
NPV = len(PV)
ROW_NW = NPV * 8
ROW_MU = ROW_NW + KT
ROW_QK = ROW_MU + 2
ROWS = ROW_QK + 2
N_ROWS = NPV + 1 + 1 + 4


def multiplicity(dist):
    dist = np.asarray(dist)
    ok = dist >= 0
    return ((ok & (dist <= 128)).astype(np.float32) + (ok & (dist % 4 == 0) & (dist <= 512))
            + (ok & (dist % 16 == 0) & (dist <= 2048))).astype(np.float32)


def constants():
    p = np.arange(128)[:, None]
    f = np.arange(128)[None, :]
    out = {}
    out["ident"] = (p == f)
    out["blk"] = (p // HD == f // HD)
    out["blkmean"] = (p // HD == f // HD) / HD
    out["causal"] = np.concatenate([p < f, p <= f], axis=1)
    for lv in range(LEVELS - 1):
        m = 2 ** lv
        out[f"lev{lv}"] = (p // (2 * m) == f // (2 * m)) & (p % (2 * m) >= m) & (f % (2 * m) < m)
    out["lev0t"] = out["lev0"].T
    out["ones"] = np.ones((128, C))
    out["spread"] = np.concatenate([(p == f // 16) & (f // 8 % 2 == h) for h in range(2)], axis=1)
    out["group"] = p % 8 == np.arange(8)[None, :]
    out["place"] = p % 16 == np.arange(16)[None, :]
    out["gather"] = p // 16 == np.arange(NB)[None, :]
    ca = {k: np.ascontiguousarray(v, dtype=np.float32) for k, v in out.items()}
    slopes = 2.0 ** (-8.0 * np.arange(1, NH + 1) / NH)
    dist = (T - 128) + p - np.arange(T)[None, :]
    mult = multiplicity(dist)
    cb = {"dist": np.where(mult > 0, -dist, -BIG), "mult": mult,
          "slope": np.broadcast_to(slopes[None, :], (128, NH))}
    ds = np.concatenate([128 - np.arange(128), 512 - 4 * np.arange(96), [0], 2048 - 16 * np.arange(96)])
    cb["sdist"] = np.broadcast_to(-ds[None, :], (128, NS))
    cb["smult"] = np.broadcast_to(multiplicity(ds)[None, :], (128, NS))
    cb["sslope"] = slopes[2 * np.arange(PAIRS)[None, :] + (np.arange(128) % 2)[:, None]]
    cb = {k: np.ascontiguousarray(v, dtype=np.float32) for k, v in cb.items()}
    return ca, cb


CONST_A, CONST_B = constants()


def layout(table):
    at, n = {}, 0
    for k, v in table.items():
        at[k] = (n, n + v.shape[1])
        n += v.shape[1]
    return at, n


AT_A, NCA = layout(CONST_A)
AT_B, NCB = layout(CONST_B)


class Steps:

    def __init__(self, names, ahead=True):
        self.first = len(names) if ahead else 0
        self.names = names
        self.n = len(names)
        self.index = {k: j for j, k in enumerate(names)}
        assert len(self.index) == self.n
        self.turn = 0

    def at(self, i, name):
        return i * self.n + (self.first + self.index[name] + 1)

    def start(self, i):
        return i * self.n + self.first

    def one(self, name):
        assert self.names[self.turn % self.n] == name, (self.names[self.turn % self.n], name)
        self.turn += 1
        return 1


class Arena:
    def __init__(self, base, size):
        self.base, self.size, self.pos = base, size, 0

    def take(self, *shape):
        n = int(np.prod(shape))
        a = self.base[:, self.pos:self.pos + n]
        self.pos += n
        assert self.pos <= self.size, (self.pos, self.size)
        if len(shape) == 2:
            a = a.rearrange("p (a b) -> p a b", a=shape[0])
        elif len(shape) == 3:
            a = a.rearrange("p (a b c) -> p a b c", a=shape[0], b=shape[1])
        return a


LV = range(1, LEVELS)
GRAMS = ("gb0", "gk0", "gb1", "gk1", "nn01", "gb2", "gk2", "gb3", "gk3", "nn23")
UNITS = 4 * KT
BEHIND_A = {"lora": 4, "kk": 3, "tail": 3, "bonus": 10, "vec": 1, "nn01": 1, "bcast": 3,
            **{f"tr{l}{h}": 1 for l in LV for h in "ab" if l < LEVELS - 1}, "qt6b": 1, "dx6b": 1,
            **{f"{s}{c}": 1 for c in range(NC) for s in ("rhs", "u", "s")},
            "y0": 2, "y1": 2, "y2": 2, "y3": 1, "st": 2, "mean": 3}
QB = T // 128
JS = [(h, b) for h in range(2) for b in range(QB)]
BEHIND_B = {"ssum": 6, "tokv": 2, "stok": 2, "qb": 13,
            **{f"s{j}": (1, 1, 2, 2)[j % QB] for j in range(len(JS))},
            **{f"t{j}": (1, 2, 2, 3)[j % QB] for j in range(len(JS))},
            "sct": 4, "pwt": 3, "av": 2}


def spread(behind, names):
    behind = dict(behind)
    behind[names[-1]] = behind.get(names[-1], 0) + UNITS - sum(behind.values())
    assert behind[names[-1]] >= 0, behind[names[-1]]
    out, at = {}, 0
    for k in names:
        out[k] = range(at, at + behind.get(k, 0))
        at += behind.get(k, 0)
    return out


def build(nc, x_prompt, x_sample, state_wkv, state_shift, cache_k, cache_v, norm_w, w_in, mu_shift,
          w0, w_up, a0, a_up, k_k, k_a, r_k, gn_w, gn_b, q_norm, k_norm, w_out, const_a, const_b,
          y_prompt, y_sample, wkv_p, shift_p, k_p, v_p, wkv_s, shift_s, k_s, v_s):
    w_view = w_in.rearrange("(t p) n -> p t n", p=128)
    wo_view = w_out.rearrange("(t p) n -> p t n", p=128)
    xp = x_prompt[0].rearrange("(t p) d -> p t d", p=128)
    xs = x_sample[:, 0, :]
    yp = y_prompt[0].rearrange("(t p) d -> p t d", p=128)
    ys = y_sample[:, 0, :]
    kc_view = cache_k.rearrange("b s h d -> s b (h d)")
    vc_view = cache_v.rearrange("b s h d -> s b (h d)")
    kp_view = k_p[0].rearrange("(t p) h d -> p t (h d)", p=128)
    vp_view = v_p[0].rearrange("(t p) h d -> p t (h d)", p=128)
    ks_view = k_s[:, 0].rearrange("b h d -> b (h d)")
    vs_view = v_s[:, 0].rearrange("b h d -> b (h d)")
    mix_d = nc.dram_tensor("mix_scratch", (D, TT), F32, kind="Internal").ap()

    with ExitStack() as ctx:
        def sb(name, shape, dt=F32):
            return ctx.enter_context(nc.sbuf_tensor(name, shape, dt))

        def sem(name):
            return ctx.enter_context(nc.semaphore(name))

        XH = sb("XH", [128, KT, TT], F32R)
        XL = sb("XL", [128, KT, TT], F32R)
        WR = sb("WR", [128, 4, 8, 128])
        WH = sb("WH", [128, 2, 8, 128], F32R)
        WL = sb("WL", [128, 2, 8, 128], F32R)
        CA = sb("CA", [128, NCA])
        PT = sb("PT", [128, ROWS])
        SST = sb("SST", [128, 26, NB])
        BIAS = sb("BIAS", [128, 3])
        ARENA_N = 26000
        AREN = sb("AREN", [128, ARENA_N])
        ACC = [ctx.enter_context(nc.psum_tensor(f"acc{j}", [128, 2, 512], F32)) for j in range(2)]
        HB = ctx.enter_context(nc.psum_tensor("head_banks", [128, 4, 512], F32))
        ca = {k: CA[:, a:b] for k, (a, b) in AT_A.items()}
        ident, blk, blkmean = ca["ident"], ca["blk"], ca["blkmean"]

        def bc(a, n):
            return a.unsqueeze(1).to_broadcast([a.shape[0], n, a.shape[1]])

        s_const, s_rows, s_srow = sem("const_landed"), sem("param_rows_landed"), sem("shift_rows_landed")
        s_xt = [sem(f"x_landed{t}") for t in range(5)]
        s_w = [sem(f"w_landed{j}") for j in range(4)]
        s_lu = sem("lora_up_landed")
        s_hi, s_lo = sem("half_rounded"), sem("half_rest")
        s_half, s_evac = sem("half_multiplied"), sem("tile_evacuated")
        s_zero = sem("pair_buffers_zeroed")
        p_pe, p_act, p_dve, p_pool = sem("pro_pe"), sem("pro_act"), sem("pro_dve"), sem("pro_pool")
        a_pe, a_act, a_dve, a_pool = sem("a_pe"), sem("a_act"), sem("a_dve"), sem("a_pool")
        b_pe, b_act, b_dve, b_pool = sem("b_pe"), sem("b_act"), sem("b_dve"), sem("b_pool")
        c_pe, c_act, c_dve, c_pool = sem("c_pe"), sem("c_act"), sem("c_dve"), sem("c_pool")
        s_passed = sem("waits_passed")
        a_mix, b_sq = sem("a_token_shift"), sem("b_squares")
        o_ltail, o_tail, o_state, o_mix = sem("lora_tail_out"), sem("tail_out"), sem("state_out"), sem("mix_out")
        o_k, o_v, o_skv = sem("k_out"), sem("v_out"), sem("sample_kv_out")
        s_krow, s_vrow = sem("k_row_landed"), sem("v_row_landed")
        s_kc, s_vc = sem("k_cache_landed"), sem("v_cache_landed")
        s_cb = sem("const_b_landed")
        s_sst, o_sst = sem("sample_state_landed"), sem("sample_state_out")
        s_mt = [sem(f"mix_landed{q}") for q in range(3)]
        s_xr = [sem(f"x_again{j}") for j in range(2)]
        o_y = [sem(f"y_out{j}") for j in range(2)]

        pro = Arena(AREN, ARENA_N)
        XTOK = pro.take(5, D)
        ROWT = pro.take(128)
        SROW = pro.take(SHIFT)
        SSQ = pro.take(16)
        SQJ = pro.take(D)
        aa = Arena(AREN, ARENA_N)
        TW, AD = aa.take(TT), aa.take(TT)
        LU = aa.take(2, 128)
        S0 = aa.take(8, HD)
        z_at, z_end = aa.pos, aa.pos + 4 * (TT + 1)
        Z = aa.take(4, TT + 1)
        PAR, PGN, SSP = aa.take(NPV - 2), aa.take(2), aa.take(3, NB)
        M3 = aa.take(3, TT)
        A_, GG, BON = aa.take(TT), aa.take(TT), aa.take(TT)
        DCS = aa.take(NB)
        GL, G = aa.take(NC), aa.take(NC)
        BT, KTL = aa.take(TT), aa.take(T)
        ARP = aa.take(NC, 4, C)
        TOKB, TOKK, TOKV = aa.take(NC, 128), aa.take(NC, 128), aa.take(NC, 128)
        GB, GK = aa.take(NC, 4, C), aa.take(NC, 4, C)
        NN = aa.take(2 * NC, C)
        RHS, U, S = aa.take(2, 128), aa.take(NC, 128), aa.take(NC, 128)
        ST = aa.take(128)
        TAIL = aa.take(3, 128)
        VEC = aa.take(6, 128)
        RV = aa.take(6, HD)
        V8, SA8, Y8 = aa.take(8), aa.take(8), aa.take(8)
        early = aa.pos
        SGW, KSQ, SSM, RN = aa.take(TT), aa.take(TT), aa.take(TT), aa.take(TT)
        LS, LC = aa.take(T), aa.take(NC, C + 1)
        E1, E2 = aa.take(NC, C + 1), aa.take(NC, C + 1)
        KP, KK, KKA, T1 = aa.take(TT), aa.take(TT), aa.take(TT), aa.take(TT)
        late = Arena(AREN, ARENA_N)
        late.pos = early
        NM = [late.take(8, C), late.take(8, C)]
        X, XT, QT = late.take(8, C), late.take(8, C), late.take(8, C)
        PX, S1 = late.take(8, HD), late.take(8, HD)
        assert late.pos <= aa.pos
        PXF = PX.rearrange("p a b -> p (a b)")
        GBF = GB.rearrange("p a b c -> p (a b c)")
        Y, YC, YSQ = GBF[:, 0:TT], GBF[:, TT:2 * TT], GBF[:, 2 * TT:3 * TT]
        MIXO = BT
        lo = Arena(AREN, ARENA_N)
        lo.pos = pro.pos
        ZL, DL, ML = lo.take(2, TT + 1), lo.take(2, TT), lo.take(2, TT)
        LTAIL = lo.take(2, LORA)
        ba = Arena(AREN, ARENA_N)
        PTR = ba.take(2, T)
        SL, SSL, QW, QS = ba.take(2), ba.take(1), ba.take(2), ba.take(NB)
        MX, ZS, RZ, SMX = ba.take(8), ba.take(8), ba.take(8), ba.take(4)
        PW, SCO = ba.take(3, 16), ba.take(3, 16)
        ZB = Z[:, :, 1:TT + 1]
        assert ba.pos <= z_at
        ba.pos = z_end
        SQ, LN, RNB = ba.take(2, TT), ba.take(2, TT), ba.take(2, TT)
        QP = ba.take(2, TT)
        KN, GGB = ba.take(TT), ba.take(TT)
        KTOK, VTOK = ba.take(QB, 128), ba.take(QB, 128)
        SKV = ba.take(2, 128)
        BTB = ba.take(2, T)
        SC2, EE, PP = ba.take(2, T), ba.take(2, T), ba.take(2, T)
        DG = ba.take(2, 128)
        MIXB = ba.take(TT)
        PR = ba.take(NB, 128)
        PRF = PR.rearrange("p b c -> p (b c)")
        BTS = ba.take(NS)
        SS_, SE, SP_, SPN = ba.take(NS), ba.take(NS), ba.take(NS), ba.take(NS)
        CB = ba.take(NCB)
        cb = {k: CB[:, a:b] for k, (a, b) in AT_B.items()}
        KC, VC = ba.take(3, NB, 128), ba.take(3, NB, 128)
        cc = Arena(AREN, ARENA_N)
        YT = cc.take(2, TT)
        XR, XRS = cc.take(2, 4, 128), cc.take(2, 128)
        YO, YOS = cc.take(2, 4, 128), cc.take(2, 128)

        PE_P = Steps(["rows", "shift", *[f"x{k}" for k in range(KT)], "ltail"], ahead=False)
        ACT_P = Steps([*[f"{s}{t}" for t in (4, 0, 1, 2, 3) for s in ("sq", "ln", "rs")],
                       *[f"hi{k}" for k in range(KT)], "tanh", "ltail"], ahead=False)
        DVE_P = Steps(["zrow", "bias", "xn4", "xn0", "xn1", "xn2", "xn3", "rows", "shift",
                       *[f"lo{k}" for k in range(KT)],
                       "lz", "ldiff", "lds", "lmix"], ahead=False)
        last = LEVELS - 1
        PE_A = Steps(["lora", "kk", "tail", "bonus", "vec", *GRAMS, "tokb", "tokk", "tokv", "bcast",
                      *[f"{s}{l}{h}" for l in LV for s in ("qt", "dx", "tr") for h in "ab"
                        if (l, s) != (last, "tr")],
                      *[f"{s}{c}" for c in range(NC) for s in ("rhs", "u", "s", "y")],
                      "st", "mean", "var"])
        ACT_A = Steps(["ksq", "sgw", "sga", "sgg", "ln", "rn", "e1", "e2", "g", "dcs", "tail", "vec",
                       "nn01", "nn23", "tokb", "tokk", "tokv", "rv",
                       *[f"{s}{l}" for l in LV for s in ("qt", "tr") if (l, s) != (last, "tr")],
                       *[f"{s}{c}" for c in range(NC) for s in ("rhs", "u")],
                       "st", "y", "ysq", "yln", "yrs"])
        DVE_M = Steps(["par", "dsh", "dss", "mix"], ahead=False)
        half_grams = lambda a, b: [f"{s}{c}" for c in (a, a + 1) for s in ("gb", "gk")] + [f"{x}{b}" for x in ("xm", "x", "xtm", "xt")]
        DVE_A = Steps(["gnp", "ssm", "scan", "lcm", "lc0", "gl0", "gl", "t1", "kp", "prod",
                       "kk", "at", "kka", "rt", "bt", "kt", "bon",
                       *half_grams(0, "a"), *half_grams(2, "b"),
                       *[f"{s}{l}" for l in LV for s in ("qt", "xa", "xb", "tr")
                         if (l, s) != (last, "tr")],
                       "s0", "vm", "v8", "p1", "sa", "sw", "s1", "p2", "sb", "p3", "s2", "sc", "p4", "ry", "ye", "s3",
                       "yc", "yn", "yb", "ym"])
        POOL_A = Steps(["gate", *[f"nm{l}" for l in LV if l < last]])
        nj = len(JS)
        two_on = lambda s, j: [f"{s}{j + 2}"] if j + 2 < nj else []
        seq = ["s0", "s1"] + [x for j in range(nj) for x in two_on("s", j) + [f"t{j}", f"o{j}"]]
        PE_B = Steps(["ssum", "tokk", "tokv", "stok", "qb", *seq, "sct", "pwt", "av", "avt"])
        ACT_B = Steps(["ln", "rn", "tokk", "tokv", "stok", "sgg", "ex0", "ex1",
                       *[x for j in range(nj) for x in [f"tp{j}"] + two_on("ex", j)], "sex", "pwc", "avc"])
        DVE_B = Steps(["sl", "kn", "qn", "qs", "gate",
                       *[x for t in range(3) for x in (f"pr{t}", f"rd{t}")],
                       "mx0", "mx1", *[x for j in range(nj) for x in [f"pm{j}", f"rz{j}", f"dg{j}"] + two_on("mx", j)],
                       "smx", "spm", "srz", "spn", "mixp", "mixs"])
        POOL_B = Steps(["bt", "bts"])
        ACT_CP = Steps([*[f"hi{k}" for k in range(KT)]], ahead=False)
        DVE_C = Steps(["ya", "yb"], ahead=False)

        span_a, span_b = spread(BEHIND_A, PE_A.names), spread(BEHIND_B, PE_B.names)

        def group_a(i):
            return i * 2 + 1

        def group_b(i):
            return i * 2 + (1 + 2 * PAIRS)

        GROUP_C = 1 + 4 * PAIRS

        def load_half(sp, g, k, src):
            if not (isinstance(g, int) and 4 * g + k < 4):
                sp.wait_ge(s_hi, g * 4 + (k - 3))
                sp.wait_ge(s_lo, g * 4 + (k - 3))
            sp.dma_start(WR[:, k % 4, :, 0:src.shape[2]], src).then_inc(s_w[k % 4], 16)

        def round_half(act, g, k, M=128):
            act.wait_ge(s_w[k % 4], (g + (k // 4 + 1)) * 16)
            if not (isinstance(g, int) and 4 * g + k < 2):
                act.wait_ge(s_half, g * 4 + (k - 1))
            act.activation(WH[:, k % 2, :, 0:M], WR[:, k % 4, :, 0:M], ACT.Copy).then_inc(s_hi, 1)

        def rest_half(pool, g, k, M=128):
            pool.wait_ge(s_w[k % 4], (g + (k // 4 + 1)) * 16)
            pool.wait_ge(s_hi, g * 4 + (k + 1))
            if not (isinstance(g, int) and 4 * g + k < 2):
                pool.wait_ge(s_half, g * 4 + (k - 1))
            pool.tensor_tensor(WL[:, k % 2, :, 0:M], WR[:, k % 4, :, 0:M],
                               WH[:, k % 2, :, 0:M].bitcast(F32), ALU.subtract).then_inc(s_lo, 1)

        def multiply_unit(pe, g, u, M=128):
            t, kt, k = u // KT, u % KT, u // 8
            if u % 8 == 0:
                pe.wait_ge(s_lo, g * 4 + (k + 1))
            if kt == 0 and not (isinstance(g, int) and 2 * g + t < 2):
                pe.wait_ge(s_evac, g * 2 + (t - 1))
            acc = ACC[t % 2]
            j = kt % 8
            for n, (w, x) in enumerate(((WH, XH), (WH, XL), (WL, XH))):
                for hf in range(2):
                    mm = pe.matmul(acc[0:M, hf, 0:HT], w[:, k % 2, j, 0:M], x[:, kt, hf * HT:(hf + 1) * HT],
                                   start=(kt == 0 and n == 0), stop=(kt == KT - 1 and n == 2))
            if u % 8 == 7:
                mm.then_inc(s_half, 1)

        def evacuate(act, g, t, dst, M=128):
            act.wait_ge(s_half, g * 4 + (2 * t + 2))
            act.activation(dst, ACC[t % 2][0:M, :, 0:HT], ACT.Copy).then_inc(s_evac, 1)

        def two(a):
            return a.rearrange("p (a b) -> p a b", a=2)

        def pe_fill(pe, span, g, name):
            for u in span[name]:
                multiply_unit(pe, g, u)

        def act_feed(act, span, g, name, dst, ahead=True):
            for u in span[name]:
                if u % 8 == 1 and (ahead or u // 8 < 7):
                    round_half(act, g, u // 8 + 1)
                if u % KT == KT - 1:
                    evacuate(act, g, u // KT, dst(u // KT))

        def pool_feed(pool, span, g, name, ahead=True):
            for u in span[name]:
                if u % 8 == 1 and (ahead or u // 8 < 7):
                    rest_half(pool, g, u // 8 + 1)

        half_t = lambda a: a.rearrange("b (i h) (c v) k -> i b (h c) v k", i=PAIRS, v=8)

        def done(count, i, n):
            return i * n + (1 + count) * n

        block = ctx.enter_context(nc.Block())
        HBF = HB[:, :, :].rearrange("p a b -> p (a b)")
        par_view = PT[:, 0:8 * NPV].rearrange("p (v i) -> p i v", i=8)
        ssp_view = SST[:, 0:24, :].rearrange("p (s i) b -> p i s b", i=8)
        P_ = {k: PAR[:, j:j + 1] for j, k in enumerate(PV[:NPV - 2])}
        eps_rms, eps_gn, ln_back = BIAS[:, 0:1], BIAS[:, 1:2], BIAS[:, 2:3]

        def w_half(off, i, k):
            cols = w_view[:, :, off:off + DR].rearrange("p t (i c) -> p t i c", i=PAIRS)
            return cols[:, 8 * (k % 2):8 * (k % 2) + 8, i, :]

        @block.sync
        def _(sp):
            sp.dma_start(XTOK[0:NB, 4, :], xs).then_inc(s_xt[4], 16)
            for t in range(4):
                sp.dma_start(XTOK[:, t, :], xp[:, t, :]).then_inc(s_xt[t], 16)
            sp.dma_start(CA[:, :], const_a).then_inc(s_const, 16)
            for s, n in ((o_tail, 32), (o_state, 32), (o_mix, 16), (o_sst, 16), (o_k, 16), (o_v, 16), (o_skv, 32),
                         (s_krow, 16), (s_vrow, 16), (c_dve, 2), (c_pe, 2), (o_y[0], 32), (o_y[1], 32)):
                sp.sem_inc(s, n)
            for k in range(4):
                src = w_view[:, 8 * (k % 2):8 * (k % 2) + 8, 3 * DR + LORA * (k // 2):3 * DR + LORA * (k // 2 + 1)]
                load_half(sp, 0, k, src)
            for k in range(8):
                load_half(sp, group_a(0), k, w_half(OFF_A[k // 2], 0, k))

            def lora_up(i):
                if not isinstance(i, int) or i > 0:
                    sp.wait_ge(a_pe, PE_A.at(i - 1, "lora"))
                else:
                    sp.wait_ge(p_pe, PE_P.at(0, f"x{KT - 1}"))
                up = (w_up, a_up)
                for j in range(2):
                    sp.dma_start(LU[0:LORA, j, :], up[j].rearrange("l (i c) -> l i c", i=PAIRS)[:, i, :]).then_inc(s_lu, 16)

            def states(i):
                if not isinstance(i, int) or i > 0:
                    sp.wait_ge(a_dve, DVE_A.at(i - 1, "sw"))
                sp.dma_start(S0, half_t(state_wkv)[i]).then_inc(s_sst, 16)

            def states_out(i):
                sp.wait_ge(a_dve, DVE_A.at(i, "ry"))
                sp.dma_start(half_t(wkv_s)[i], S1).then_inc(o_sst, 16)

            lora_up(0)
            states(0)
            with sp.Fori(1, PAIRS) as i:
                for k in range(8):
                    load_half(sp, group_a(i), k, w_half(OFF_A[k // 2], i, k))
                    if k == 3:
                        lora_up(i)
                states(i)
                states_out(i - 1)

            def phase_a_done():
                sp.wait_ge(a_pe, PE_A.start(PAIRS))
                sp.wait_ge(a_act, ACT_A.start(PAIRS))
                sp.wait_ge(a_dve, DVE_A.start(PAIRS))
                sp.wait_ge(a_pool, POOL_A.start(PAIRS))
                sp.wait_ge(o_mix, done(0, PAIRS, 16))
                sp.wait_ge(o_sst, done(0, PAIRS, 16))
                sp.wait_ge(o_state, done(0, PAIRS, 32))
                sp.wait_ge(o_tail, done(0, PAIRS, 32))

            def caches(i):
                if not isinstance(i, int) or i > 0:
                    sp.wait_ge(b_dve, DVE_B.at(i - 1, "pr2"))
                for n, (dst, view, s) in enumerate(((KC, kc_view, s_kc), (VC, vc_view, s_vc))):
                    if n == 1 and (not isinstance(i, int) or i > 0):
                        sp.wait_ge(b_pe, PE_B.at(i - 1, "av"))
                    cols = view.rearrange("s b (i c) -> s b i c", i=PAIRS)
                    sp.dma_start(dst[:, 0, :, :], cols[WIN - 128:WIN, :, i, :]).then_inc(s, 16)
                    sp.dma_start(dst[0:96, 1, :, :], cols[WIN - 512:WIN - 128:4, :, i, :]).then_inc(s, 16)
                    sp.dma_start(dst[0:96, 2, :, :], cols[0:WIN - 512:16, :, i, :]).then_inc(s, 16)

            def group_b_on(i):
                for k in range(1, 8):
                    load_half(sp, group_b(i), k, w_half(OFF_B[k // 2], i, k))
                load_half(sp, group_b(i), 8, w_half(OFF_B[0], i + 1, 0))

            load_half(sp, group_b(0), 0, w_half(OFF_B[0], 0, 0))
            group_b_on(0)
            states_out(PAIRS - 1)
            phase_a_done()
            sp.dma_start(CB, const_b).then_inc(s_cb, 16)
            caches(0)
            with sp.Fori(1, PAIRS - 1) as i:
                group_b_on(i)
                caches(i)
            for k in range(1, 8):
                load_half(sp, group_b(PAIRS - 1), k, w_half(OFF_B[k // 2], PAIRS - 1, k))
            wo_half = lambda m, k: (wo_view.rearrange("p t (m u c) -> p t m u c", u=2, c=128)
                                    [:, 8 * (k % 2):8 * (k % 2) + 8, m, k // 2, :])
            load_half(sp, GROUP_C, 0, wo_half(0, 0))
            caches(PAIRS - 1)

            def x_again(m, t):
                cols = xp.rearrange("p t (m u c) -> p t m u c", u=2, c=128)
                scol = xs.rearrange("b (m u c) -> b m u c", u=2, c=128)
                sp.wait_ge(c_dve, done(0, m, 2))
                sp.dma_start(XR[:, t, :, :], cols[:, :, m, t, :]).then_inc(s_xr[t], 16)
                sp.dma_start(XRS[0:NB, t, :], scol[:, m, t, :]).then_inc(s_xr[t], 16)

            for k in range(1, 4):
                load_half(sp, GROUP_C, k, wo_half(0, k))
            sp.wait_ge(s_half, 4 * GROUP_C)
            mt = mix_d.rearrange("(t p) c -> p t c", p=128)
            for q, (a, b, pairs) in enumerate(((0, KT // 2, 0), (KT // 2, KT - 1, PAIRS - 1), (KT - 1, KT, PAIRS))):
                sp.wait_ge(o_mix, done(0, PAIRS + pairs, 16))
                sp.dma_start(XL[:, a:b, :].bitcast(F32), mt[:, a:b, :]).then_inc(s_mt[q], 16)
            sp.wait_ge(b_pe, PE_B.start(PAIRS))
            sp.wait_ge(b_act, ACT_B.start(PAIRS))
            sp.wait_ge(b_dve, DVE_B.start(PAIRS))
            for t in range(2):
                x_again(0, t)
            with sp.Fori(1, D // 256) as m:
                for k in range(4):
                    load_half(sp, m + GROUP_C, k, wo_half(m, k))
                for t in range(2):
                    x_again(m, t)

        @block.gpsimd
        def _(pool):
            pool.sem_inc(a_pool, POOL_A.n)
            pool.sem_inc(b_pool, POOL_B.n)
            for k in range(4):
                rest_half(pool, 0, k, LORA)
            for k in range(9):
                rest_half(pool, group_a(0), k)

            def pair_a(i, g, ahead=True):
                def feed(name):
                    pool_feed(pool, span_a, g, name, ahead)

                pool.wait_ge(a_act, ACT_A.at(i, "sgg"))
                pool.tensor_tensor(GG, GG, Z[:, 3, 1:TT + 1], ALU.mult).then_inc(a_pool, POOL_A.one("gate"))
                for name in ("lora", "kk", "tail", "bonus", "vec", *GRAMS):
                    feed(name)
                for l in range(1, last):
                    if l == 1:
                        pool.wait_ge(a_act, ACT_A.at(i, "nn23"))
                        pool.wait_ge(a_dve, DVE_A.at(i, "bt"))
                    elif l > 2:
                        pool.wait_ge(a_pe, PE_A.at(i, f"qt{l - 2}b"))
                    pool.tensor_tensor(NM[(l - 1) % 2], NN, bc(ca[f"lev{l}"], 8), ALU.mult)\
                        .then_inc(a_pool, POOL_A.one(f"nm{l}"))
                    if l == 1:
                        for name in ("tokb", "tokk", "tokv", "bcast"):
                            feed(name)
                    if l > 1:
                        for s in ("qt", "dx", "tr"):
                            for h in "ab":
                                feed(f"{s}{l - 1}{h}")
                for name in PE_A.names[PE_A.index[f"qt{last - 1}a"]:]:
                    feed(name)

            with pool.Fori(0, PAIRS - 1) as i:
                pair_a(i, group_a(i + 1))
            pair_a(PAIRS - 1, group_b(0))

            def pair_b(i, g, ahead=True, fill=True):
                def feed(name):
                    if fill:
                        pool_feed(pool, span_b, g, name, ahead)

                feed("ssum")
                pool.wait_ge(b_dve, DVE_B.at(i, "sl"))
                pool.sem_inc(s_passed, 1)
                pool.wait_ge(s_cb, 16)
                for h in range(2):
                    bt = pool.tensor_scalar(BTB[:, h, :], cb["dist"], SL[:, h:h + 1], 1.0, ALU.mult, ALU.mult)
                bt.then_inc(b_pool, POOL_B.one("bt"))
                pool.tensor_scalar(BTS[0:16, :], cb["sdist"][0:16, :], SSL[0:16, :], 1.0, ALU.mult, ALU.mult)\
                    .then_inc(b_pool, POOL_B.one("bts"))
                for name in PE_B.names[1:]:
                    feed(name)

            with pool.Fori(0, PAIRS - 1) as i:
                pair_b(i, group_b(i + 1))
            pair_b(PAIRS - 1, 0, fill=False)

            rest_half(pool, GROUP_C, 1)
            for k in range(KT):
                pool.wait_ge(c_act, ACT_CP.at(0, f"hi{k}"))
                pool.tensor_tensor(XL[:, k, :], XL[:, k, :].bitcast(F32), XH[:, k, :].bitcast(F32),
                                   ALU.subtract).then_inc(c_pool, 1)
            for k in range(2, 4):
                rest_half(pool, GROUP_C, k)
            with pool.Fori(1, D // 256) as m:
                for k in range(4):
                    rest_half(pool, m + GROUP_C, k)

        @block.tensor
        def _(pe):
            pe.sem_inc(a_pe, PE_A.n)
            pe.sem_inc(b_pe, PE_B.n)
            pe.wait_ge(s_const, 16)
            pe.wait_ge(s_rows, 16 * N_ROWS)
            pe.transpose(HB[:, 0, 0:ROWS], ROWT[0:ROWS, :], ident[0:ROWS, 0:ROWS]).then_inc(p_pe, PE_P.one("rows"))
            pe.wait_ge(s_srow, 16)
            for j in range(24):
                pe.transpose(HB[:, 1, NB * j:NB * (j + 1)], SROW[0:NB, 128 * j:128 * (j + 1)], ident[0:NB, 0:NB])
            for j in range(2):
                tr = pe.transpose(HB[0:LORA, 1, NB * (24 + j):NB * (25 + j)],
                                  SROW[0:NB, 3 * DR + LORA * j:3 * DR + LORA * (j + 1)], ident[0:NB, 0:NB])
            tr.then_inc(p_pe, PE_P.one("shift"))
            for k in range(KT + 2):
                b = k % 2
                if k < KT:
                    if k == 0:
                        pe.wait_ge(p_dve, DVE_P.at(0, "xn3"))
                    if k < 2:
                        pe.wait_ge(p_dve, DVE_P.at(0, "shift"))
                    else:
                        pe.wait_ge(p_dve, DVE_P.at(0, f"lo{k - 2}"))
                    for t in range(4):
                        pe.transpose(HB[:, 2 * b, 128 * t:128 * (t + 1)], XTOK[:, t, 128 * k:128 * (k + 1)], ident)
                    pe.transpose(HB[:, 2 * b + 1, 0:NB], XTOK[0:NB, 4, 128 * k:128 * (k + 1)], ident[0:NB, 0:NB])\
                        .then_inc(p_pe, PE_P.one(f"x{k}"))
                if k >= 2:
                    pe.wait_ge(p_dve, DVE_P.at(0, f"lo{k - 2}"))
                    multiply_unit(pe, 0, k - 2, LORA)
            for u in range(KT, 2 * KT):
                multiply_unit(pe, 0, u, LORA)
            for u in range(UNITS):
                if u == 2 * KT:
                    pe.wait_ge(s_evac, 2)
                    for j in range(2):
                        tr = pe.transpose(HB[0:NB + 1, 0, LORA * j:LORA * (j + 1)], ZL[0:LORA, j, T:TT + 1],
                                          ident[0:LORA, 0:LORA])
                    tr.then_inc(p_pe, PE_P.one("ltail"))
                multiply_unit(pe, group_a(0), u)

            pe.wait_ge(p_act, ACT_P.n)

            def pair_a(i, g):
                def fill(name):
                    pe_fill(pe, span_a, g, name)

                def step(mm, name):
                    mm.then_inc(a_pe, PE_A.one(name))

                pe.wait_ge(s_lu, (i + 1) * 32)
                pe.wait_ge(a_act, ACT_A.at(i - 1, "yln"))
                pe.wait_ge(a_dve, DVE_A.at(i - 1, "yc"))
                for j, act_in in enumerate((TW, AD)):
                    for hf in range(2):
                        mm = pe.matmul(HB[:, 2 * j + hf, 0:HT], LU[0:LORA, j, :],
                                       act_in[0:LORA, hf * HT:(hf + 1) * HT], start=True, stop=True)
                mm.then_inc(a_pe, PE_A.one("lora"))
                fill("lora")
                pe.wait_ge(a_act, ACT_A.at(i, "sga"))
                for hf in range(2):
                    mm = pe.matmul(HB[:, hf, 0:HT], blk, KSQ[:, hf * HT:(hf + 1) * HT], start=True, stop=True)
                mm.then_inc(a_pe, PE_A.one("kk"))
                fill("kk")
                for s in range(3):
                    mm = pe.transpose(HB[0:NB + 1, 2, 128 * s:128 * (s + 1)], Z[:, s, T:TT + 1], ident)
                mm.then_inc(a_pe, PE_A.one("tail"))
                fill("tail")
                pe.wait_ge(a_dve, DVE_A.at(i, "prod"))
                pe.wait_ge(a_act, ACT_A.at(i, "tail"))
                for hf in range(2):
                    mm = pe.matmul(HB[:, 2 + hf, 0:HT], blk, T1[:, hf * HT:(hf + 1) * HT], start=True, stop=True)
                mm.then_inc(a_pe, PE_A.one("bonus"))
                fill("bonus")
                pe.wait_ge(a_dve, DVE_A.at(i, "kka"))
                pe.wait_ge(a_act, ACT_A.at(i, "dcs"))
                for v, src in enumerate((M3[:, 0], None, KP, M3[:, 2], KK, KKA)):
                    src = DCS if src is None else src[:, T:TT]
                    mm = pe.transpose(HB[0:NB, v // 4, 128 * (v % 4):128 * (v % 4 + 1)], src, ident)
                mm.then_inc(a_pe, PE_A.one("vec"))
                fill("vec")
                read_by = {"gb0": (a_dve, DVE_A, "bon"), "gk0": (a_dve, DVE_A, "bon"),
                           "gb1": (a_act, ACT_A, "vec"), "gk1": (a_act, ACT_A, "vec"),
                           "nn01": (a_dve, DVE_A, "gb0"), "gb2": (a_dve, DVE_A, "gk0"),
                           "gk2": (a_dve, DVE_A, "gb1"), "gb3": (a_dve, DVE_A, "gk1"),
                           "gk3": (a_act, ACT_A, "nn01"), "nn23": (a_dve, DVE_A, "gb2"),
                           "tokb": (a_dve, DVE_A, "gk2"), "tokk": (a_dve, DVE_A, "gb3"),
                           "tokv": (a_dve, DVE_A, "gk3"), "bcast": (a_act, ACT_A, "nn23")}
                for n, name in enumerate((*GRAMS, "tokb", "tokk", "tokv", "bcast")):
                    bank = (2 + n) % 4
                    s, steps, what = read_by[name]
                    pe.wait_ge(s, steps.at(i, what))
                    if name[:2] in ("gb", "gk"):
                        c = int(name[2])
                        lhs = (BT if name[1] == "b" else KTL)[:, c * C:(c + 1) * C]
                        mm = pe.matmul(HB[:, bank, :], lhs, ARP[:, c, :, :].rearrange("p a b -> p (a b)"),
                                       start=True, stop=True)
                    elif name[:2] == "nn":
                        for q in range(4):
                            c = int(name[2]) + q // 2
                            mm = pe.matmul(HB[:, bank, q * C:(q + 1) * C], ARP[:, c, q % 2, :],
                                           BT[:, c * C:(c + 1) * C], start=True, stop=True)
                    elif name == "bcast":
                        pe.wait_ge(a_act, ACT_A.at(i, "vec"))
                        for h in range(2):
                            mm = pe.matmul(HB[:, bank, 0:6 * HD], ca["spread"][0:NB, 128 * h:128 * (h + 1)],
                                           VEC[0:NB, :, HD * h:HD * (h + 1)], start=(h == 0), stop=(h == 1))
                    else:
                        src = {"tokb": BT, "tokk": KTL, "tokv": M3[:, 2]}[name]
                        for c in range(NC):
                            mm = pe.transpose(HB[:, bank, c * C:(c + 1) * C], src[:, c * C:(c + 1) * C], ident)
                    mm.then_inc(a_pe, PE_A.one(name))
                    fill(name)
                for l in LV:
                    nm = NM[(l - 1) % 2]
                    for h in range(2):
                        hn = "ab"[h]
                        bank = (3, 0)[h]
                        if h == 0:
                            if l < last:
                                pe.wait_ge(a_pool, POOL_A.at(i, f"nm{l}"))
                            if l == 1:
                                pe.wait_ge(a_dve, DVE_A.at(i, "xtb"))
                                pe.wait_ge(a_act, ACT_A.at(i, "rv"))
                            else:
                                pe.wait_ge(a_act, ACT_A.at(i, f"tr{l - 1}"))
                        elif l == 1:
                            pe.wait_ge(a_act, ACT_A.at(i, "tokb"))
                        else:
                            pe.wait_ge(a_dve, DVE_A.at(i, f"tr{l - 1}"))
                        if l == last:
                            pe.sem_inc(s_passed, 1)
                        for q in range(4):
                            if l < last:
                                mm = pe.matmul(HB[:, bank, q * C:(q + 1) * C], nm[:, 4 * h + q, :],
                                               XT[:, 4 * h + q, :], start=True, stop=True)
                            else:
                                mm = pe.matmul(HB[0:64, bank, q * 64:(q + 1) * 64], NN[64:128, 4 * h + q, 0:64],
                                               XT[64:128, 4 * h + q, 64:128], start=True, stop=True)
                        mm.then_inc(a_pe, PE_A.one(f"qt{l}{hn}"))
                        fill(f"qt{l}{hn}")
                    for h in range(2):
                        hn = "ab"[h]
                        bank = (1, 2)[h]
                        if h == 0:
                            pe.wait_ge(a_act, ACT_A.at(i, f"qt{l}"))
                            if l == 1:
                                pe.wait_ge(a_act, ACT_A.at(i, "tokk"))
                            else:
                                pe.wait_ge(a_dve, DVE_A.at(i, f"xa{l - 1}"))
                        else:
                            pe.wait_ge(a_dve, DVE_A.at(i, f"qt{l}"))
                            if l == 1:
                                pe.wait_ge(a_act, ACT_A.at(i, "tokv"))
                        if l == last:
                            pe.sem_inc(s_passed, 1)
                        for q in range(4):
                            if l < last:
                                mm = pe.matmul(HB[:, bank, q * C:(q + 1) * C], QT[:, 4 * h + q, :],
                                               X[:, 4 * h + q, :], start=True, stop=True)
                            else:
                                mm = pe.matmul(HB[0:64, bank, q * 64:(q + 1) * 64], X[0:64, 4 * h + q, 0:64],
                                               QT[0:64, 4 * h + q, 64:128], start=True, stop=True)
                        mm.then_inc(a_pe, PE_A.one(f"dx{l}{hn}"))
                        fill(f"dx{l}{hn}")
                    for h in range(2) if l < last else ():
                        hn = "ab"[h]
                        bank = (3, 0)[h]
                        pe.wait_ge(a_dve, DVE_A.at(i, f"x{hn}{l}"))
                        for q in range(4):
                            mm = pe.transpose(HB[:, bank, q * C:(q + 1) * C], X[:, 4 * h + q, :], ident)
                        mm.then_inc(a_pe, PE_A.one(f"tr{l}{hn}"))
                        fill(f"tr{l}{hn}")
                for c in range(NC):
                    if c == 0:
                        pe.wait_ge(a_dve, DVE_A.at(i, f"xb{last}"))
                        pe.wait_ge(a_act, ACT_A.at(i, f"qt{last}"))
                    else:
                        pe.wait_ge(a_dve, DVE_A.at(i, f"s{c - 1}"))
                        pe.wait_ge(a_act, ACT_A.at(i, f"rhs{c - 1}"))
                    first = True
                    for kind in ("state", "chunk") if c else ("chunk",):
                        for h in range(2):
                            cols = slice(HD * h, HD * (h + 1))
                            lhs, rhs = ((ARP[:, c, h, :], S[:, c - 1, cols]) if kind == "state" else
                                        (GK[:, c, h, :], TOKV[:, c, cols]))
                            mm = pe.matmul(HB[:, 3, cols], lhs, rhs, start=first, stop=(kind == "chunk"),
                                           skip_group_check=True)
                            first = False
                    mm.then_inc(a_pe, PE_A.one(f"rhs{c}"))
                    fill(f"rhs{c}")
                    pe.wait_ge(a_act, ACT_A.at(i, f"rhs{c}"))
                    if c:
                        pe.wait_ge(a_act, ACT_A.at(i, f"u{c - 1}"))
                    for h in range(2):
                        cols = slice(HD * h, HD * (h + 1))
                        mm = pe.matmul(HB[:, 0, cols], XT[:, 2 * c + h, :], RHS[:, c % 2, cols],
                                       start=(h == 0), stop=True, skip_group_check=True)
                    mm.then_inc(a_pe, PE_A.one(f"u{c}"))
                    fill(f"u{c}")
                    pe.wait_ge(a_act, ACT_A.at(i, f"u{c}"))
                    if c:
                        pe.matmul(HB[:, 2, 0:128], ident, S[:, c - 1, :], start=True, stop=False)
                    pe.matmul(HB[:, 2, 0:128], TOKK[:, c, :], TOKV[:, c, :], start=(c == 0), stop=False)
                    pe.matmul(HB[:, 2, 0:128], TOKB[:, c, :], U[:, c, :], start=False, stop=True)\
                        .then_inc(a_pe, PE_A.one(f"s{c}"))
                    fill(f"s{c}")
                    for h in range(2):
                        cols = slice(HD * h, HD * (h + 1))
                        out = HB[cols, 1, c * C:(c + 1) * C]
                        first = c == 0
                        if c:
                            pe.matmul(out, S[:, c - 1, cols], ARP[:, c, 2 + h, :], start=first, stop=False,
                                      skip_group_check=True)
                        pe.matmul(out, TOKV[:, c, cols], GK[:, c, 2 + h, :], start=first, stop=False,
                                  skip_group_check=True)
                        mm = pe.matmul(out, U[:, c, cols], GB[:, c, 2 + h, :], start=False, stop=True,
                                       skip_group_check=True)
                    mm.then_inc(a_pe, PE_A.one(f"y{c}"))
                    fill(f"y{c}")
                pe.wait_ge(a_dve, DVE_A.at(i, f"s{NC - 1}"))
                pe.transpose(HB[:, 3, 0:128], S[:, NC - 1, :], ident)
                pe.matmul(HB[:, 3, 128:128 + NB], PXF[:, 0:128], ca["gather"], start=True, stop=True)\
                    .then_inc(a_pe, PE_A.one("st"))
                fill("st")
                pe.wait_ge(a_act, ACT_A.at(i, "y"))
                for hf in range(2):
                    mm = pe.matmul(HB[:, hf, 0:HT], blkmean, Y[:, hf * HT:(hf + 1) * HT], start=True, stop=True)
                mm.then_inc(a_pe, PE_A.one("mean"))
                fill("mean")
                pe.wait_ge(a_act, ACT_A.at(i, "ysq"))
                for hf in range(2):
                    mm = pe.matmul(HB[:, 2 + hf, 0:HT], blkmean, YSQ[:, hf * HT:(hf + 1) * HT], start=True, stop=True)
                mm.then_inc(a_pe, PE_A.one("var"))
                fill("var")

            with pe.Fori(0, PAIRS - 1) as i:
                pair_a(i, group_a(i + 1))
            pair_a(PAIRS - 1, group_b(0))

            def pair_b(i, g, fills=True):
                def fill(name):
                    if fills:
                        pe_fill(pe, span_b, g, name)

                pe.wait_ge(b_sq, i + 1)
                pe.wait_ge(b_dve, DVE_B.start(i))
                for j in range(2):
                    for hf in range(2):
                        mm = pe.matmul(HB[:, 2 * j + hf, 0:HT], blkmean, SQ[:, j, hf * HT:(hf + 1) * HT],
                                       start=True, stop=True)
                mm.then_inc(b_pe, PE_B.one("ssum"))
                fill("ssum")
                pe.wait_ge(b_act, ACT_B.at(i, "ln"))
                pe.wait_ge(b_dve, DVE_B.at(i, "kn"))
                for t in range(QB):
                    mm = pe.transpose(HB[:, 0, 128 * t:128 * (t + 1)], KN[:, 128 * t:128 * (t + 1)], ident)
                mm.then_inc(b_pe, PE_B.one("tokk"))
                for t in range(QB):
                    mm = pe.transpose(HB[:, 1, 128 * t:128 * (t + 1)], ZB[:, 2, 128 * t:128 * (t + 1)], ident)
                mm.then_inc(b_pe, PE_B.one("tokv"))
                fill("tokv")
                pe.transpose(HB[0:NB, 2, 0:128], KN[:, T:TT], ident)
                pe.transpose(HB[0:NB, 2, 128:256], ZB[:, 2, T:TT], ident).then_inc(b_pe, PE_B.one("stok"))
                fill("stok")
                pe.wait_ge(b_dve, DVE_B.at(i, "qs"))
                pe.wait_ge(b_act, ACT_B.at(i, "tokv"))
                for b in range(NB):
                    mm = pe.matmul(HB[:, b // 4, 128 * (b % 4):128 * (b % 4 + 1)], QS[:, b:b + 1].to_broadcast([128, 128]),
                                   ident, start=True, stop=True)
                mm.then_inc(b_pe, PE_B.one("qb"))
                fill("qb")

                def score(j):
                    h, b = JS[j]
                    n = 128 * (b + 1)
                    if j < 2:
                        pe.wait_ge(b_dve, DVE_B.at(i, "pr2"))
                    else:
                        pe.wait_ge(b_dve, DVE_B.at(i, f"mx{j - 2}"))
                    pe.matmul(HB[:, j % 2, 0:n], QP[:, h, 128 * b:128 * (b + 1)], KN[:, 0:n], start=True, stop=True)\
                        .then_inc(b_pe, PE_B.one(f"s{j}"))
                    fill(f"s{j}")

                score(0)
                score(1)
                for j, (h, b) in enumerate(JS):
                    if j + 2 < nj:
                        score(j + 2)
                    pe.wait_ge(b_dve, DVE_B.at(i, f"dg{j}"))
                    pe.wait_ge(b_act, ACT_B.at(i, f"tp{j - 1}" if j else "stok"))
                    for t in range(b + 1):
                        mm = pe.matmul(HB[:, 2, 128 * t:128 * (t + 1)], PP[:, j % 2, 128 * t:128 * (t + 1)],
                                       DG[:, j % 2, :], start=True, stop=True)
                    mm.then_inc(b_pe, PE_B.one(f"t{j}"))
                    fill(f"t{j}")
                    pe.wait_ge(b_act, ACT_B.at(i, f"tp{j}"))
                    cols = slice(HD * h, HD * (h + 1))
                    for t in range(b + 1):
                        mm = pe.matmul(HB[cols, 3, 128 * b:128 * (b + 1)], VTOK[:, t, cols],
                                       PTR[:, j % 2, 128 * t:128 * (t + 1)], start=(b == 0 and t == 0),
                                       stop=(t == b), skip_group_check=True)
                    mm.then_inc(b_pe, PE_B.one(f"o{j}"))
                    fill(f"o{j}")
                pe.wait_ge(b_dve, DVE_B.at(i, f"dg{nj - 1}"))
                at = 0
                for t, n in enumerate(TS):
                    mm = pe.transpose(HB[0:16, 0, at:at + n], SCO[0:n, t, :], ident[0:n, 0:n])
                    at += n
                mm.then_inc(b_pe, PE_B.one("sct"))
                fill("sct")
                pe.wait_ge(b_dve, DVE_B.at(i, "spn"))
                pe.sem_inc(s_passed, 1)
                at = 0
                for t, n in enumerate(TS):
                    mm = pe.transpose(HB[0:n, 1, 16 * t:16 * (t + 1)], SPN[0:16, at:at + n], ident[0:16, 0:16])
                    at += n
                mm.then_inc(b_pe, PE_B.one("pwt"))
                fill("pwt")
                pe.wait_ge(b_act, ACT_B.at(i, "pwc"))
                pe.wait_ge(s_vc, (i + 1) * 48)
                pe.wait_ge(s_vrow, done(1, i, 16))
                for q in range(2):
                    for t, n in enumerate(TS):
                        mm = pe.matmul(HB[0:16, 2 * q, :], PW[0:n, t, :],
                                       VC[0:n, t, 4 * q:4 * q + 4, :].rearrange("p b c -> p (b c)"),
                                       start=(t == 0), stop=(t == 2))
                mm.then_inc(b_pe, PE_B.one("av"))
                fill("av")
                pe.wait_ge(b_act, ACT_B.at(i, "avc"))
                pe.sem_inc(s_passed, 1)
                for b in range(NB):
                    mm = pe.transpose(HB[:, 1, 16 * b:16 * (b + 1)], PRF[0:16, 128 * b:128 * (b + 1)], ident[0:16, 0:16])
                mm.then_inc(b_pe, PE_B.one("avt"))
                fill("avt")

            with pe.Fori(0, PAIRS - 1) as i:
                pair_b(i, group_b(i + 1))
            pair_b(PAIRS - 1, 0, fills=False)

            def by_token(m, t):
                pe.wait_ge(s_evac, m * 2 + (2 * GROUP_C + t + 1))
                pe.wait_ge(c_dve, done(0, m, 2))
                for q in range(4):
                    pe.transpose(HB[:, 2 * t, 128 * q:128 * (q + 1)], YT[:, t, 128 * q:128 * (q + 1)], ident)
                pe.transpose(HB[0:NB, 2 * t + 1, 0:128], YT[:, t, T:TT], ident).then_inc(c_pe, 1)

            def out_pair(m, first=False):
                for u in range(2 * KT):
                    if first and u < KT:
                        pe.wait_ge(c_pool, u + 1)
                    multiply_unit(pe, m + GROUP_C, u)
                    if u == 3 and not first:
                        by_token(m - 1, 1)
                    if u == KT + 3:
                        if first:
                            pe.wait_ge(b_dve, DVE_B.start(PAIRS))
                        by_token(m, 0)

            out_pair(0, first=True)
            with pe.Fori(1, D // 256) as m:
                out_pair(m)
            by_token(D // 256 - 1, 1)

        @block.scalar
        def _(act):
            act.sem_inc(a_act, ACT_A.n)
            act.sem_inc(b_act, ACT_B.n)
            act.wait_ge(p_dve, DVE_P.at(0, "zrow"))
            n = 0
            for v in (mu_shift[0:DR], mu_shift[DR:2 * DR], mu_shift[2 * DR:3 * DR], w0, a0, k_k, k_a,
                      r_k.rearrange("h d -> (h d)"), gn_w, gn_b, norm_w):
                m = v.shape[0] // 128
                act.dma_start(ROWT[n:n + m, :], v.rearrange("(i c) -> i c", c=128)).then_inc(s_rows, 16)
                n += m
            act.dma_start(ROWT[ROW_MU:ROW_MU + 2, 0:LORA], mu_shift[3 * DR:SHIFT].rearrange("(i c) -> i c", c=LORA))\
               .then_inc(s_rows, 16)
            for j, v in enumerate((q_norm, k_norm)):
                for h in range(2):
                    act.dma_start(ROWT[ROW_QK + j:ROW_QK + j + 1, HD * h:HD * (h + 1)],
                                  v.rearrange("(a c) -> a c", a=1)).then_inc(s_rows, 16)
            act.dma_start(SROW[0:NB, :], state_shift).then_inc(s_srow, 16)
            act.wait_ge(p_dve, DVE_P.at(0, "bias"))
            act.preload_act_table_set("natural_log_exp_and_others")
            for t in (4, 0, 1, 2, 3):
                m = 128 if t < 4 else NB
                act.wait_ge(s_xt[t], 16)
                if t < 4:
                    act.wait_ge(p_act, ACT_P.at(0, f"sq{(t - 1) % 5}"))
                act.activation(SQJ[0:m, :], XTOK[0:m, t, :], ACT.Square, accum_out=SSQ[0:m, t:t + 1])\
                   .then_inc(p_act, ACT_P.one(f"sq{t}"))
                act.wait_ge(p_act, ACT_P.at(0, f"sq{t}"))
                act.activation(SSQ[0:m, 5 + t:6 + t], SSQ[0:m, t:t + 1], ACT.Ln, bias=eps_rms[0:m], scale=1.0 / D)\
                   .then_inc(p_act, ACT_P.one(f"ln{t}"))
                act.wait_ge(p_act, ACT_P.at(0, f"ln{t}"))
                act.activation(SSQ[0:m, 10 + t:11 + t], SSQ[0:m, 5 + t:6 + t], ACT.Exp, scale=-0.5)\
                   .then_inc(p_act, ACT_P.one(f"rs{t}"))
            round_half(act, 0, 0, LORA)
            round_half(act, 0, 1, LORA)
            act.wait_ge(p_dve, DVE_P.at(0, "rows"))
            for k in range(KT):
                act.wait_ge(p_pe, PE_P.at(0, f"x{k}"))
                act.activation(XH[:, k, :], HBF[:, 1024 * (k % 2):1024 * (k % 2) + TT], ACT.Copy,
                               scale=PT[:, ROW_NW + k:ROW_NW + k + 1]).then_inc(p_act, ACT_P.one(f"hi{k}"))
            round_half(act, 0, 2, LORA)
            round_half(act, 0, 3, LORA)
            act.wait_ge(p_dve, DVE_P.at(0, "lz"))
            evacuate(act, 0, 0, two(ZL[0:LORA, 0, 1:TT + 1]), LORA)
            round_half(act, group_a(0), 0)
            round_half(act, group_a(0), 1)
            evacuate(act, 0, 1, two(ZL[0:LORA, 1, 1:TT + 1]), LORA)
            for k in range(1, 8):
                round_half(act, group_a(0), k + 1)
                if k % 2:
                    if k == 1:
                        act.wait_ge(s_zero, 1)
                    evacuate(act, group_a(0), k // 2, two(Z[:, k // 2, 1:TT + 1]))
                if k == 3:
                    act.wait_ge(p_dve, DVE_P.at(0, "lmix"))
                    act.activation(TW[0:LORA, :], ML[0:LORA, 0, :], ACT.Tanh)
                    act.activation(AD[0:LORA, :], ML[0:LORA, 1, :], ACT.Copy).then_inc(p_act, ACT_P.one("tanh"))
                if k == 6:
                    act.wait_ge(p_pe, PE_P.at(0, "ltail"))
                    act.activation(LTAIL[0:NB + 1, :, :], HB[0:NB + 1, 0, 0:2 * LORA].rearrange("p (a b) -> p a b", a=2),
                                   ACT.Copy).then_inc(p_act, ACT_P.one("ltail"))
                    act.wait_ge(p_act, ACT_P.at(0, "ltail"))
                    act.dma_start(shift_p[0:1, 3 * DR:SHIFT], LTAIL[0:1, :, :].rearrange("p a b -> p (a b)"))\
                       .then_inc(o_ltail, 16)
                    act.dma_start(shift_s[:, 3 * DR:SHIFT], LTAIL[1:NB + 1, :, :].rearrange("p a b -> p (a b)"))\
                       .then_inc(o_ltail, 16)
            act.wait_ge(o_ltail, 32)

            def pair_a(i, g, z_next):
                def feed(name):
                    act_feed(act, span_a, g, name, z_next)

                act.preload_act_table(ACT.Sigmoid)
                act.wait_ge(a_mix, DVE_M.at(i, "mix"))
                act.activation(KSQ, M3[:, 1], ACT.Square, scale=P_["k_k"]).then_inc(a_act, ACT_A.one("ksq"))
                act.wait_ge(a_pe, PE_A.at(i, "lora"))
                act.activation(two(SGW), HB[:, 0:2, 0:HT], ACT.Sigmoid, bias=P_["w0"]).then_inc(a_act, ACT_A.one("sgw"))
                act.activation(two(A_), HB[:, 2:4, 0:HT], ACT.Sigmoid, bias=P_["a0"]).then_inc(a_act, ACT_A.one("sga"))
                act.wait_ge(s_evac, group_a(i) * 2 + 4)
                act.wait_ge(a_dve, DVE_A.start(i))
                act.activation(GG, Z[:, 3, 1:TT + 1], ACT.Sigmoid).then_inc(a_act, ACT_A.one("sgg"))
                act.preload_act_table_set("natural_log_exp_and_others")
                feed("lora")
                feed("kk")
                act.wait_ge(a_dve, DVE_A.at(i, "ssm"))
                act.activation(SSM, SSM, ACT.Ln, scale=float(2 ** LNS)).then_inc(a_act, ACT_A.one("ln"))
                act.wait_ge(a_act, ACT_A.at(i, "ln"))
                act.activation(RN, SSM, ACT.Exp, scale=-0.5, bias=ln_back).then_inc(a_act, ACT_A.one("rn"))
                act.wait_ge(a_dve, DVE_A.at(i, "gl"))
                act.activation(E1, LC, ACT.Exp, scale=-DEC).then_inc(a_act, ACT_A.one("e1"))
                act.activation(E2, LC, ACT.Exp, scale=DEC).then_inc(a_act, ACT_A.one("e2"))
                act.activation(G, GL, ACT.Exp, scale=-DEC).then_inc(a_act, ACT_A.one("g"))
                act.activation(DCS, SGW[:, T:TT], ACT.Exp, scale=-DEC).then_inc(a_act, ACT_A.one("dcs"))
                act.wait_ge(a_pe, PE_A.at(i, "tail"))
                act.wait_ge(o_tail, done(0, i, 32))
                act.activation(TAIL[0:NB + 1, :, :].rearrange("p a b -> p (a b)"), HB[0:NB + 1, 2, 0:384], ACT.Copy)\
                   .then_inc(a_act, ACT_A.one("tail"))
                act.wait_ge(a_act, ACT_A.at(i, "tail"))
                tails = lambda v: v[:, 0:3 * DR].rearrange("p (s i c) -> p i s c", s=3, i=PAIRS)[:, i, :, :]
                act.dma_start(tails(shift_p), TAIL[0:1, :, :]).then_inc(o_tail, 16)
                act.dma_start(tails(shift_s), TAIL[1:NB + 1, :, :]).then_inc(o_tail, 16)
                feed("tail")
                feed("bonus")
                act.wait_ge(a_pe, PE_A.at(i, "vec"))
                act.activation(VEC[0:NB, :, :].rearrange("p a b -> p (a b)"), HBF[0:NB, 0:768], ACT.Copy)\
                   .then_inc(a_act, ACT_A.one("vec"))
                feed("vec")
                for name in GRAMS:
                    if name[:2] == "nn":
                        act.wait_ge(a_pe, PE_A.at(i, name))
                        q = 2 * int(name[2])
                        act.activation(NN[:, q:q + 4, :].rearrange("p a b -> p (a b)"), HB[:, 2 + q // 4, :], ACT.Copy)\
                           .then_inc(a_act, ACT_A.one(name))
                    feed(name)
                for name, bank, dst in (("tokb", 0, TOKB), ("tokk", 1, TOKK), ("tokv", 2, TOKV)):
                    act.wait_ge(a_pe, PE_A.at(i, name))
                    act.activation(dst.rearrange("p a b -> p (a b)"), HB[:, bank, :], ACT.Copy)\
                       .then_inc(a_act, ACT_A.one(name))
                    feed(name)
                act.wait_ge(a_pe, PE_A.at(i, "bcast"))
                act.activation(RV.rearrange("p a b -> p (a b)"), HB[:, 3, 0:6 * HD], ACT.Copy)\
                   .then_inc(a_act, ACT_A.one("rv"))
                feed("bcast")
                for l in LV:
                    for s in ("qt", "tr") if l < last else ("qt",):
                        act.wait_ge(a_pe, PE_A.at(i, f"{s}{l}a"))
                        dst = (QT if s == "qt" else XT)[:, 0:4, :].rearrange("p a b -> p (a b)")
                        if l < last:
                            act.activation(dst, HB[:, 3, :], ACT.Copy).then_inc(a_act, ACT_A.one(f"{s}{l}"))
                        else:
                            act.activation(QT[0:64, 0:4, 64:128], HB[0:64, 3, 0:256].rearrange("p (q t) -> p q t", q=4),
                                           ACT.Copy).then_inc(a_act, ACT_A.one(f"{s}{l}"))
                        feed(f"{s}{l}a")
                        feed(f"{s}{l}b")
                        if s == "qt":
                            feed(f"dx{l}a")
                            feed(f"dx{l}b")
                for c in range(NC):
                    act.wait_ge(a_pe, PE_A.at(i, f"rhs{c}"))
                    act.activation(RHS[:, c % 2, :], HB[:, 3, 0:128], ACT.Copy).then_inc(a_act, ACT_A.one(f"rhs{c}"))
                    feed(f"rhs{c}")
                    act.wait_ge(a_pe, PE_A.at(i, f"u{c}"))
                    act.activation(U[:, c, :], HB[:, 0, 0:128], ACT.Copy, scale=-1.0).then_inc(a_act, ACT_A.one(f"u{c}"))
                    feed(f"u{c}")
                    feed(f"s{c}")
                    feed(f"y{c}")
                act.wait_ge(a_pe, PE_A.at(i, "st"))
                act.wait_ge(o_state, done(0, i, 32))
                act.activation(ST, HB[:, 3, 0:128], ACT.Copy).then_inc(a_act, ACT_A.one("st"))
                act.activation(Y[:, T:TT], HB[:, 3, 128:128 + NB], ACT.Copy)
                act.activation(Y[:, 0:T], HB[:, 1, :], ACT.Copy).then_inc(a_act, ACT_A.one("y"))
                act.wait_ge(a_act, ACT_A.at(i, "st"))
                for h in range(2):
                    act.dma_start(wkv_p[0].rearrange("(i h) v k -> i h v k", h=2)[i, h],
                                  ST[HD * h:HD * (h + 1), HD * h:HD * (h + 1)]).then_inc(o_state, 16)
                feed("st")
                act.wait_ge(a_dve, DVE_A.at(i, "yc"))
                act.activation(YSQ, YC, ACT.Square).then_inc(a_act, ACT_A.one("ysq"))
                feed("mean")
                act.wait_ge(a_pe, PE_A.at(i, "var"))
                act.activation(two(Y), HB[:, 2:4, 0:HT], ACT.Ln, bias=eps_gn).then_inc(a_act, ACT_A.one("yln"))
                act.wait_ge(a_act, ACT_A.at(i, "yln"))
                act.activation(Y, Y, ACT.Exp, scale=-0.5).then_inc(a_act, ACT_A.one("yrs"))
                feed("var")
                act.wait_ge(a_dve, DVE_A.at(i, "ym"))
                act.dma_start(mix_d[0:DR, :].rearrange("(i p) t -> i p t", p=128)[i], MIXO).then_inc(o_mix, 16)

            def next_a(i):
                def dst(s):
                    if s == 0:
                        act.wait_ge(a_pool, POOL_A.at(i, "gate"))
                        act.wait_ge(a_pe, PE_A.at(i, "tail"))
                    return two(Z[:, s, 1:TT + 1])
                return dst

            with act.Fori(0, PAIRS - 1) as i:
                pair_a(i, group_a(i + 1), next_a(i))
            pair_a(PAIRS - 1, group_b(0), next_a(PAIRS - 1))

            def squares(i):
                act.wait_ge(s_evac, group_b(i) * 2 + 2)
                if not isinstance(i, int) or i > 0:
                    act.wait_ge(b_pe, PE_B.at(i - 1, "ssum"))
                for j in range(2):
                    sq = act.activation(SQ[:, j, :], ZB[:, j, :], ACT.Square)
                sq.then_inc(b_sq, 1)

            def mix_tile(k):
                act.wait_ge(s_mt[0 if k < KT // 2 else 1 if k < KT - 1 else 2], 16)
                act.activation(XH[:, k, :], XL[:, k, :].bitcast(F32), ACT.Copy).then_inc(c_act, ACT_CP.one(f"hi{k}"))

            def pair_b(i, g, fills=True):
                def dst(s):
                    if s == 0:
                        act.wait_ge(b_dve, DVE_B.at(i, "gate"))
                        act.wait_ge(b_pe, PE_B.at(i, "stok"))
                    return two(ZB[:, s, :])

                def feed(name):
                    if fills:
                        act_feed(act, span_b, g, name, dst, ahead=True)

                act.wait_ge(b_dve, DVE_B.start(i))
                act.wait_ge(b_pe, PE_B.at(i, "ssum"))
                for j in range(2):
                    ln = act.activation(two(LN[:, j, :]), HB[:, 2 * j:2 * j + 2, 0:HT], ACT.Ln, bias=eps_rms)
                ln.then_inc(b_act, ACT_B.one("ln"))
                act.wait_ge(b_act, ACT_B.at(i, "ln"))
                for j in range(2):
                    rn = act.activation(RNB[:, j, :], LN[:, j, :], ACT.Exp, scale=-0.5)
                rn.then_inc(b_act, ACT_B.one("rn"))
                feed("ssum")
                tokens = (("tokk", 0, KTOK, kp_view, o_k), ("tokv", 1, VTOK, vp_view, o_v))
                for name, bank, dstk, view, o in tokens:
                    act.wait_ge(b_pe, PE_B.at(i, name))
                    act.wait_ge(o, done(0, i, 16))
                    act.activation(dstk.rearrange("p a b -> p (a b)"), HB[:, bank, :], ACT.Copy)\
                       .then_inc(b_act, ACT_B.one(name))
                act.wait_ge(b_pe, PE_B.at(i, "stok"))
                act.wait_ge(o_skv, done(0, i, 32))
                act.wait_ge(s_krow, done(0, i, 16))
                act.wait_ge(s_vrow, done(0, i, 16))
                act.activation(SKV[0:NB, :, :].rearrange("p a b -> p (a b)"), HB[0:NB, 2, 0:256], ACT.Copy)\
                   .then_inc(b_act, ACT_B.one("stok"))
                feed("tokv")
                act.wait_ge(b_act, ACT_B.at(i, "stok"))
                if not isinstance(i, int) or i > 0:
                    act.wait_ge(b_dve, DVE_B.start(i))
                    act.wait_ge(b_pe, PE_B.start(i))
                act.dma_start(KC[96:97, 1, :, :], SKV[0:NB, 0, :]).then_inc(s_krow, 16)
                act.preload_act_table(ACT.Sigmoid)
                act.wait_ge(s_evac, group_b(i) * 2 + 4)
                act.activation(GGB, ZB[:, 3, :], ACT.Sigmoid).then_inc(b_act, ACT_B.one("sgg"))
                act.preload_act_table_set("natural_log_exp_and_others")
                feed("stok")
                act.dma_start(VC[96:97, 1, :, :], SKV[0:NB, 1, :]).then_inc(s_vrow, 16)
                for name, bank, dstk, view, o in tokens:
                    act.dma_start(view.rearrange("p t (i c) -> p t i c", i=PAIRS)[:, :, i, :], dstk).then_inc(o, 16)
                act.dma_start(ks_view.rearrange("b (i c) -> b i c", i=PAIRS)[:, i, :], SKV[0:NB, 0, :]).then_inc(o_skv, 16)
                act.dma_start(vs_view.rearrange("b (i c) -> b i c", i=PAIRS)[:, i, :], SKV[0:NB, 1, :]).then_inc(o_skv, 16)
                feed("qb")

                def exps(j):
                    n = 128 * (JS[j][1] + 1)
                    act.wait_ge(b_dve, DVE_B.at(i, f"mx{j}"))
                    act.activation(EE[:, j % 2, 0:n], SC2[:, j % 2, 0:n], ACT.Exp, scale=-1.0, bias=MX[:, j:j + 1])\
                       .then_inc(b_act, ACT_B.one(f"ex{j}"))

                for j in range(2):
                    feed(f"s{j}")
                    exps(j)
                for j, (h, b) in enumerate(JS):
                    n = 128 * (b + 1)
                    if j + 2 < nj:
                        feed(f"s{j + 2}")
                    act.wait_ge(b_pe, PE_B.at(i, f"t{j}"))
                    act.activation(PTR[:, j % 2, 0:n], HB[:, 2, 0:n], ACT.Copy).then_inc(b_act, ACT_B.one(f"tp{j}"))
                    if j + 2 < nj:
                        exps(j + 2)
                    feed(f"t{j}")
                    feed(f"o{j}")
                    if not fills and j < 7:
                        if j == 0:
                            round_half(act, GROUP_C, 1)
                        for k in (2 * j, 2 * j + 1):
                            mix_tile(k)
                act.wait_ge(b_dve, DVE_B.at(i, "smx"))
                act.activation(SE[0:16, :], SS_[0:16, :], ACT.Exp, scale=-1.0, bias=SMX[0:16, 0:1])\
                   .then_inc(b_act, ACT_B.one("sex"))
                feed("sct")
                act.wait_ge(b_pe, PE_B.at(i, "pwt"))
                for t, n in enumerate(TS):
                    pw = act.activation(PW[0:n, t, :], HB[0:n, 1, 16 * t:16 * (t + 1)], ACT.Copy)
                pw.then_inc(b_act, ACT_B.one("pwc"))
                feed("pwt")
                if fills:
                    squares(i + 1)
                act.wait_ge(b_pe, PE_B.at(i, "av"))
                for q in range(2):
                    avc = act.activation(PRF[0:16, 512 * q:512 * (q + 1)], HB[0:16, 2 * q, :], ACT.Copy)
                avc.then_inc(b_act, ACT_B.one("avc"))
                feed("av")
                feed("avt")
                act.wait_ge(b_dve, DVE_B.at(i, "mixs"))
                act.dma_start(mix_d[DR:D, :].rearrange("(i p) t -> i p t", p=128)[i], MIXB).then_inc(o_mix, 16)

            for s, n in ((o_mix, 16), (o_state, 32), (o_sst, 16), (o_tail, 32)):
                act.wait_ge(s, done(0, PAIRS, n))
            act.wait_ge(a_pe, PE_A.start(PAIRS))
            act.wait_ge(a_dve, DVE_A.start(PAIRS))
            squares(0)
            with act.Fori(0, PAIRS - 1) as i:
                pair_b(i, group_b(i + 1))
            pair_b(PAIRS - 1, 0, fills=False)

            mix_tile(KT - 2)
            mix_tile(KT - 1)
            for s, n in ((o_k, 16), (o_v, 16), (o_skv, 32)):
                act.wait_ge(s, done(0, PAIRS, n))
            act.wait_ge(b_pe, PE_B.start(PAIRS))
            act.wait_ge(b_dve, DVE_B.start(PAIRS))

            def out_pair(m, first=False, more=True):
                def tile_to(t):
                    act.wait_ge(c_pe, m * 2 + (t + 1))
                    return two(YT[:, t, :])

                if not first:
                    round_half(act, m + GROUP_C, 1)
                round_half(act, m + GROUP_C, 2)
                round_half(act, m + GROUP_C, 3)
                evacuate(act, m + GROUP_C, 0, tile_to(0))
                if more:
                    round_half(act, m + GROUP_C, 4)
                evacuate(act, m + GROUP_C, 1, tile_to(1))

            def store(m):
                yv = yp.rearrange("p t (m u c) -> p t m u c", u=2, c=128)
                ysv = ys.rearrange("b (m u c) -> b m u c", u=2, c=128)
                for t in range(2):
                    act.wait_ge(c_dve, m * 2 + (t + 3))
                    act.dma_start(yv[:, :, m, t, :], YO[:, t, :, :]).then_inc(o_y[t], 16)
                    act.dma_start(ysv[:, m, t, :], YOS[0:NB, t, :]).then_inc(o_y[t], 16)

            out_pair(0, first=True)
            with act.Fori(1, D // 256 - 1) as m:
                out_pair(m)
                store(m - 1)
            out_pair(D // 256 - 1, more=False)
            store(D // 256 - 2)
            store(D // 256 - 1)
            for t in range(2):
                act.wait_ge(o_y[t], 32 * (D // 256) + 32)

        @block.vector
        def _(dve):
            dve.sem_inc(a_dve, DVE_A.n)
            dve.sem_inc(b_dve, DVE_B.n)
            dve.memset(ROWT, 0.0).then_inc(p_dve, DVE_P.one("zrow"))
            dve.memset(SSQ, 1.0)
            dve.memset(BIAS[:, 0:1], RMS_EPS)
            dve.memset(BIAS[:, 1:2], GN_EPS)
            dve.memset(BIAS[:, 2:3], 0.5 * LNS * float(np.log(2.0))).then_inc(p_dve, DVE_P.one("bias"))
            for t in (4, 0, 1, 2, 3):
                m = 128 if t < 4 else NB
                dve.wait_ge(p_act, ACT_P.at(0, f"rs{t}"))
                dve.tensor_scalar(XTOK[0:m, t, :], XTOK[0:m, t, :], SSQ[0:m, 10 + t:11 + t], None, ALU.mult)\
                   .then_inc(p_dve, DVE_P.one(f"xn{t}"))
            dve.wait_ge(p_pe, PE_P.at(0, "rows"))
            dve.tensor_copy(PT[:, :], HB[:, 0, 0:ROWS]).then_inc(p_dve, DVE_P.one("rows"))
            dve.wait_ge(p_pe, PE_P.at(0, "shift"))
            dve.tensor_copy(SST[:, 0:24, :], HB[:, 1, 0:24 * NB].rearrange("p (s b) -> p s b", b=NB))
            dve.tensor_copy(SST[0:LORA, 24:26, :], HB[0:LORA, 1, 24 * NB:26 * NB].rearrange("p (s b) -> p s b", b=NB))\
               .then_inc(p_dve, DVE_P.one("shift"))
            for k in range(KT):
                dve.wait_ge(p_act, ACT_P.at(0, f"hi{k}"))
                dve.scalar_tensor_tensor(out=XL[:, k, :], in0=HBF[:, 1024 * (k % 2):1024 * (k % 2) + TT],
                                         scalar=PT[:, ROW_NW + k:ROW_NW + k + 1], in1=XH[:, k, :].bitcast(F32),
                                         op0=ALU.mult, op1=ALU.subtract).then_inc(p_dve, DVE_P.one(f"lo{k}"))
            dve.wait_ge(p_pe, PE_P.at(0, f"x{KT - 1}"))
            dve.memset(Z[:, :, 0:1], 0.0)
            dve.memset(ARP, 0.0).then_inc(s_zero, 1)
            dve.memset(ZL[0:LORA, :, 0:1], 0.0).then_inc(p_dve, DVE_P.one("lz"))
            dve.wait_ge(s_evac, 2)
            dve.wait_ge(p_dve, DVE_P.at(0, "lz"))
            dve.tensor_tensor(DL[0:LORA, :, 0:T], ZL[0:LORA, :, 0:T], ZL[0:LORA, :, 1:T + 1], ALU.subtract)\
               .then_inc(p_dve, DVE_P.one("ldiff"))
            dve.wait_ge(p_dve, DVE_P.at(0, "shift"))
            dve.tensor_tensor(DL[0:LORA, :, T:TT], SST[0:LORA, 24:26, :], ZL[0:LORA, :, T + 1:TT + 1], ALU.subtract)\
               .then_inc(p_dve, DVE_P.one("lds"))
            dve.wait_ge(p_dve, DVE_P.at(0, "lds"))
            for j in range(2):
                mix = dve.scalar_tensor_tensor(out=ML[0:LORA, j, :], in0=DL[0:LORA, j, :],
                                               scalar=PT[0:LORA, ROW_MU + j:ROW_MU + j + 1],
                                               in1=ZL[0:LORA, j, 1:TT + 1], op0=ALU.mult, op1=ALU.add)
            mix.then_inc(p_dve, DVE_P.one("lmix"))
            dve.wait_ge(p_act, ACT_P.n)
            dve.wait_ge(o_ltail, 32)
            dve.wait_ge(s_zero, 1)

            def shift(i, g):
                if not isinstance(i, int) or i > 0:
                    dve.wait_ge(a_dve, DVE_A.at(i - 1, "yc"))
                dve.tensor_copy(PAR, par_view[:, i, 0:NPV - 2])
                dve.tensor_copy(SSP, ssp_view[:, i, :, :]).then_inc(a_mix, DVE_M.one("par"))
                dve.wait_ge(s_evac, g * 2 + 3)
                dve.tensor_tensor(M3[:, :, 0:T], Z[:, 0:3, 0:T], Z[:, 0:3, 1:T + 1], ALU.subtract)\
                   .then_inc(a_mix, DVE_M.one("dsh"))
                dve.wait_ge(a_mix, DVE_M.at(i, "par"))
                dve.tensor_tensor(M3[:, :, T:TT], SSP, Z[:, 0:3, T + 1:TT + 1], ALU.subtract)\
                   .then_inc(a_mix, DVE_M.one("dss"))
                dve.wait_ge(a_mix, DVE_M.at(i, "dss"))
                for s, mu in enumerate(("mu_r", "mu_k", "mu_v")):
                    mix = dve.scalar_tensor_tensor(out=M3[:, s], in0=M3[:, s], scalar=P_[mu],
                                                   in1=Z[:, s, 1:TT + 1], op0=ALU.mult, op1=ALU.add)
                mix.then_inc(a_mix, DVE_M.one("mix"))

            def pair_a(i, next_shift=True):
                def after(name):
                    dve.wait_ge(a_dve, DVE_A.at(i, name))

                dve.wait_ge(a_dve, DVE_A.start(i))
                dve.tensor_copy(PGN, par_view[:, i, NPV - 2:NPV]).then_inc(a_dve, DVE_A.one("gnp"))
                dve.wait_ge(a_pe, PE_A.at(i, "kk"))
                dve.tensor_scalar(two(SSM), HB[:, 0:2, 0:HT], L2_EPS * L2_EPS, None, ALU.max)\
                   .then_inc(a_dve, DVE_A.one("ssm"))
                by_chunk = lambda a: a[:, 0:T].rearrange("p (c t) -> p c t", c=NC)
                dve.wait_ge(a_act, ACT_A.at(i, "sgw"))
                for c in range(NC):
                    scan = dve.tensor_tensor_scan(LS[:, c * C:(c + 1) * C], ca["ones"], SGW[:, c * C:(c + 1) * C], 0.0,
                                                  ALU.mult, ALU.add)
                scan.then_inc(a_dve, DVE_A.one("scan"))
                after("scan")
                lsc = LS.rearrange("p (c t) -> p c t", c=NC)
                dve.tensor_tensor(LC[:, :, 1:C + 1], lsc, lsc[:, :, MID:MID + 1].to_broadcast([128, NC, C]), ALU.subtract)\
                   .then_inc(a_dve, DVE_A.one("lcm"))
                dve.tensor_scalar(LC[:, :, 0:1], lsc[:, :, MID:MID + 1], -1.0, None, ALU.mult)\
                   .then_inc(a_dve, DVE_A.one("lc0"))
                after("lc0")
                dve.tensor_copy(GL[:, NC - 1:NC], LC[:, NC - 1, C:C + 1]).then_inc(a_dve, DVE_A.one("gl0"))
                dve.tensor_tensor(GL[:, 0:NC - 1], LC[:, 0:NC - 1, C], LC[:, 1:NC, 0], ALU.subtract)\
                   .then_inc(a_dve, DVE_A.one("gl"))
                dve.wait_ge(a_act, ACT_A.at(i, "sga"))
                dve.wait_ge(o_sst, done(0, i, 16))
                dve.tensor_scalar(T1, A_, 1.0, P_["k_a"], ALU.subtract, ALU.mult).then_inc(a_dve, DVE_A.one("t1"))
                after("t1")
                dve.scalar_tensor_tensor(out=KP, in0=T1, scalar=1.0, in1=M3[:, 1], op0=ALU.add, op1=ALU.mult)\
                   .then_inc(a_dve, DVE_A.one("kp"))
                after("kp")
                dve.scalar_tensor_tensor(out=T1, in0=M3[:, 0], scalar=P_["r_k"], in1=KP, op0=ALU.mult, op1=ALU.mult)\
                   .then_inc(a_dve, DVE_A.one("prod"))
                dve.wait_ge(a_act, ACT_A.at(i, "rn"))
                dve.scalar_tensor_tensor(out=KK, in0=M3[:, 1], scalar=P_["k_k"], in1=RN, op0=ALU.mult, op1=ALU.mult)\
                   .then_inc(a_dve, DVE_A.one("kk"))
                after("kk")
                dve.wait_ge(a_act, ACT_A.at(i, "e1"))
                for h in range(2):
                    rows = slice(HD * h, HD * (h + 1))
                    at = dve.tensor_tensor(ARP[rows, :, h, :], by_chunk(KK)[rows], E1[rows, :, 0:C], ALU.mult)
                at.then_inc(a_dve, DVE_A.one("at"))
                dve.tensor_tensor(KKA, KK, A_, ALU.mult).then_inc(a_dve, DVE_A.one("kka"))
                for h in range(2):
                    rows = slice(HD * h, HD * (h + 1))
                    rt = dve.tensor_tensor(ARP[rows, :, 2 + h, :], by_chunk(M3[:, 0])[rows], E1[rows, :, 1:C + 1], ALU.mult)
                rt.then_inc(a_dve, DVE_A.one("rt"))
                after("kka")
                dve.wait_ge(o_mix, done(0, i, 16))
                dve.wait_ge(a_act, ACT_A.at(i, "e2"))
                dve.tensor_tensor(by_chunk(BT), by_chunk(KKA), E2[:, :, 1:C + 1], ALU.mult).then_inc(a_dve, DVE_A.one("bt"))
                dve.tensor_tensor(by_chunk(KTL), by_chunk(KP), E2[:, :, 1:C + 1], ALU.mult).then_inc(a_dve, DVE_A.one("kt"))
                dve.wait_ge(a_pe, PE_A.at(i, "bonus"))
                dve.tensor_tensor(two(BON), HB[:, 2:4, 0:HT], two(M3[:, 2]), ALU.mult).then_inc(a_dve, DVE_A.one("bon"))
                causal = ca["causal"].rearrange("p (k t) -> p k t", k=2).unsqueeze(2).to_broadcast([128, 2, 2, C])
                halves = {"a": (("gb0", 2), ("gk0", 3), ("gb1", 0), ("gk1", 1)),
                          "b": (("gb2", 3), ("gk2", 0), ("gb3", 1), ("gk3", 2))}
                for hn in "ab":
                    for name, bank in halves[hn]:
                        dve.wait_ge(a_pe, PE_A.at(i, name))
                        dst = (GB if name[1] == "b" else GK)[:, int(name[2]), :, :].rearrange("p (k h) t -> p k h t", k=2)
                        dve.tensor_tensor(dst, HB[:, bank, :].rearrange("p (k h t) -> p k h t", k=2, h=2), causal, ALU.mult)\
                           .then_inc(a_dve, DVE_A.one(name))
                    q = 4 * (hn == "b")
                    xh, xth = X[:, q:q + 4, :], XT[:, q:q + 4, :]
                    dve.wait_ge(a_act, ACT_A.at(i, "nn01" if hn == "a" else "nn23"))
                    dve.wait_ge(a_pe, PE_A.at(i, "vec"))
                    dve.tensor_tensor(xh, NN[:, q:q + 4, :], bc(ca["lev0"], 4), ALU.mult)\
                       .then_inc(a_dve, DVE_A.one(f"xm{hn}"))
                    after(f"xm{hn}")
                    dve.tensor_tensor(xh, bc(ident, 4), xh, ALU.subtract).then_inc(a_dve, DVE_A.one(f"x{hn}"))
                    dve.tensor_tensor(xth.rearrange("p (c h) t -> p c h t", h=2), GB[:, q // 2:q // 2 + 2, 0:2, :],
                                      ca["lev0t"].unsqueeze(1).unsqueeze(1).to_broadcast([128, 2, 2, C]), ALU.mult)\
                       .then_inc(a_dve, DVE_A.one(f"xtm{hn}"))
                    after(f"xtm{hn}")
                    dve.tensor_tensor(xth, bc(ident, 4), xth, ALU.subtract).then_inc(a_dve, DVE_A.one(f"xt{hn}"))
                flat = lambda a: a.rearrange("p a b -> p (a b)")
                quarter = lambda a: a.rearrange("p (q t) -> p q t", q=4)
                for l in LV:
                    dve.wait_ge(a_pe, PE_A.at(i, f"qt{l}b"))
                    if l < last:
                        dve.tensor_copy(flat(QT[:, 4:8, :]), HB[:, 0, :]).then_inc(a_dve, DVE_A.one(f"qt{l}"))
                    else:
                        dve.tensor_copy(QT[0:64, 4:8, 64:128], quarter(HB[0:64, 0, 0:256])).then_inc(a_dve, DVE_A.one(f"qt{l}"))
                    for h in range(2):
                        dve.wait_ge(a_pe, PE_A.at(i, f"dx{l}{'ab'[h]}"))
                        if l < last:
                            part = flat(X[:, 4 * h:4 * h + 4, :])
                            dve.tensor_tensor(part, part, HB[:, 1 + h, :], ALU.subtract)\
                               .then_inc(a_dve, DVE_A.one(f"x{'ab'[h]}{l}"))
                        else:
                            dve.tensor_scalar(XT[0:64, 4 * h:4 * h + 4, 64:128], quarter(HB[0:64, 1 + h, 0:256]), -1.0, None,
                                              ALU.mult).then_inc(a_dve, DVE_A.one(f"x{'ab'[h]}{l}"))
                    if l < last:
                        dve.wait_ge(a_pe, PE_A.at(i, f"tr{l}b"))
                        dve.tensor_copy(flat(XT[:, 4:8, :]), HB[:, 0, :]).then_inc(a_dve, DVE_A.one(f"tr{l}"))

                def state(c):
                    dve.wait_ge(a_pe, PE_A.at(i, f"s{c}"))
                    dve.tensor_scalar(S[:, c, :], HB[:, 2, 0:128], G[:, c:c + 1], None, ALU.mult)\
                       .then_inc(a_dve, DVE_A.one(f"s{c}"))

                r, w, kq, v, kk, kka = (RV[:, j, :] for j in range(6))
                row = lambda a: a.unsqueeze(1).to_broadcast([128, 8, HD])
                col = lambda a: a.unsqueeze(2).to_broadcast([128, 8, HD])
                VM = PXF[:, 0:HD].rearrange("p (c v) -> p c v", c=8)
                state(0)
                dve.tensor_tensor(VM, v.rearrange("p (c v) -> p c v", c=8),
                                  ca["group"].unsqueeze(2).to_broadcast([128, 8, 8]), ALU.mult)\
                   .then_inc(a_dve, DVE_A.one("vm"))
                after("vm")
                dve.tensor_reduce(V8, VM.rearrange("p c v -> p v c"), mybir.AxisListType.X, ALU.add)\
                   .then_inc(a_dve, DVE_A.one("v8"))
                after("v8")
                dve.wait_ge(s_sst, i * 16 + 16)
                dve.tensor_tensor(PX, S0, row(kk), ALU.mult).then_inc(a_dve, DVE_A.one("p1"))
                after("p1")
                dve.tensor_reduce(SA8, PX, mybir.AxisListType.X, ALU.add).then_inc(a_dve, DVE_A.one("sa"))
                dve.tensor_tensor(S1, S0, row(w), ALU.mult).then_inc(a_dve, DVE_A.one("sw"))
                after("sw")
                state(1)
                dve.tensor_tensor(PX, col(SA8), row(kka), ALU.mult).then_inc(a_dve, DVE_A.one("p2"))
                after("p2")
                dve.tensor_tensor(S1, S1, PX, ALU.subtract).then_inc(a_dve, DVE_A.one("sb"))
                after("sb")
                dve.tensor_tensor(PX, col(V8), row(kq), ALU.mult).then_inc(a_dve, DVE_A.one("p3"))
                after("p3")
                state(2)
                dve.tensor_tensor(S1, S1, PX, ALU.add).then_inc(a_dve, DVE_A.one("sc"))
                after("sc")
                dve.tensor_tensor(PX, S1, row(r), ALU.mult).then_inc(a_dve, DVE_A.one("p4"))
                after("p4")
                dve.tensor_reduce(Y8, PX, mybir.AxisListType.X, ALU.add).then_inc(a_dve, DVE_A.one("ry"))
                after("ry")
                dve.tensor_tensor(PXF[:, 0:128].rearrange("p (j v) -> p j v", v=8),
                                  ca["place"].unsqueeze(2).to_broadcast([128, 16, 8]),
                                  Y8.unsqueeze(1).to_broadcast([128, 16, 8]), ALU.mult).then_inc(a_dve, DVE_A.one("ye"))
                state(3)
                dve.wait_ge(a_pe, PE_A.at(i, "mean"))
                dve.tensor_tensor(two(YC), two(Y), HB[:, 0:2, 0:HT], ALU.subtract).then_inc(a_dve, DVE_A.one("yc"))
                if next_shift:
                    shift(i + 1, group_a(i + 1))
                dve.wait_ge(a_act, ACT_A.at(i, "yrs"))
                dve.scalar_tensor_tensor(out=YC, in0=YC, scalar=PGN[:, 0:1], in1=Y, op0=ALU.mult, op1=ALU.mult)\
                   .then_inc(a_dve, DVE_A.one("yn"))
                after("yn")
                dve.scalar_tensor_tensor(out=YC, in0=YC, scalar=PGN[:, 1:2], in1=BON, op0=ALU.add, op1=ALU.add)\
                   .then_inc(a_dve, DVE_A.one("yb"))
                after("yb")
                dve.wait_ge(a_pool, POOL_A.at(i, "gate"))
                dve.tensor_tensor(MIXO, YC, GG, ALU.mult).then_inc(a_dve, DVE_A.one("ym"))

            shift(0, group_a(0))
            with dve.Fori(0, PAIRS - 1) as i:
                pair_a(i)
            pair_a(PAIRS - 1, next_shift=False)

            dve.wait_ge(a_pe, PE_A.start(PAIRS))
            dve.wait_ge(a_act, ACT_A.start(PAIRS))
            dve.wait_ge(a_dve, DVE_A.start(PAIRS))
            dve.wait_ge(o_sst, done(0, PAIRS, 16))
            dve.wait_ge(o_state, done(0, PAIRS, 32))
            dve.wait_ge(o_mix, done(0, PAIRS, 16))
            dve.wait_ge(o_tail, done(0, PAIRS, 32))
            dve.memset(QP, 0.0)
            dve.tensor_scalar(QW[:, 0:1], PT[:, ROW_QK:ROW_QK + 1], HD ** -0.5, None, ALU.mult)
            dve.tensor_copy(QW[:, 1:2], PT[:, ROW_QK + 1:ROW_QK + 2]).then_inc(s_zero, 1)
            dve.wait_ge(s_zero, 2)
            dve.wait_ge(s_cb, 16)

            def pair_b(i):
                def after(name):
                    dve.wait_ge(b_dve, DVE_B.at(i, name))

                dve.wait_ge(b_pe, PE_B.start(i))
                dve.wait_ge(b_act, ACT_B.start(i))
                dve.wait_ge(b_pool, POOL_B.start(i))
                dve.wait_ge(b_dve, DVE_B.start(i))
                dve.tensor_copy(SL, cb["slope"].rearrange("p (i h) -> p i h", h=2)[:, i, :])
                dve.tensor_copy(SSL[0:16, :], cb["sslope"].rearrange("p (i o) -> p i o", o=1)[0:16, i, :])\
                   .then_inc(b_dve, DVE_B.one("sl"))
                dve.wait_ge(b_act, ACT_B.at(i, "rn"))
                dve.scalar_tensor_tensor(out=KN, in0=ZB[:, 1, :], scalar=QW[:, 1:2], in1=RNB[:, 1, :],
                                         op0=ALU.mult, op1=ALU.mult).then_inc(b_dve, DVE_B.one("kn"))
                for h in range(2):
                    rows = slice(HD * h, HD * (h + 1))
                    qn = dve.scalar_tensor_tensor(out=QP[rows, h, :], in0=ZB[rows, 0, :], scalar=QW[rows, 0:1],
                                                  in1=RNB[rows, 0, :], op0=ALU.mult, op1=ALU.mult)
                qn.then_inc(b_dve, DVE_B.one("qn"))
                after("qn")
                for h in range(2):
                    rows = slice(HD * h, HD * (h + 1))
                    qs = dve.tensor_copy(QS[rows, :], QP[rows, h, T:TT])
                qs.then_inc(b_dve, DVE_B.one("qs"))
                dve.wait_ge(b_act, ACT_B.at(i, "sgg"))
                dve.tensor_tensor(GGB, GGB, ZB[:, 3, :], ALU.mult).then_inc(b_dve, DVE_B.one("gate"))
                dve.wait_ge(b_pe, PE_B.at(i, "qb"))
                dve.wait_ge(s_kc, (i + 1) * 48)
                dve.wait_ge(s_krow, done(1, i, 16))
                for t, n in enumerate(TS):
                    if t:
                        after(f"rd{t - 1}")
                    dve.tensor_tensor(PR[0:n, :, :].rearrange("p b c -> p (b c)"),
                                      KC[0:n, t, :, :].rearrange("p b c -> p (b c)"), HBF[0:n, 0:NB * 128], ALU.mult)\
                       .then_inc(b_dve, DVE_B.one(f"pr{t}"))
                    after(f"pr{t}")
                    dve.tensor_reduce(SCO[0:n, t, :], PR[0:n, :, :].rearrange("p b (h d) -> p (b h) d", h=2),
                                      mybir.AxisListType.X, ALU.add).then_inc(b_dve, DVE_B.one(f"rd{t}"))

                def largest(j):
                    h, b = JS[j]
                    n = 128 * (b + 1)
                    dve.wait_ge(b_pe, PE_B.at(i, f"s{j}"))
                    if j == 0:
                        dve.wait_ge(b_pool, POOL_B.at(i, "bt"))
                    if j >= 2:
                        dve.wait_ge(b_act, ACT_B.at(i, f"ex{j - 2}"))
                    dve.sem_inc(s_passed, 1)
                    dve.tensor_tensor_reduce(out=SC2[:, j % 2, 0:n], in0=HB[:, j % 2, 0:n],
                                             in1=BTB[:, h, T - n:T], scale=-1.0, scalar=3e38,
                                             op0=ALU.add, op1=ALU.min, accum_out=MX[:, j:j + 1])\
                       .then_inc(b_dve, DVE_B.one(f"mx{j}"))

                largest(0)
                largest(1)
                for j, (h, b) in enumerate(JS):
                    n = 128 * (b + 1)
                    dve.wait_ge(b_act, ACT_B.at(i, f"ex{j}"))
                    if j >= 2:
                        dve.wait_ge(b_pe, PE_B.at(i, f"t{j - 2}"))
                    dve.tensor_tensor_reduce(out=PP[:, j % 2, 0:n], in0=EE[:, j % 2, 0:n], in1=cb["mult"][:, T - n:T],
                                             scale=1.0, scalar=0.0, op0=ALU.mult, op1=ALU.add,
                                             accum_out=ZS[:, j:j + 1]).then_inc(b_dve, DVE_B.one(f"pm{j}"))
                    after(f"pm{j}")
                    dve.reciprocal(RZ[:, j:j + 1], ZS[:, j:j + 1]).then_inc(b_dve, DVE_B.one(f"rz{j}"))
                    after(f"rz{j}")
                    dve.tensor_scalar(DG[:, j % 2, :], ident, RZ[:, j:j + 1], None, ALU.mult)\
                       .then_inc(b_dve, DVE_B.one(f"dg{j}"))
                    if j + 2 < nj:
                        largest(j + 2)
                dve.wait_ge(b_pe, PE_B.at(i, "sct"))
                dve.wait_ge(b_pool, POOL_B.at(i, "bts"))
                dve.sem_inc(s_passed, 1)
                dve.tensor_tensor_reduce(out=SS_[0:16, :], in0=HB[0:16, 0, 0:NS], in1=BTS[0:16, :], scale=-1.0,
                                         scalar=3e38, op0=ALU.add, op1=ALU.min, accum_out=SMX[0:16, 0:1])\
                   .then_inc(b_dve, DVE_B.one("smx"))
                dve.wait_ge(b_act, ACT_B.at(i, "sex"))
                dve.tensor_tensor_reduce(out=SP_[0:16, :], in0=SE[0:16, :], in1=cb["smult"][0:16, :], scale=1.0,
                                         scalar=0.0, op0=ALU.mult, op1=ALU.add, accum_out=SMX[0:16, 1:2])\
                   .then_inc(b_dve, DVE_B.one("spm"))
                after("spm")
                dve.reciprocal(SMX[0:16, 2:3], SMX[0:16, 1:2]).then_inc(b_dve, DVE_B.one("srz"))
                after("srz")
                dve.tensor_scalar(SPN[0:16, :], SP_[0:16, :], SMX[0:16, 2:3], None, ALU.mult)\
                   .then_inc(b_dve, DVE_B.one("spn"))
                dve.wait_ge(b_pe, PE_B.at(i, f"o{nj - 1}"))
                dve.wait_ge(o_mix, done(PAIRS, i, 16))
                dve.tensor_tensor(MIXB[:, 0:T], HB[:, 3, :], GGB[:, 0:T], ALU.mult).then_inc(b_dve, DVE_B.one("mixp"))
                dve.wait_ge(b_pe, PE_B.at(i, "avt"))
                for h in range(2):
                    rows = slice(HD * h, HD * (h + 1))
                    ms = dve.tensor_tensor(MIXB[rows, T:TT], HB[rows, 1, h:128:18],
                                           GGB[rows, T:TT], ALU.mult)
                ms.then_inc(b_dve, DVE_B.one("mixs"))

            with dve.Fori(0, PAIRS) as i:
                pair_b(i)

            dve.wait_ge(o_mix, done(PAIRS, PAIRS, 16))
            for s, n in ((o_k, 16), (o_v, 16), (o_skv, 32)):
                dve.wait_ge(s, done(0, PAIRS, n))
            with dve.Fori(0, D // 256) as m:
                for t in range(2):
                    dve.wait_ge(c_pe, m * 2 + (t + 3))
                    dve.wait_ge(s_xr[t], (m + 1) * 32)
                    dve.wait_ge(o_y[t], done(0, m, 32))
                    dve.tensor_tensor(YO[:, t, :, :].rearrange("p a b -> p (a b)"), HB[:, 2 * t, :],
                                      XR[:, t, :, :].rearrange("p a b -> p (a b)"), ALU.add)
                    dve.tensor_tensor(YOS[0:NB, t, :], HB[0:NB, 2 * t + 1, 0:128], XRS[0:NB, t, :], ALU.add)\
                       .then_inc(c_dve, 1)


_INS = ["x_prompt", "x_sample", "state_wkv", "state_shift", "cache_k_win", "cache_v_win", "norm_w", "w_in",
        "mu_shift", "w0", "w_up", "a0", "a_up", "k_k", "k_a", "r_k", "gn_w", "gn_b", "q_norm", "k_norm", "w_out"]
_OUTS = [(1, T, D), (NB, 1, D), (1, NH, HD, HD), (1, SHIFT), (1, T, NH, HD), (1, T, NH, HD),
         (NB, NH, HD, HD), (NB, SHIFT), (NB, 1, NH, HD), (NB, 1, NH, HD)]


def kernel(**inputs):
    import concourse.bacc as bacc
    from concourse.bass_utils import run_bass_kernel_spmd

    nc = bacc.Bacc("TRN2", target_bir_lowering=False, num_devices=1)
    arrays = {f"in_{name}": np.ascontiguousarray(inputs[name]) for name in _INS}
    arrays["in_const_a"] = np.concatenate(list(CONST_A.values()), axis=1)
    arrays["in_const_b"] = np.concatenate(list(CONST_B.values()), axis=1)
    args = [nc.dram_tensor(k, a.shape, mybir.dt.from_np(a.dtype), kind="ExternalInput").ap()
            for k, a in arrays.items()]
    args += [nc.dram_tensor(f"out_{i}", shape, F32, kind="ExternalOutput").ap() for i, shape in enumerate(_OUTS)]
    build(nc, *args)
    r = run_bass_kernel_spmd(nc, [arrays], core_ids=[0])
    return tuple(r.results[0][f"out_{i}"] for i in range(len(_OUTS)))
```
